# Optimizing a Trainium2 kernel written in Bass

```python
import math
import jax, jax.numpy as jnp
from jax import lax
import numpy as np

D_MODEL = 2048
BATCH = 1
SEQ = 256
DEPTH = 1

CHUNK = 64
Q_BLOCK = 128
ROPE_THETA = 10000.0
NORM_EPS = 1e-6

MLA_HEADS = 8
MLA_Q_RANK = 512
MLA_KV_RANK = 512
MLA_NOPE_DIM = 128
MLA_ROPE_DIM = 64
MLA_V_DIM = 128
MLA_QK_DIM = MLA_NOPE_DIM + MLA_ROPE_DIM

DIFF_HEADS = 4
DIFF_HEAD_DIM = 128
DIFF_V_DIM = 2 * DIFF_HEAD_DIM

MLA_OUT = MLA_HEADS * MLA_V_DIM
DIFF_OUT = DIFF_HEADS * DIFF_V_DIM
MIX_WIDTH = MLA_OUT + DIFF_OUT

DIFF_QK_W = DIFF_HEADS * 2 * DIFF_HEAD_DIM
IN_WIDTHS = (MLA_Q_RANK, MLA_KV_RANK, MLA_ROPE_DIM, DIFF_QK_W, DIFF_QK_W, DIFF_OUT)
IN_SPLITS = tuple(int(v) for v in np.cumsum(IN_WIDTHS)[:-1])
IN_WIDTH = int(sum(IN_WIDTHS))

D_FF = 5632

kernel_name = "hybrid_mla_diffattn_macaron_block"

def rms_norm(x, g):
    xf = x.astype(jnp.float32)
    y = xf * lax.rsqrt(jnp.mean(xf * xf, axis=-1, keepdims=True) + NORM_EPS)
    return (y * g.astype(jnp.float32)).astype(x.dtype)

def rotate_half(x):
    x1, x2 = jnp.split(x, 2, axis=-1)
    return jnp.concatenate([-x2, x1], axis=-1)

def apply_rope(x):
    s, d = x.shape[1], x.shape[-1]
    pos = jnp.arange(s, dtype=jnp.float32)
    inv_freq = ROPE_THETA ** (-jnp.arange(0, d, 2, dtype=jnp.float32) / d)
    ang = pos[:, None] * inv_freq[None, :]
    ang = jnp.concatenate([ang, ang], axis=-1)
    bshape = (1, s) + (1,) * (x.ndim - 3) + (d,)
    cos = jnp.cos(ang).reshape(bshape).astype(x.dtype)
    sin = jnp.sin(ang).reshape(bshape).astype(x.dtype)
    return x * cos + rotate_half(x) * sin

def swiglu(x, w_gate, w_up, w_down):
    return (jax.nn.silu(x @ w_gate) * (x @ w_up)) @ w_down

def query_blocks(t):
    b, s = t.shape[0], t.shape[1]
    return jnp.moveaxis(t.reshape((b, s // Q_BLOCK, Q_BLOCK) + t.shape[2:]), 1, 0)

def merge_blocks(t):
    t = jnp.moveaxis(t, 0, 1)
    return t.reshape((t.shape[0], t.shape[1] * t.shape[2]) + t.shape[3:])

def chunk_mask(start, seq):
    q_pos = start + jnp.arange(Q_BLOCK, dtype=jnp.int32)
    k_pos = jnp.arange(seq, dtype=jnp.int32)
    return (q_pos[:, None] // CHUNK) >= (k_pos[None, :] // CHUNK)

def block_starts(seq):
    return jnp.arange(seq // Q_BLOCK, dtype=jnp.int32) * Q_BLOCK

def mla_attention(q, k, v):
    seq = q.shape[1]
    scale = MLA_QK_DIM ** -0.5

    def step(args):
        qb, start = args
        s = jnp.einsum('bqhd,bkhd->bhqk', qb, k, preferred_element_type=jnp.float32) * scale
        s = jnp.where(chunk_mask(start, seq)[None, None], s, -jnp.inf)
        p = jax.nn.softmax(s, axis=-1).astype(v.dtype)
        return jnp.einsum('bhqk,bkhd->bqhd', p, v)

    return merge_blocks(lax.map(step, (query_blocks(q), block_starts(seq))))

def diff_attention(q, k, v, lam):
    seq = q.shape[1]
    scale = DIFF_HEAD_DIM ** -0.5

    def step(args):
        qb, start = args
        s = jnp.einsum('bqhcd,bkhcd->bhcqk', qb, k, preferred_element_type=jnp.float32) * scale
        s = jnp.where(chunk_mask(start, seq)[None, None, None], s, -jnp.inf)
        p = jax.nn.softmax(s, axis=-1)
        a = (p[:, :, 0] - lam * p[:, :, 1]).astype(v.dtype)
        return jnp.einsum('bhqk,bkhe->bqhe', a, v)

    return merge_blocks(lax.map(step, (query_blocks(q), block_starts(seq))))

def setup_inputs(seed: int = 0) -> dict:
    key = jax.random.key(seed)
    ks = iter(jax.random.split(key, 32))

    def w(shape, fan_in):
        return jax.random.normal(next(ks), (DEPTH,) + shape, jnp.float32) * (fan_in ** -0.5)

    def gain(dim):
        return 1.0 + 0.02 * jax.random.normal(next(ks), (DEPTH, dim), jnp.float32)

    def lam_vec():
        return 0.1 * jax.random.normal(next(ks), (DEPTH, DIFF_HEAD_DIM), jnp.float32)

    x = jax.random.normal(next(ks), (BATCH, SEQ, D_MODEL), jnp.float32)
    return {
        "x": x,
        "ffn1_pre_g": gain(D_MODEL),
        "ffn1_w_gate": w((D_MODEL, D_FF), D_MODEL),
        "ffn1_w_up": w((D_MODEL, D_FF), D_MODEL),
        "ffn1_w_down": w((D_FF, D_MODEL), D_FF),
        "ffn1_post_g": gain(D_MODEL),
        "mix_pre_g": gain(D_MODEL),
        "w_in": w((D_MODEL, IN_WIDTH), D_MODEL),
        "mla_q_norm_g": gain(MLA_Q_RANK),
        "mla_w_uq": w((MLA_Q_RANK, MLA_HEADS * MLA_QK_DIM), MLA_Q_RANK),
        "mla_kv_norm_g": gain(MLA_KV_RANK),
        "mla_w_ukv": w((MLA_KV_RANK, MLA_HEADS * (MLA_NOPE_DIM + MLA_V_DIM)), MLA_KV_RANK),
        "diff_lambda_q1": lam_vec(),
        "diff_lambda_k1": lam_vec(),
        "diff_lambda_q2": lam_vec(),
        "diff_lambda_k2": lam_vec(),
        "diff_subln_g": gain(DIFF_V_DIM),
        "w_out": w((MIX_WIDTH, D_MODEL), MIX_WIDTH),
        "mix_post_g": gain(D_MODEL),
        "ffn2_pre_g": gain(D_MODEL),
        "ffn2_w_gate": w((D_MODEL, D_FF), D_MODEL),
        "ffn2_w_up": w((D_MODEL, D_FF), D_MODEL),
        "ffn2_w_down": w((D_FF, D_MODEL), D_FF),
        "ffn2_post_g": gain(D_MODEL),
    }

def reference(x, ffn1_pre_g, ffn1_w_gate, ffn1_w_up, ffn1_w_down, ffn1_post_g,
              mix_pre_g, w_in, mla_q_norm_g, mla_w_uq, mla_kv_norm_g, mla_w_ukv,
              diff_lambda_q1, diff_lambda_k1, diff_lambda_q2, diff_lambda_k2, diff_subln_g,
              w_out, mix_post_g, ffn2_pre_g, ffn2_w_gate, ffn2_w_up, ffn2_w_down, ffn2_post_g):
    b, s, _ = x.shape
    for l in range(DEPTH):
        f = swiglu(rms_norm(x, ffn1_pre_g[l]), ffn1_w_gate[l], ffn1_w_up[l], ffn1_w_down[l])
        x = x + 0.5 * rms_norm(f, ffn1_post_g[l])

        h = rms_norm(x, mix_pre_g[l])
        c_q, c_kv, k_rope, dq, dk, dv = jnp.split(h @ w_in[l], IN_SPLITS, axis=-1)

        q = (rms_norm(c_q, mla_q_norm_g[l]) @ mla_w_uq[l]).reshape(b, s, MLA_HEADS, MLA_QK_DIM)
        q_nope, q_pe = jnp.split(q, [MLA_NOPE_DIM], axis=-1)
        q = jnp.concatenate([q_nope, apply_rope(q_pe)], axis=-1)
        kv = (rms_norm(c_kv, mla_kv_norm_g[l]) @ mla_w_ukv[l]).reshape(b, s, MLA_HEADS, MLA_NOPE_DIM + MLA_V_DIM)
        k_nope, v = jnp.split(kv, [MLA_NOPE_DIM], axis=-1)
        k_pe = jnp.broadcast_to(apply_rope(k_rope)[:, :, None, :], (b, s, MLA_HEADS, MLA_ROPE_DIM))
        k = jnp.concatenate([k_nope, k_pe], axis=-1)
        o_mla = mla_attention(q, k, v).reshape(b, s, MLA_OUT)

        lambda_init = 0.8 - 0.6 * math.exp(-0.3 * l)
        lam = (jnp.exp(jnp.sum(diff_lambda_q1[l].astype(jnp.float32) * diff_lambda_k1[l].astype(jnp.float32)))
               - jnp.exp(jnp.sum(diff_lambda_q2[l].astype(jnp.float32) * diff_lambda_k2[l].astype(jnp.float32)))
               + lambda_init)
        dq = apply_rope(dq.reshape(b, s, DIFF_HEADS, 2, DIFF_HEAD_DIM))
        dk = apply_rope(dk.reshape(b, s, DIFF_HEADS, 2, DIFF_HEAD_DIM))
        dv = dv.reshape(b, s, DIFF_HEADS, DIFF_V_DIM)
        o_diff = diff_attention(dq, dk, dv, lam)
        o_diff = (rms_norm(o_diff, diff_subln_g[l]) * (1.0 - lambda_init)).reshape(b, s, DIFF_OUT)

        o = jnp.concatenate([o_mla, o_diff], axis=-1) @ w_out[l]
        x = x + rms_norm(o, mix_post_g[l])

        f = swiglu(rms_norm(x, ffn2_pre_g[l]), ffn2_w_gate[l], ffn2_w_up[l], ffn2_w_down[l])
        x = x + 0.5 * rms_norm(f, ffn2_post_g[l])
    return x


_drawn_inputs = setup_inputs


def setup_inputs(seed=0):
    import zlib

    import numpy as np

    out = dict(_drawn_inputs(seed))
    spreads = {}
    factors = {'ffn1_pre_g': 2.961,
     'ffn1_post_g': 4.284,
     'mla_q_norm_g': 8.0,
     'mla_kv_norm_g': 8.0,
     'diff_subln_g': 27.75,
     'mix_post_g': 11.22,
     'ffn2_pre_g': 20.27,
     'ffn2_post_g': 35.51}
    for name, (base, spread) in spreads.items():
        noise = np.random.default_rng([zlib.crc32(name.encode()), seed]).standard_normal(out[name].shape)
        drawn = base * np.exp(spread * noise) if base else spread * noise
        out[name] = __import__('jax').numpy.asarray(drawn.astype(out[name].dtype))
    for name, factor in factors.items():
        out[name] = (out[name] * factor).astype(out[name].dtype)
    return out
```

```python
from contextlib import ExitStack

import numpy as np

import concourse.bass as bass
from concourse import mybir

F32 = mybir.dt.float32
F32R = mybir.dt.float32r
ALU = mybir.AluOpType
ACT = mybir.ActivationFunctionType
AX_X = mybir.AxisListType.X

P = 128
SEQ, D_MODEL, D_FF = 256, 2048, 5632
TT = SEQ // P
KT = D_MODEL // P
FT = D_FF // P
RANK = 512
RT = RANK // P
MLA_HEADS, NOPE, ROPE, MLA_V = 8, 128, 64, 128
QK_DIM = NOPE + ROPE
DIFF_HEADS, DIFF_D = 4, 128
DIFF_V = 2 * DIFF_D
DIFF_W = DIFF_HEADS * 2 * DIFF_D
LATENT_W = 2 * RANK + ROPE
EPS = 1e-6
LAMBDA_INIT = 0.2
CHUNK_FRAMES = 64
MASKED = -1.0e30

RAW = 3
SPLIT = 4
CHUNK = 2048
PIECE = CHUNK // 2
NB = 512
BANKS = 8
MAPS = 2 * DIFF_HEADS + MLA_HEADS
UNITS = DIFF_HEADS + MLA_HEADS
MAP_W = P + 2 * P
Q_COLS = [(0, P), (P, MAP_W)]


class Stage:

    def __init__(self, name, iters, chunks, pieces_per_chunk=2, dmas=1):
        self.name, self.iters, self.chunks, self.ppc, self.dmas = name, iters, chunks, pieces_per_chunk, dmas
        self.pieces = chunks * pieces_per_chunk


def stage_list():
    return [
        Stage("up1", FT // 2, 4), Stage("down1", 4, FT // 4),
        Stage("diff_in", 3, 8), Stage("rope_in", 1, 1, 1), Stage("latent_in", 1, 8),
        Stage("expand", 1, 7, dmas=RT), Stage("out", 4, 4),
        Stage("up2", FT // 2, 4), Stage("down2", 4, FT // 4),
    ]


class Stream:

    def __init__(self):
        self.stages = {s.name: s for s in stage_list()}
        self.piece0, self.fill0, self.raw_owner, self.split_owner = {}, {}, {}, {}
        piece, fills, raw_last, split_last = 0, [0] * RAW, {}, {}
        for s in self.stages.values():
            self.piece0[s.name] = piece
            self.fill0[s.name] = list(fills)
            for i in range(s.iters):
                for j in range(s.chunks):
                    self.raw_owner[s.name, i, j] = raw_last.get(j % RAW)
                    raw_last[j % RAW] = piece + (j + 1) * s.ppc
                    fills[j % RAW] += s.dmas
                for q in range(s.pieces):
                    self.split_owner[s.name, i, q] = split_last.get(q % SPLIT)
                    split_last[q % SPLIT] = piece + q + 1
                piece += s.pieces

    def pieces(self, name, i, q):
        return self.piece0[name] + i * self.stages[name].pieces + q + 1

    def filled(self, name, i, j):
        s = self.stages[name]
        per = len(range(j % RAW, s.chunks, RAW))
        return 16 * (self.fill0[name][j % RAW] + s.dmas * (j // RAW + 1)) + i * (16 * s.dmas * per)

    def owner(self, table, name, i, q):
        if isinstance(i, int):
            return table[name, i, q]
        s = self.stages[name]
        known = [(n, table[name, n, q]) for n in range(s.iters) if table[name, n, q] is not None]
        return max(v - n * s.pieces for n, v in known) + i * s.pieces


class Order:

    def __init__(self, *events):
        self.at, n = {}, 0
        for name, count in events:
            self.at[name] = n
            n += count

    def after(self, name, n=1):
        return self.at[name] + n


RSQRT = Order(("ffn1_pre", 1), ("ffn1_post", 1), ("mix_pre", 1), ("cq", 1), ("ckv", 1),
              ("diff", DIFF_HEADS), ("mix_post", 1), ("ffn2_pre", 1), ("ffn2_post", 1))
N_RSQRT = RSQRT.after("ffn2_post")
SQUARES = Order(("ffn1_pre", TT), ("ffn1_post", 4 * TT), ("mix_pre", TT), ("cq", TT), ("ckv", TT),
                ("diff", DIFF_HEADS * TT), ("mix_post", 4 * TT), ("ffn2_pre", TT), ("ffn2_post", 4 * TT))
SCALED = Order(("ffn1_pre", TT), ("mix_pre", TT), ("cq", TT), ("ckv", TT), ("ffn2_pre", TT))
NORM_GROUPS = Order(("ffn1_pre", KT // 2), ("mix_pre", KT // 2), ("cq", RT // 2), ("ckv", RT // 2),
                    ("ffn2_pre", KT // 2))
NORM_TILES = Order(("ffn1_pre", KT), ("mix_pre", KT), ("cq", RT), ("ckv", RT), ("ffn2_pre", KT))
TOKEN_MAJOR = Order(("diff_in", 6), ("cq", 1), ("ckv", 1), ("q_pe", 1), ("v", 2))
QK_TURNS = Order(("dqk", 8), ("k_pe", 1), ("q_pe", MLA_HEADS // 2))
RESIDUAL = Order(("ffn1_post", TT), ("mix_post", TT), ("ffn2_post", TT))
BRANCH = Order(("ffn1_post", 4 * TT), ("mix_post", 4 * TT), ("ffn2_post", 4 * TT))
GAIN_COLS = {"ffn1_pre": 0, "mix_pre": KT, "ffn2_pre": 2 * KT, "cq": 3 * KT, "ckv": 3 * KT + RT}
GAIN_ROWS = 3 * KT + 2 * RT


def encoder_block(nc, io, out):
    stream = Stream()

    with ExitStack() as ctx:
        def sb(name, shape, dt=F32):
            return ctx.enter_context(nc.sbuf_tensor(name, shape, dt))

        def sem(name):
            return ctx.enter_context(nc.semaphore(name))

        x = sb("x", [P, TT, D_MODEL])
        w_raw = sb("w_raw", [P, RAW, CHUNK])
        w_hi = sb("w_hi", [P, SPLIT, PIECE], F32R)
        w_lo = sb("w_lo", [P, SPLIT, PIECE], F32R)
        post_gain = sb("post_gain", [P, D_MODEL])
        part = sb("part", [P, 2, SEQ])
        gate = sb("gate", [P, 2, SEQ])
        up = sb("up", [P, 2, SEQ])
        ident = sb("ident", [P, P])
        gains = sb("gains", [P, GAIN_ROWS])
        square_sum = sb("square_sum", [P, N_RSQRT, TT])
        block_squares = sb("block_squares", [P, TT, 4])
        mean_square = sb("mean_square", [P, N_RSQRT, TT])
        inv_rms = sb("inv_rms", [P, N_RSQRT, TT])
        minus_half = sb("minus_half", [P, TT])

        def region(name, size):
            sb(name, [P, size // 4])
            start, end = nc.sbuf_base - size, [0]

            def place(name, shape, dt=F32, at=None):
                at = end[0] if at is None else at
                end[0] = at + 4 * int(np.prod(shape[1:]))
                assert end[0] <= size, (name, end[0], size)
                return nc.alloc_sbuf_tensor_at(name, shape, dt, offset=start + at)

            return place

        in_b = region("region_b", KT * 2 * SEQ * 4)
        in_a = region("region_a", FT * 2 * SEQ * 4)

        xn = in_b("xn", [P, KT, 2, SEQ], F32R)
        branch_b = in_b("branch_b", [P, TT, D_MODEL], at=0)
        cn = in_b("cn", [P, 2, RT, 2, SEQ], F32R, at=0)
        mixed = in_b("mixed", [P, KT, 2, SEQ], F32R, at=0)

        hidden = in_a("hidden", [P, FT, 2, SEQ], F32R)
        proj = in_a("proj", [P, 3, TT, DIFF_W], at=0)
        dqk_t = in_a("dqk_t", [P, 2, 2 * DIFF_HEADS, SEQ])
        latent_at = 4 * (3 * TT * DIFF_W + 4 * DIFF_HEADS * SEQ)
        latent = in_a("latent", [P, TT, LATENT_W])
        v_tok = in_a("v_tok", [P, TT, MLA_HEADS * MLA_V])
        q_pe_t = in_a("q_pe_t", [ROPE, MLA_HEADS, SEQ])
        k_pe_t = in_a("k_pe_t", [ROPE, SEQ])
        q_pe = in_a("q_pe", [P, TT, MLA_HEADS * ROPE])
        turn_a = in_a("turn_a", [P, 512])
        turn_b = in_a("turn_b", [P, 512])
        rope = in_a("rope", [P, TT, 2 * (64 + 32)])
        mask = in_a("mask", [P, MAP_W])
        sub_gain = in_a("sub_gain", [P, DIFF_V])
        probs_t = in_a("probs_t", [P, 2, MAP_W])
        small = in_a("small", [P, 8 + 3 * TT * MAPS])
        probs = in_a("probs", [P, 4, MAP_W])
        lam_vec = in_a("lam_vec", [P, 4, DIFF_D], at=probs.manual_sbuf_range[0] - proj.manual_sbuf_range[0])
        nope_t = in_a("nope_t", [P, 2, MLA_HEADS, SEQ], at=0)
        diff_out = in_a("diff_out", [P, 2, TT, DIFF_V], at=latent_at)
        xs = in_a("xs", [P, TT, D_MODEL], at=0)
        branch_a = in_a("branch_a", [P, TT, D_MODEL], at=16384)

        lam = small[:, 0:8]
        row_min, row_sum, row_inv = (
            small[:, 8 + n * TT * MAPS:8 + (n + 1) * TT * MAPS].rearrange("p (m t) -> p m t", t=TT)
            for n in range(3))

        ps = ctx.enter_context(nc.psum_tensor("ps", [P, BANKS, NB], F32))

        raw_filled = [sem(f"raw_filled{r}") for r in range(RAW)]
        pieces_rounded = sem("pieces_rounded")
        pieces_split = sem("pieces_split")
        pieces_multiplied = sem("pieces_multiplied")
        x_loaded = sem("x_loaded")
        gains_loaded = sem("gains_loaded")
        tables_loaded = sem("tables_loaded")
        post_gain_loaded = sem("post_gain_loaded")
        ident_ready = sem("ident_ready")
        consts_ready = sem("consts_ready")
        mask_ready = sem("mask_ready")
        gains_turned = sem("gains_turned")
        gains_ready = sem("gains_ready")
        squares_summed = sem("squares_summed")
        mean_squares = sem("mean_squares")
        rms_inverted = sem("rms_inverted")
        vector_step = sem("vector_step")
        scaled = sem("scaled")
        norm_turned = sem("norm_turned")
        norm_rounded = sem("norm_rounded")
        norm_split = sem("norm_split")
        part_copied = sem("part_copied")
        gate_banks_free = sem("gate_banks_free")
        up_banks_free = sem("up_banks_free")
        silu_done = sem("silu_done")
        hidden_full = sem("hidden_full")
        hidden_rounded = sem("hidden_rounded")
        hidden_split = sem("hidden_split")
        branch_done = sem("branch_done")
        x_updated = sem("x_updated")
        rows0_copied = sem("rows0_copied")
        rows1_copied = sem("rows1_copied")
        nope_part = sem("nope_part")
        nope_done = sem("nope_done")
        k_rope_copied = sem("k_rope_copied")
        roped_k_pe = sem("roped_k_pe")
        roped_q_pe = sem("roped_q_pe")
        roped_dqk = sem("roped_dqk")
        qk_turned = sem("qk_turned")
        qk_copied = sem("qk_copied")
        lam_dots = sem("lam_dots")
        lam_exps = sem("lam_exps")
        scores_ready = sem("scores_ready")
        scores_masked = sem("scores_masked")
        exps_done = sem("exps_done")
        probs_ready = sem("probs_ready")
        probs_turned = sem("probs_turned")
        probs_copied = sem("probs_copied")
        values_summed = sem("values_summed")
        mla_rounded = sem("mla_rounded")
        mla_split = sem("mla_split")
        diff_normed = sem("diff_normed")
        diff_turned = sem("diff_turned")
        diff_rounded = sem("diff_rounded")
        diff_split = sem("diff_split")
        stored = sem("stored")

        block = ctx.enter_context(nc.Block())

        def rows_by_tile(w):
            return w[0].rearrange("(k p) n -> p k n", p=P)

        def columns(w, k0, nk, start, n):
            return rows_by_tile(w)[:, k0:k0 + nk, bass.ds(start, n)]

        ukv = io["mla_w_ukv"][0].rearrange("(k p) (h c) -> p k h c", p=P, c=NOPE + MLA_V)
        uq = io["mla_w_uq"][0].rearrange("(k p) (h c) -> p k h c", p=P, c=QK_DIM)

        def expand_chunk(j):
            if j == 0:
                return [(uq[:, k, :, NOPE:QK_DIM], k) for k in range(RT)]
            w, c0 = [(uq, 0), (ukv, 0), (ukv, NOPE)][(j - 1) // 2]
            h0 = 4 * ((j - 1) % 2)
            return [(w[:, k, h0:h0 + 4, c0:c0 + P], k) for k in range(RT)]

        def load(sp, name, i, j):
            free = stream.owner(stream.raw_owner, name, i, j)
            if free is not None:
                sp.wait_ge(pieces_split, free)
            slot, full = w_raw[:, j % RAW, :], raw_filled[j % RAW]
            if name in ("up1", "up2"):
                w = io[f"ffn{name[2]}_w_{('gate', 'up')[j // 2]}"]
                src = columns(w, 8 * (j % 2), 8, i * 256, 256)
                sp.dma_start(slot.rearrange("p (k n) -> p k n", k=8), src).then_inc(full, 16)
            elif name in ("down1", "down2"):
                src = columns(io[f"ffn{name[4]}_w_down"], 4 * j, 4, i * NB, NB)
                sp.dma_start(slot.rearrange("p (k n) -> p k n", k=4), src).then_inc(full, 16)
            elif name == "diff_in":
                src = columns(io["w_in"], 4 * (j % 4), 4, i * 2 * NB + (LATENT_W + NB * (j // 4)), NB)
                sp.dma_start(slot.rearrange("p (k n) -> p k n", k=4), src).then_inc(full, 16)
            elif name == "latent_in":
                src = columns(io["w_in"], 4 * (j % 4), 4, NB * (j // 4), NB)
                sp.dma_start(slot.rearrange("p (k n) -> p k n", k=4), src).then_inc(full, 16)
            elif name == "rope_in":
                src = columns(io["w_in"], 0, KT, 2 * RANK, ROPE)
                sp.dma_start(slot[:, 0:PIECE].rearrange("p (k n) -> p k n", k=KT), src).then_inc(full, 16)
            elif name == "expand":
                for src, k in expand_chunk(j):
                    dst = slot[:, k * NB:(k + 1) * NB].rearrange("p (h c) -> p h c", h=src.shape[1])
                    sp.dma_start(dst, src).then_inc(full, 16)
            else:
                src = columns(io["w_out"], 4 * j, 4, i * NB, NB)
                sp.dma_start(slot.rearrange("p (k n) -> p k n", k=4), src).then_inc(full, 16)

        def round_piece(act, name, i, q):
            s = stream.stages[name]
            j, half = q // s.ppc, q % s.ppc
            act.wait_ge(raw_filled[j % RAW], stream.filled(name, i, j))
            free = stream.owner(stream.split_owner, name, i, q)
            if free is not None:
                act.wait_ge(pieces_multiplied, free)
            nc.scalar.activation(w_hi[:, q % SPLIT, :], w_raw[:, j % RAW, half * PIECE:(half + 1) * PIECE],
                                 ACT.Copy).then_inc(pieces_rounded, 1)

        def split_piece(dve, name, i, q):
            s = stream.stages[name]
            j, half = q // s.ppc, q % s.ppc
            dve.wait_ge(pieces_rounded, stream.pieces(name, i, q))
            nc.vector.tensor_tensor(w_lo[:, q % SPLIT, :], w_raw[:, j % RAW, half * PIECE:(half + 1) * PIECE],
                                    w_hi[:, q % SPLIT, :].bitcast(F32), ALU.subtract)\
                .then_inc(pieces_split, 1)

        def norm_bank(name, k):
            first, ring = (4, 2) if name in ("cq", "ckv") else (0, 4)
            return ps[:, first + (k // 2) % ring, (k % 2) * SEQ:(k % 2 + 1) * SEQ]

        def turn_bank(name, g):
            return 6 + g % 2 if name == "dqk" else 4 if name == "k_pe" else 4 + (g + 1) % 4

        def nope_bank(n):
            return (2, 0, 4, 6)[n % 4]

        K_ROPE_BANK = 6
        V_BANK = (2, 0)

        nope_part_buf = (part[:, :, :], up[:, :, :])

        def bank(b):
            return ps[:, bass.ds(b, 1), :].rearrange("p a n -> p (a n)")

        def proj_rows(i, blk, tt):
            return proj[:, bass.ds(i, 1), tt, blk * NB:(blk + 1) * NB].rearrange("p a n -> p (a n)")

        def heads_of(name, g):
            for tt in range(TT):
                if name == "k_pe":
                    yield 0, tt, latent[:, tt, 2 * RANK:LATENT_W]
                for h in range(2):
                    if name == "dqk":
                        yield h, tt, proj[:, g // 4, tt, (2 * (g % 4) + h) * P:(2 * (g % 4) + h + 1) * P]
                    if name == "q_pe":
                        yield h, tt, q_pe[:, tt, (2 * g + h) * ROPE:(2 * g + h + 1) * ROPE]

        def turned(name, g):
            if name == "k_pe":
                return k_pe_t[:, :].rearrange("p (h s) -> p h s", h=1), ROPE
            if name == "q_pe":
                return q_pe_t[:, 2 * g:2 * g + 2, :], ROPE
            return dqk_t[:, g // 4, 2 * (g % 4):2 * (g % 4) + 2, :], P

        def unit_of(s):
            if s < 0 or s >= MAPS:
                return None
            if s < 2 * DIFF_HEADS:
                return s // 2 if s % 2 else None
            return s - DIFF_HEADS

        def first_map(u):
            return 2 * u if u < DIFF_HEADS else u + DIFF_HEADS

        @block.sync
        def _(sp):
            for tt in range(TT):
                sp.dma_start(x[:, tt, :], io["x"][0, tt * P:(tt + 1) * P, :]).then_inc(x_loaded, 16)
            for name, s in stream.stages.items():
                first = 1 if name == "up1" else 0
                if first or s.iters == 1:
                    for j in range(s.chunks):
                        load(sp, name, 0, j)
                if s.iters > 1:
                    with sp.Fori(first, s.iters) as i:
                        for j in range(s.chunks):
                            load(sp, name, i, j)
            for tt in range(TT):
                sp.wait_ge(x_updated, RESIDUAL.after("ffn2_post", tt + 1))
                sp.dma_start(out[0, tt * P:(tt + 1) * P, :], x[:, tt, :]).then_inc(stored, 16)
            sp.wait_ge(stored, 16 * TT)

        @block.gpsimd
        def _(pool):
            nc.gpsimd.memset(ident[:, :], 0.0).then_inc(ident_ready, 1)
            nc.gpsimd.memset(minus_half[:, :], -0.5).then_inc(consts_ready, 1)
            pool.wait_ge(ident_ready, 1)
            nc.gpsimd.affine_select(out=ident[:, :], in_=ident[:, :], compare_op=ALU.not_equal, fill=1.0,
                                    base=0, pattern=[[-1, P]], channel_multiplier=1).then_inc(ident_ready, 1)
            pool.wait_ge(consts_ready, 1)
            for n in range(N_RSQRT):
                if n == RSQRT.after("mix_pre"):
                    pool.wait_ge(x_updated, RESIDUAL.after("ffn1_post", TT))
                    nc.gpsimd.memset(mask[:, :], 0.0).then_inc(mask_ready, 1)
                    pool.wait_ge(mask_ready, 1)
                    for _, end in Q_COLS:
                        nc.gpsimd.memset(mask[0:CHUNK_FRAMES, end - CHUNK_FRAMES:end], MASKED)\
                            .then_inc(mask_ready, 1)
                pool.wait_ge(mean_squares, n + 1)
                nc.gpsimd.tensor_tensor(inv_rms[:, n, :], mean_square[:, n, :], minus_half[:, :], ALU.pow)\
                    .then_inc(rms_inverted, 1)

        @block.scalar
        def _(act):
            row = 0
            for name in ("ffn1_pre_g", "mix_pre_g", "ffn2_pre_g", "mla_q_norm_g", "mla_kv_norm_g"):
                g = io[name][0].rearrange("(k p) -> k p", p=P)
                act.dma_start(up[row:row + g.shape[0], 0, 0:P], g).then_inc(gains_loaded, 16)
                row += g.shape[0]

            def load_post_gain(name):
                act.dma_start(post_gain[:, :], io[name][0].partition_broadcast(P)).then_inc(post_gain_loaded, 16)

            load_post_gain("ffn1_post_g")

            dump = [t[:, :, :].rearrange("p a b -> p (a b)") for t in (gate, up)]

            def dump_free(name, n):
                act.wait_ge(squares_summed, SQUARES.at[name] - 1 + n)

            def square_rows(name, rows):
                for tt in range(TT):
                    dump_free(name, tt)
                    nc.scalar.activation(dump[tt], rows[tt], ACT.Square,
                                         accum_out=square_sum[:, RSQRT.at[name], tt:tt + 1])\
                        .then_inc(squares_summed, 1)

            def square_x(name, residual):
                for tt in range(TT):
                    if residual is None:
                        act.wait_ge(x_loaded, 16 * TT)
                    else:
                        act.wait_ge(x_updated, RESIDUAL.after(residual, tt + 1))
                    nc.scalar.activation(xs[:, tt, :], x[:, tt, :], ACT.Square,
                                         accum_out=square_sum[:, RSQRT.at[name], tt:tt + 1])\
                        .then_inc(squares_summed, 1)

            def round_norm(name, dst, tiles):
                for k in range(tiles):
                    act.wait_ge(norm_turned, NORM_GROUPS.after(name, k // 2 + 1))
                    g = GAIN_COLS[name] + k
                    nc.scalar.activation(dst[:, k, 0, :], norm_bank(name, k), ACT.Copy, scale=gains[:, g:g + 1])\
                        .then_inc(norm_rounded, 1)

            def gate_part(L, i):
                act.wait_ge(pieces_multiplied, stream.pieces(f"up{L}", i, 3))
                nc.scalar.activation(part[:, :, :], ps[:, 4:6, SEQ:2 * SEQ], ACT.Copy).then_inc(part_copied, 1)

            def gate_silu(L, i):
                act.wait_ge(gate_banks_free, (L - 1) * (FT // 2) + i + 2)
                nc.scalar.activation(gate[:, :, :], gate[:, :, :], ACT.Silu).then_inc(silu_done, 1)

            def up_part(L, i):
                act.wait_ge(pieces_multiplied, stream.pieces(f"up{L}", i, 7))
                nc.scalar.activation(part[:, :, :], ps[:, 6:8, SEQ:2 * SEQ], ACT.Copy).then_inc(part_copied, 1)

            def round_hidden(L, i):
                act.wait_ge(hidden_full, (L - 1) * (FT // 2) + i + 1)
                nc.scalar.activation(hidden[:, bass.ds(2 * i, 2), 0, :], up[:, :, :], ACT.Copy)\
                    .then_inc(hidden_rounded, 1)

            def square_block(name, stage, b):
                act.wait_ge(pieces_multiplied, stream.pieces(stage, b, stream.stages[stage].pieces - 1))
                for tt in range(TT):
                    dump_free(name, b * TT + tt)
                    nc.scalar.activation(dump[tt], bank(2 * b + tt), ACT.Square,
                                         accum_out=block_squares[:, tt, bass.ds(b, 1)]).then_inc(squares_summed, 1)

            def up_stage(L):
                def body(i, lead):
                    for q in range(8):
                        round_piece(act, f"up{L}", i, q)
                        if lead and q == 2:
                            up_part(L, i - 1)
                        if lead and q == 3:
                            round_hidden(L, i - 1)
                        if q == 6:
                            gate_part(L, i)
                        if q == 7:
                            gate_silu(L, i)
                body(0, False)
                with act.Fori(1, FT // 2) as i:
                    body(i, True)

            def down_stage(L):
                stage = f"down{L}"

                def body(b, lead):
                    for q in range(stream.stages[stage].pieces):
                        round_piece(act, stage, b, q)
                        if not lead and q == 2:
                            up_part(L, FT // 2 - 1)
                        if not lead and q == 3:
                            round_hidden(L, FT // 2 - 1)
                        if lead and q == 3:
                            square_block(f"ffn{L}_post", stage, b - 1)
                body(0, False)
                with act.Fori(1, 4) as b:
                    body(b, True)
                square_block(f"ffn{L}_post", stage, 3)

            act.wait_ge(gains_turned, 1)
            nc.scalar.activation(gains[:, :], ps[:, 4, 0:GAIN_ROWS], ACT.Copy).then_inc(gains_ready, 1)
            act.wait_ge(gains_ready, 1)
            square_x("ffn1_pre", None)
            round_norm("ffn1_pre", xn, KT)
            up_stage(1)
            down_stage(1)
            act.wait_ge(branch_done, BRANCH.after("ffn1_post", 4 * TT))
            load_post_gain("mix_post_g")
            square_x("mix_pre", "ffn1_post")
            act.dma_start(rope[:, :, :], io["rope_table"].rearrange("(t p) c -> p t c", p=P)).then_inc(tables_loaded, 16)
            act.dma_start(sub_gain[:, :], io["diff_subln_g"][0].partition_broadcast(P)).then_inc(tables_loaded, 16)
            for n, name in enumerate(("diff_lambda_q1", "diff_lambda_k1", "diff_lambda_q2", "diff_lambda_k2")):
                act.dma_start(lam_vec[:, n, :], io[name][0].partition_broadcast(P)).then_inc(tables_loaded, 16)
            round_norm("mix_pre", xn, KT)

            def copy_rows0(stage, i, q, b, dst):
                act.wait_ge(pieces_multiplied, stream.pieces(stage, i, q))
                nc.scalar.activation(dst, ps[:, b, :], ACT.Copy).then_inc(rows0_copied, 1)

            def copy_turned(name, g):
                act.wait_ge(qk_turned, QK_TURNS.after(name, g + 1))
                dst, rows = turned(name, g)
                nc.scalar.activation(dst, ps[0:rows, turn_bank(name, g), 0:dst.shape[1] * SEQ]
                                     .rearrange("p (h s) -> p h s", s=SEQ), ACT.Copy).then_inc(qk_copied, 1)

            def diff_in(i, lead):
                for q in range(16):
                    round_piece(act, "diff_in", i, q)
                    if lead and q == 2:
                        copy_rows0("diff_in", i - 1, 15, 2, proj_rows(i - 1, 1, 0))
                    if q == 10:
                        copy_rows0("diff_in", i, 7, 0, proj_rows(i, 0, 0))
            diff_in(0, False)
            with act.Fori(1, 3) as i:
                diff_in(i, True)
            round_piece(act, "rope_in", 0, 0)
            for q in range(16):
                round_piece(act, "latent_in", 0, q)
                if q == 2:
                    copy_rows0("diff_in", 2, 15, 2, proj_rows(2, 1, 0))
                    act.wait_ge(pieces_multiplied, stream.pieces("rope_in", 0, 0))
                    nc.scalar.activation(latent[:, :, 2 * RANK:LATENT_W],
                                         ps[:, K_ROPE_BANK, 0:TT * ROPE].rearrange("p (t c) -> p t c", t=TT),
                                         ACT.Copy).then_inc(k_rope_copied, 1)
                if q == 10:
                    copy_rows0("latent_in", 0, 7, 0, latent[:, 0, 0:RANK])
                    act.wait_ge(rows1_copied, TOKEN_MAJOR.after("cq"))
                    act.wait_ge(rows0_copied, TOKEN_MAJOR.after("cq"))
                    square_rows("cq", [latent[:, tt, 0:RANK] for tt in range(TT)])
                if q in (13, 14):
                    for g in (2 * (q - 13), 2 * (q - 13) + 1):
                        copy_turned("dqk", g)
            round_norm("cq", cn[:, 0], RT)
            copy_rows0("latent_in", 0, 15, 2, latent[:, 0, RANK:2 * RANK])
            act.wait_ge(rows1_copied, TOKEN_MAJOR.after("ckv"))
            act.wait_ge(rows0_copied, TOKEN_MAJOR.after("ckv"))
            square_rows("ckv", [latent[:, tt, RANK:2 * RANK] for tt in range(TT)])
            for q in range(4):
                round_piece(act, "expand", 0, q)
            copy_rows0("expand", 0, 1, 0, q_pe[:, 0, :])
            for g in range(4, 8):
                copy_turned("dqk", g)
            round_norm("ckv", cn[:, 1], RT)
            act.wait_ge(lam_dots, 2)
            nc.scalar.activation(lam[:, 2:4], lam[:, 0:2], ACT.Exp).then_inc(lam_exps, 1)
            for j in range(1, 7):
                for q in (2 * j + 2, 2 * j + 3):
                    if q < 14:
                        round_piece(act, "expand", 0, q)
                if j <= 4:
                    for n in (2 * j - 2, 2 * j - 1):
                        act.wait_ge(pieces_multiplied, stream.pieces("expand", 0, 2 * j + 1))
                        if n >= 2:
                            act.wait_ge(nope_done, n - 1)
                        nc.scalar.activation(nope_part_buf[n % 2], ps[:, nope_bank(n):nope_bank(n) + 2, SEQ:2 * SEQ],
                                             ACT.Copy).then_inc(nope_part, 1)
                else:
                    copy_rows0("expand", 0, 2 * j + 1, V_BANK[j - 5], v_tok[:, 0, (j - 5) * NB:(j - 4) * NB])
            copy_turned("k_pe", 0)
            for g in range(MLA_HEADS // 2):
                copy_turned("q_pe", g)

            def exps(s):
                for tt, (a, b) in enumerate(Q_COLS):
                    act.wait_ge(scores_masked, 2 * s + tt + 1)
                    nc.scalar.activation(probs[:, s % 4, a:b], probs[:, s % 4, a:b], ACT.Exp, scale=-1.0,
                                         bias=row_min[:, s, tt:tt + 1], accum_out=row_sum[:, s, tt:tt + 1])\
                        .then_inc(exps_done, 1)

            def copy_probs(u):
                act.wait_ge(probs_turned, u + 1)
                if u >= 2:
                    act.wait_ge(values_summed, u - 1)
                nc.scalar.activation(probs_t[:, u % 2, :], ps[:, 2 + u % 2, 0:MAP_W], ACT.Copy).then_inc(probs_copied, 1)

            def round_mla(u):
                act.wait_ge(values_summed, u + 1)
                nc.scalar.activation(mixed[:, u - DIFF_HEADS, 0, :], ps[:, 4 + u % 2, 0:SEQ], ACT.Copy)\
                    .then_inc(mla_rounded, 1)

            def square_diff(d):
                act.wait_ge(values_summed, d + 1)
                for tt in range(TT):
                    dump_free("diff", TT * d + tt)
                    nc.scalar.activation(dump[tt][:, 0:DIFF_V], ps[:, 4 + d % 2, tt * DIFF_V:(tt + 1) * DIFF_V],
                                         ACT.Square, accum_out=square_sum[:, RSQRT.at["diff"] + d, tt:tt + 1])\
                        .then_inc(squares_summed, 1)

            def round_diff(d):
                act.wait_ge(diff_turned, d + 1)
                k = MLA_HEADS + 2 * d
                nc.scalar.activation(mixed[:, k:k + 2, 0, :], ps[:, 6, :].rearrange("p (k s) -> p k s", k=2), ACT.Copy)\
                    .then_inc(diff_rounded, 1)

            for t in range(MAPS + 3):
                if t < MAPS:
                    exps(t)
                if unit_of(t - 2) is not None:
                    copy_probs(unit_of(t - 2))
                u = unit_of(t - 3)
                if u is not None:
                    if u < DIFF_HEADS:
                        square_diff(u)
                    else:
                        round_mla(u)
                u = unit_of(t - 5)
                if u is not None and u < DIFF_HEADS:
                    round_diff(u)

            def out_body(b, lead):
                for q in range(8):
                    round_piece(act, "out", b, q)
                    if lead and q == 3:
                        square_block("mix_post", "out", b - 1)
            out_body(0, False)
            with act.Fori(1, 4) as b:
                out_body(b, True)
            square_block("mix_post", "out", 3)
            act.wait_ge(branch_done, BRANCH.after("mix_post", 4 * TT))
            load_post_gain("ffn2_post_g")
            square_x("ffn2_pre", "mix_post")
            round_norm("ffn2_pre", xn, KT)
            up_stage(2)
            down_stage(2)

        @block.vector
        def _(dve):
            steps = [0]

            def then(instruction):
                steps[0] += 1
                instruction.then_inc(vector_step, 1)
                dve.wait_ge(vector_step, steps[0])

            nc.vector.memset(mean_square[:, :, 0:1], 1.0).then_inc(gate_banks_free, 1)
            nc.vector.memset(mean_square[:, :, 1:2], 1.0).then_inc(up_banks_free, 1)
            dve.wait_ge(gate_banks_free, 1)
            dve.wait_ge(up_banks_free, 1)

            def mean_square_of(name, n, width, factor=1.0):
                dve.wait_ge(squares_summed, n)
                k = RSQRT.at[name.split(":")[0]] + (int(name.split(":")[1]) if ":" in name else 0)
                nc.vector.tensor_scalar(mean_square[:, k, :], square_sum[:, k, :], factor / width, factor * EPS,
                                        ALU.mult, ALU.add).then_inc(mean_squares, 1)
                return k

            def scale_rows(name, dst, src):
                k = RSQRT.at[name]
                dve.wait_ge(rms_inverted, k + 1)
                for tt in range(TT):
                    nc.vector.tensor_scalar(dst[tt], src[tt], inv_rms[:, k, tt:tt + 1], None, ALU.mult)\
                        .then_inc(scaled, 1)

            def split_norm(name, dst, tiles):
                for k in range(tiles):
                    if k % 2 == 0:
                        dve.wait_ge(norm_rounded, NORM_TILES.after(name, k + 2))
                    g = GAIN_COLS[name] + k
                    nc.vector.scalar_tensor_tensor(out=dst[:, k, 1, :], in0=norm_bank(name, k), scalar=gains[:, g:g + 1],
                                                   in1=dst[:, k, 0, :].bitcast(F32), op0=ALU.mult, op1=ALU.subtract)\
                        .then_inc(norm_split, 1)

            def gate_sum(L, i):
                dve.wait_ge(part_copied, (L - 1) * FT + 2 * i + 1)
                nc.vector.tensor_tensor(gate[:, :, :], ps[:, 4:6, 0:SEQ], part[:, :, :], ALU.add)\
                    .then_inc(gate_banks_free, 1)

            def up_sum(L, i):
                dve.wait_ge(part_copied, (L - 1) * FT + 2 * i + 2)
                nc.vector.tensor_tensor(up[:, :, :], ps[:, 6:8, 0:SEQ], part[:, :, :], ALU.add)\
                    .then_inc(up_banks_free, 1)
                dve.wait_ge(up_banks_free, (L - 1) * (FT // 2) + i + 2)
                dve.wait_ge(silu_done, (L - 1) * (FT // 2) + i + 1)
                nc.vector.tensor_tensor(up[:, :, :], up[:, :, :], gate[:, :, :], ALU.mult).then_inc(hidden_full, 1)

            def split_hidden(L, i):
                dve.wait_ge(hidden_rounded, (L - 1) * (FT // 2) + i + 1)
                nc.vector.tensor_tensor(hidden[:, bass.ds(2 * i, 2), 1, :], up[:, :, :],
                                        hidden[:, bass.ds(2 * i, 2), 0, :].bitcast(F32), ALU.subtract)\
                    .then_inc(hidden_split, 1)

            def up_stage(L):
                def body(i, lead):
                    for q in range(8):
                        split_piece(dve, f"up{L}", i, q)
                        if lead and q == 2:
                            up_sum(L, i - 1)
                        if lead and q == 3:
                            split_hidden(L, i - 1)
                        if q == 6:
                            gate_sum(L, i)
                body(0, False)
                with dve.Fori(1, FT // 2) as i:
                    body(i, True)

            def branch_block(name, branch, b):
                dve.wait_ge(squares_summed, b * TT + SQUARES.after(name, TT))
                for tt in range(TT):
                    nc.vector.tensor_tensor(branch[:, tt, bass.ds(b * NB, NB)], bank(2 * b + tt),
                                            post_gain[:, bass.ds(b * NB, NB)], ALU.mult).then_inc(branch_done, 1)

            def down_stage(L, branch):
                stage, name = f"down{L}", f"ffn{L}_post"

                def body(b, lead):
                    for q in range(stream.stages[stage].pieces):
                        split_piece(dve, stage, b, q)
                        if not lead and q == 2:
                            up_sum(L, FT // 2 - 1)
                        if not lead and q == 3:
                            split_hidden(L, FT // 2 - 1)
                        if lead and q == 3:
                            branch_block(name, branch, b - 1)
                body(0, False)
                with dve.Fori(1, 4) as b:
                    body(b, True)
                branch_block(name, branch, 3)

            def add_branch(name, branch, factor):
                k = RSQRT.at[name]
                dve.wait_ge(squares_summed, SQUARES.after(name, 4 * TT))
                then(nc.vector.tensor_reduce(square_sum[:, k, :], block_squares[:, :, :], AX_X, ALU.add))
                mean_square_of(name, SQUARES.after(name, 4 * TT), D_MODEL, factor)
                dve.wait_ge(branch_done, BRANCH.after(name, 4 * TT))
                dve.wait_ge(rms_inverted, k + 1)
                for tt in range(TT):
                    nc.vector.scalar_tensor_tensor(out=x[:, tt, :], in0=branch[:, tt, :], scalar=inv_rms[:, k, tt:tt + 1],
                                                   in1=x[:, tt, :], op0=ALU.mult, op1=ALU.add).then_inc(x_updated, 1)

            x_rows = [x[:, tt, :] for tt in range(TT)]
            xs_rows = [xs[:, tt, :] for tt in range(TT)]

            def norm_x(name):
                mean_square_of(name, SQUARES.after(name, TT), D_MODEL)
                scale_rows(name, xs_rows, x_rows)
                split_norm(name, xn, KT)

            norm_x("ffn1_pre")
            up_stage(1)
            dve.wait_ge(post_gain_loaded, 16)
            down_stage(1, branch_b)
            add_branch("ffn1_post", branch_b, 4.0)
            norm_x("mix_pre")

            def copy_rows1(stage, i, q, b, dst):
                dve.wait_ge(pieces_multiplied, stream.pieces(stage, i, q))
                nc.vector.tensor_copy(dst, ps[:, b, :]).then_inc(rows1_copied, 1)

            def rotary(x_pairs, cos, sin, t1, t2, done):
                x1, x2 = x_pairs
                tt = nc.vector.tensor_tensor
                yield lambda: then(tt(t1, x2, sin, ALU.mult))
                yield lambda: then(tt(t2, x1, sin, ALU.mult))
                yield lambda: then(tt(x1, x1, cos, ALU.mult))
                yield lambda: tt(x1, x1, t1, ALU.subtract).then_inc(done, 1)
                yield lambda: then(tt(x2, x2, cos, ALU.mult))
                yield lambda: tt(x2, x2, t2, ALU.add).then_inc(done, 1)

            def diff_in(i, lead):
                for q in range(16):
                    split_piece(dve, "diff_in", i, q)
                    if lead and q == 2:
                        copy_rows1("diff_in", i - 1, 15, 3, proj_rows(i - 1, 1, 1))
                    if q == 10:
                        copy_rows1("diff_in", i, 7, 1, proj_rows(i, 0, 1))
            diff_in(0, False)
            with dve.Fori(1, 3) as i:
                diff_in(i, True)

            dqk_steps = []
            for n in range(2):
                for tt in range(TT):
                    h = proj[:, n, tt, :].rearrange("p (h two d) -> p h two d", two=2, d=64)
                    wide = [P, 2 * DIFF_HEADS, 64]
                    dqk_steps += rotary((h[:, :, 0, :], h[:, :, 1, :]),
                                        rope[:, tt, 0:64].unsqueeze(1).broadcast_to(wide),
                                        rope[:, tt, 64:128].unsqueeze(1).broadcast_to(wide),
                                        turn_a[:, :].rearrange("p (h d) -> p h d", d=64),
                                        turn_b[:, :].rearrange("p (h d) -> p h d", d=64), roped_dqk)
            dve.wait_ge(tables_loaded, 16 * 6)
            split_piece(dve, "rope_in", 0, 0)
            for q in range(16):
                split_piece(dve, "latent_in", 0, q)
                if q == 2:
                    copy_rows1("diff_in", 2, 15, 3, proj_rows(2, 1, 1))
                    dve.wait_ge(rows0_copied, TOKEN_MAJOR.after("diff_in", 4))
                    dve.wait_ge(rows1_copied, TOKEN_MAJOR.after("diff_in", 4))
                if 3 <= q < 15:
                    for step in dqk_steps[2 * (q - 3):2 * (q - 3) + 2]:
                        step()
                if q == 10:
                    copy_rows1("latent_in", 0, 7, 1, latent[:, 1, 0:RANK])
                    mean_square_of("cq", SQUARES.after("cq", TT), RANK)
                if q == 11:
                    rows = [latent[:, tt, 0:RANK] for tt in range(TT)]
                    dve.wait_ge(rows1_copied, TOKEN_MAJOR.after("cq"))
                    scale_rows("cq", rows, rows)
            split_norm("cq", cn[:, 0], RT)
            copy_rows1("latent_in", 0, 15, 3, latent[:, 1, RANK:2 * RANK])
            mean_square_of("ckv", SQUARES.after("ckv", TT), RANK)
            split_piece(dve, "expand", 0, 0)
            rows = [latent[:, tt, RANK:2 * RANK] for tt in range(TT)]
            dve.wait_ge(rows1_copied, TOKEN_MAJOR.after("ckv"))
            scale_rows("ckv", rows, rows)
            for q in (1, 2, 3):
                split_piece(dve, "expand", 0, q)
            copy_rows1("expand", 0, 1, 1, q_pe[:, 1, :])
            dve.wait_ge(roped_dqk, 8)
            for n in range(2):
                nc.vector.tensor_tensor_reduce(turn_a[:, n * DIFF_D:(n + 1) * DIFF_D], lam_vec[:, 2 * n, :], lam_vec[:, 2 * n + 1, :],
                                               1.0, 0.0, ALU.mult, ALU.add, lam[:, n:n + 1]).then_inc(lam_dots, 1)
            split_norm("ckv", cn[:, 1], RT)
            dve.wait_ge(lam_exps, 1)
            then(nc.vector.tensor_tensor(lam[:, 4:5], lam[:, 3:4], lam[:, 2:3], ALU.subtract))
            then(nc.vector.tensor_scalar(lam[:, 4:5], lam[:, 4:5], -LAMBDA_INIT, None, ALU.add))
            then(nc.vector.tensor_scalar(sub_gain[:, :], sub_gain[:, :], 1.0 - LAMBDA_INIT, None, ALU.mult))

            kr = latent[:, :, 2 * RANK:LATENT_W].rearrange("p t (two d) -> p t two d", two=2)
            cos32, sin32 = rope[:, :, 128:160], rope[:, :, 160:192]
            k_steps = list(rotary((kr[:, :, 0, :], kr[:, :, 1, :]), cos32, sin32,
                                  turn_a[:, 0:64].rearrange("p (t d) -> p t d", t=TT),
                                  turn_b[:, 0:64].rearrange("p (t d) -> p t d", t=TT), roped_k_pe))
            q_steps = []
            for tt in range(TT):
                qh = q_pe[:, tt, :].rearrange("p (h two d) -> p h two d", two=2, d=32)
                wide = [P, MLA_HEADS, 32]
                q_steps += rotary((qh[:, :, 0, :], qh[:, :, 1, :]),
                                  rope[:, tt, 128:160].unsqueeze(1).broadcast_to(wide),
                                  rope[:, tt, 160:192].unsqueeze(1).broadcast_to(wide),
                                  turn_a[:, 0:256].rearrange("p (h d) -> p h d", d=32),
                                  turn_b[:, 0:256].rearrange("p (h d) -> p h d", d=32), roped_q_pe)
            rest = k_steps + q_steps
            for j in range(1, 7):
                for q in (2 * j + 2, 2 * j + 3):
                    if q < 14:
                        split_piece(dve, "expand", 0, q)
                if j <= 4:
                    for n in (2 * j - 2, 2 * j - 1):
                        dve.wait_ge(nope_part, n + 1)
                        nc.vector.tensor_tensor(nope_t[:, n // 4, 2 * (n % 4):2 * (n % 4) + 2, :],
                                                ps[:, nope_bank(n):nope_bank(n) + 2, 0:SEQ], nope_part_buf[n % 2],
                                                ALU.add).then_inc(nope_done, 1)
                else:
                    copy_rows1("expand", 0, 2 * j + 1, V_BANK[j - 5] + 1, v_tok[:, 1, (j - 5) * NB:(j - 4) * NB])
                if j == 1:
                    dve.wait_ge(k_rope_copied, 1)
                    dve.wait_ge(rows0_copied, TOKEN_MAJOR.after("q_pe"))
                    dve.wait_ge(rows1_copied, TOKEN_MAJOR.after("q_pe"))
                for step in rest[3 * j - 3:3 * j]:
                    step()

            dve.wait_ge(mask_ready, 3)
            dve.wait_ge(rows0_copied, TOKEN_MAJOR.after("v", 2))

            def mask_scores(s):
                if s >= 4:
                    dve.wait_ge(probs_turned, ((s - 4) // 2 if s - 4 < 2 * DIFF_HEADS else s - 4 - DIFF_HEADS) + 1)
                dve.wait_ge(scores_ready, s + 1)
                scale = DIFF_D ** -0.5 if s < 2 * DIFF_HEADS else QK_DIM ** -0.5
                for tt, (a, b) in enumerate(Q_COLS):
                    nc.vector.tensor_tensor_reduce(probs[:, s % 4, a:b], ps[:, s % 2, a:b], mask[:, a:b], -scale, 3.0e38,
                                                   ALU.add, ALU.min, row_min[:, s, tt:tt + 1])\
                        .then_inc(scores_masked, 1)

            def normalise(s):
                dve.wait_ge(exps_done, 2 * s + 2)
                then(nc.vector.reciprocal(row_inv[:, s, :], row_sum[:, s, :]))
                second = s < 2 * DIFF_HEADS and s % 2
                if second:
                    then(nc.vector.tensor_scalar(row_inv[:, s, :], row_inv[:, s, :], lam[:, 4:5], None, ALU.mult))
                for tt, (a, b) in enumerate(Q_COLS):
                    inv = row_inv[:, s, tt:tt + 1]
                    if second:
                        nc.vector.scalar_tensor_tensor(out=probs[:, (s - 1) % 4, a:b], in0=probs[:, s % 4, a:b], scalar=inv,
                                                       in1=probs[:, (s - 1) % 4, a:b], op0=ALU.mult, op1=ALU.add)\
                            .then_inc(probs_ready, 1)
                    elif s < 2 * DIFF_HEADS:
                        then(nc.vector.tensor_scalar(probs[:, s % 4, a:b], probs[:, s % 4, a:b], inv, None, ALU.mult))
                    else:
                        nc.vector.tensor_scalar(probs[:, s % 4, a:b], probs[:, s % 4, a:b], inv, None, ALU.mult)\
                            .then_inc(probs_ready, 1)

            def split_mla(u):
                m = u - DIFF_HEADS
                dve.wait_ge(mla_rounded, m + 1)
                nc.vector.tensor_tensor(mixed[:, m, 1, :], ps[:, 4 + u % 2, 0:SEQ], mixed[:, m, 0, :].bitcast(F32),
                                        ALU.subtract).then_inc(mla_split, 1)

            def norm_diff(d):
                k = RSQRT.at["diff"] + d
                dve.wait_ge(rms_inverted, k + 1)
                if d >= 2:
                    dve.wait_ge(diff_turned, d - 1)
                for tt in range(TT):
                    nc.vector.scalar_tensor_tensor(out=diff_out[:, d % 2, tt, :],
                                                   in0=ps[:, 4 + d % 2, tt * DIFF_V:(tt + 1) * DIFF_V],
                                                   scalar=inv_rms[:, k, tt:tt + 1], in1=sub_gain[:, :],
                                                   op0=ALU.mult, op1=ALU.mult).then_inc(diff_normed, 1)

            def split_diff(d):
                k = MLA_HEADS + 2 * d
                dve.wait_ge(diff_rounded, d + 1)
                nc.vector.tensor_tensor(mixed[:, k:k + 2, 1, :], ps[:, 6, :].rearrange("p (k s) -> p k s", k=2),
                                        mixed[:, k:k + 2, 0, :].bitcast(F32), ALU.subtract).then_inc(diff_split, 1)

            for t in range(MAPS + 3):
                if t < MAPS:
                    mask_scores(t)
                if 1 <= t <= MAPS:
                    normalise(t - 1)
                u = unit_of(t - 3)
                if u is not None:
                    if u < DIFF_HEADS:
                        mean_square_of(f"diff:{u}", SQUARES.after("diff", TT * (u + 1)), DIFF_V)
                    else:
                        split_mla(u)
                u = unit_of(t - 4)
                if u is not None and u < DIFF_HEADS:
                    norm_diff(u)
                u = unit_of(t - 5)
                if u is not None and u < DIFF_HEADS:
                    split_diff(u)

            dve.wait_ge(post_gain_loaded, 32)

            def out_body(b, lead):
                for q in range(8):
                    split_piece(dve, "out", b, q)
                    if lead and q == 3:
                        branch_block("mix_post", branch_a, b - 1)
            out_body(0, False)
            with dve.Fori(1, 4) as b:
                out_body(b, True)
            branch_block("mix_post", branch_a, 3)
            add_branch("mix_post", branch_a, 1.0)
            norm_x("ffn2_pre")
            up_stage(2)
            dve.wait_ge(post_gain_loaded, 48)
            down_stage(2, branch_b)
            add_branch("ffn2_post", branch_b, 4.0)

        @block.tensor
        def _(pe):
            mm = nc.tensor.matmul

            def ready(name, i, q):
                pe.wait_ge(pieces_split, stream.pieces(name, i, q))

            def feature_major(b, slot, col, right, start, stop):
                mm(ps[:, b, :], w_hi[:, slot, col:col + P], right.rearrange("p a s -> p (a s)"), start=start, stop=False)
                return mm(ps[:, b, 0:SEQ], w_lo[:, slot, col:col + P], right[:, 0, :], start=False, stop=stop)

            def token_major(dst, left, slot, cols, start, stop):
                mm(dst, left[:, 0, :], w_hi[:, slot, cols], start=start, stop=False)
                mm(dst, left[:, 0, :], w_lo[:, slot, cols], start=False, stop=False)
                return mm(dst, left[:, 1, :], w_hi[:, slot, cols], start=False, stop=stop)

            def turn_norm(name, src, g):
                if g == 0:
                    pe.wait_ge(scaled, SCALED.after(name, TT))
                ring = 2 if name in ("cq", "ckv") else 4
                if name == "ckv":
                    pe.wait_ge(norm_split, NORM_TILES.after("cq", 2 * g + 2))
                elif g >= ring:
                    pe.wait_ge(norm_split, NORM_TILES.after(name, 2 * (g - ring) + 2))
                for k in (2 * g, 2 * g + 1):
                    for tt in range(TT):
                        last = nc.tensor.transpose(norm_bank(name, k)[:, tt * P:(tt + 1) * P],
                                                   src[tt][:, k * P:(k + 1) * P], ident[:, :])
                last.then_inc(norm_turned, 1)

            def turn_heads(name, g):
                b = turn_bank(name, g)
                for h, tt, src in heads_of(name, g):
                    rows = src.shape[1]
                    last = nc.tensor.transpose(ps[0:rows, b, h * SEQ + tt * P:h * SEQ + (tt + 1) * P], src, ident[:, :])
                last.then_inc(qk_turned, 1)

            xs_rows = [xs[:, tt, :] for tt in range(TT)]

            def up_stage(L, norm):
                for g in range(KT // 2):
                    turn_norm(norm, xs_rows, g)
                with pe.Fori(0, FT // 2) as i:
                    for q in range(8):
                        side, k0 = q // 4, 4 * (q % 4)
                        if q % 4 == 0:
                            pe.wait_ge((gate_banks_free, up_banks_free)[side], (L - 1) * (FT // 2) + i + 1)
                        if side == 0:
                            pe.wait_ge(norm_split, NORM_TILES.after(norm, k0 + 4))
                        ready(f"up{L}", i, q)
                        for f in range(2):
                            for k in range(4):
                                last = feature_major(4 + 2 * side + f, q % SPLIT, k * 256 + f * P, xn[:, k0 + k, :, :],
                                                     start=k0 + k == 0, stop=k0 + k == KT - 1)
                        last.then_inc(pieces_multiplied, 1)

            def column_blocks(stage, left, tiles, operands_ready):
                with pe.Fori(0, 4) as b:
                    for q in range(tiles // 2):
                        operands_ready(q)
                        ready(stage, b, q)
                        for k in (2 * q, 2 * q + 1):
                            for tt in range(TT):
                                last = token_major(bank(2 * b + tt), left[:, k, :, tt * P:(tt + 1) * P], q % SPLIT,
                                                   slice((k % 2) * NB, (k % 2 + 1) * NB), start=k == 0, stop=k == tiles - 1)
                        last.then_inc(pieces_multiplied, 1)

            def hidden_ready(L):
                return lambda q: pe.wait_ge(hidden_split, (L - 1) * (FT // 2) + q + 1)

            pe.wait_ge(ident_ready, 2)
            pe.wait_ge(gains_loaded, 16 * 5)
            nc.tensor.transpose(ps[:, 4, 0:GAIN_ROWS], up[0:GAIN_ROWS, 0, 0:P], ident[0:GAIN_ROWS, 0:GAIN_ROWS])\
                .then_inc(gains_turned, 1)
            up_stage(1, "ffn1_pre")
            column_blocks("down1", hidden, FT, hidden_ready(1))

            for g in range(KT // 2):
                turn_norm("mix_pre", xs_rows, g)

            def in_block(stage, i, blk, q):
                ready(stage, i, 8 * blk + q)
                for k in (2 * q, 2 * q + 1):
                    for tt in range(TT):
                        last = token_major(ps[:, 2 * blk + tt, :], xn[:, k, :, tt * P:(tt + 1) * P], q % SPLIT,
                                           slice((k % 2) * NB, (k % 2 + 1) * NB), start=k == 0, stop=k == KT - 1)
                last.then_inc(pieces_multiplied, 1)

            def diff_in(i, lead):
                for blk in range(2):
                    for q in range(8):
                        if q == 0 and lead:
                            pe.wait_ge(rows0_copied, 2 * i + (blk - 1))
                            pe.wait_ge(rows1_copied, 2 * i + (blk - 1))
                        if not lead and blk == 0:
                            pe.wait_ge(norm_split, NORM_TILES.after("mix_pre", 2 * q + 2))
                        in_block("diff_in", i, blk, q)
            diff_in(0, False)
            with pe.Fori(1, 3) as i:
                diff_in(i, True)

            ready("rope_in", 0, 0)
            for tt in range(TT):
                for k in range(KT):
                    last = token_major(ps[:, K_ROPE_BANK, tt * ROPE:(tt + 1) * ROPE], xn[:, k, :, tt * P:(tt + 1) * P], 0,
                                       slice(k * ROPE, (k + 1) * ROPE), start=k == 0, stop=k == KT - 1)
            last.then_inc(pieces_multiplied, 1)

            for blk in range(2):
                for q in range(8):
                    if q == 0:
                        pe.wait_ge(rows0_copied, TOKEN_MAJOR.after("diff_in", 5 + blk))
                        pe.wait_ge(rows1_copied, TOKEN_MAJOR.after("diff_in", 5 + blk))
                    in_block("latent_in", 0, blk, q)
                    if blk == 1 and q in (2, 3):
                        for g in (2 * (q - 2), 2 * (q - 2) + 1):
                            pe.wait_ge(roped_dqk, 4)
                            pe.wait_ge(k_rope_copied, 1)
                            if g >= 2:
                                pe.wait_ge(qk_copied, QK_TURNS.after("dqk", g - 1))
                            turn_heads("dqk", g)
                    if blk == 1 and q == 5:
                        for g in range(RT // 2):
                            turn_norm("cq", [latent[:, tt, 0:RANK] for tt in range(TT)], g)
            def expand_rows(j, b0, c):
                for q in (2 * j, 2 * j + 1):
                    ready("expand", 0, q)
                    for k in (2 * (q % 2), 2 * (q % 2) + 1):
                        for tt in range(TT):
                            last = token_major(ps[:, b0 + tt, :], cn[:, c, k, :, tt * P:(tt + 1) * P], q % SPLIT,
                                               slice((k % 2) * NB, (k % 2 + 1) * NB), start=k == 0, stop=k == RT - 1)
                    last.then_inc(pieces_multiplied, 1)

            pe.wait_ge(norm_split, NORM_TILES.after("cq", RT))
            pe.wait_ge(rows0_copied, TOKEN_MAJOR.after("cq"))
            pe.wait_ge(rows1_copied, TOKEN_MAJOR.after("cq"))
            expand_rows(0, 0, 0)
            for g in range(RT // 2):
                turn_norm("ckv", [latent[:, tt, RANK:2 * RANK] for tt in range(TT)], g)
            pe.wait_ge(roped_dqk, 8)
            for g in range(4, 8):
                pe.wait_ge(qk_copied, QK_TURNS.after("dqk", g - 1))
                turn_heads("dqk", g)
            for j in range(1, 5):
                for q in (2 * j, 2 * j + 1):
                    ready("expand", 0, q)
                    for n in (2 * j - 2, 2 * j - 1):
                        if q % 2 == 0:
                            if n == 0:
                                pe.wait_ge(rows0_copied, TOKEN_MAJOR.after("ckv"))
                                pe.wait_ge(rows1_copied, TOKEN_MAJOR.after("ckv"))
                            elif n == 1:
                                pe.wait_ge(rows0_copied, TOKEN_MAJOR.after("q_pe"))
                                pe.wait_ge(rows1_copied, TOKEN_MAJOR.after("q_pe"))
                            elif n == 2:
                                pe.wait_ge(norm_split, NORM_TILES.after("ckv", RT))
                            elif n == 3:
                                pe.wait_ge(qk_copied, QK_TURNS.after("dqk", 8))
                            else:
                                pe.wait_ge(nope_done, n - 3)
                        for h in range(2):
                            for k in (2 * (q % 2), 2 * (q % 2) + 1):
                                last = feature_major(nope_bank(n) + h, q % SPLIT, (k % 2) * NB + (2 * (n % 2) + h) * P,
                                                     cn[:, n // 4, k, :, :], start=k == 0, stop=k == RT - 1)
                    last.then_inc(pieces_multiplied, 1)
            for j in (5, 6):
                pe.wait_ge(nope_done, j)
                expand_rows(j, V_BANK[j - 5], 1)
            pe.wait_ge(nope_done, 8)
            pe.wait_ge(roped_k_pe, 2)
            turn_heads("k_pe", 0)
            pe.wait_ge(roped_q_pe, 4)
            for g in range(MLA_HEADS // 2):
                if g == 3:
                    pe.wait_ge(qk_copied, QK_TURNS.after("k_pe"))
                turn_heads("q_pe", g)

            def scores(s):
                b = s % 2
                if s >= 2:
                    pe.wait_ge(scores_masked, 2 * (s - 2) + 2)
                for tt, (a, e) in enumerate(Q_COLS):
                    q_cols, n = slice(tt * P, (tt + 1) * P), e - a
                    if s < 2 * DIFF_HEADS:
                        last = mm(ps[:, b, a:e], dqk_t[:, 0, s, q_cols], dqk_t[:, 1, s, 0:n], start=True, stop=True)
                    else:
                        m = s - 2 * DIFF_HEADS
                        mm(ps[:, b, a:e], nope_t[:, 0, m, q_cols], nope_t[:, 1, m, 0:n], start=True, stop=False)
                        last = mm(ps[:, b, a:e], q_pe_t[:, m, q_cols], k_pe_t[:, 0:n], start=False, stop=True)
                last.then_inc(scores_ready, 1)

            def turn_probs(u):
                pe.wait_ge(probs_ready, 2 * u + 2)
                if u >= 2:
                    pe.wait_ge(probs_copied, u - 1)
                for n in range(3):
                    last = nc.tensor.transpose(ps[:, 2 + u % 2, n * P:(n + 1) * P],
                                               probs[:, first_map(u) % 4, n * P:(n + 1) * P], ident[:, :])
                last.then_inc(probs_turned, 1)

            def values(u):
                b = 4 + u % 2
                pe.wait_ge(probs_copied, u + 1)
                if 2 <= u < 2 + DIFF_HEADS:
                    pe.wait_ge(diff_normed, 2 * (u - 2) + 2)
                elif u >= 2 + DIFF_HEADS:
                    pe.wait_ge(mla_split, u - 2 - DIFF_HEADS + 1)
                for tt in range(TT):
                    for kb in range(tt + 1):
                        block_t = probs_t[:, u % 2, (tt + kb) * P:(tt + kb + 1) * P]
                        if u < DIFF_HEADS:
                            last = mm(ps[:, b, tt * DIFF_V:(tt + 1) * DIFF_V], block_t,
                                      proj[:, 2, kb, u * DIFF_V:(u + 1) * DIFF_V], start=kb == 0, stop=kb == tt)
                        else:
                            m = u - DIFF_HEADS
                            last = mm(ps[:, b, tt * P:(tt + 1) * P], v_tok[:, kb, m * P:(m + 1) * P], block_t,
                                      start=kb == 0, stop=kb == tt)
                last.then_inc(values_summed, 1)

            def turn_diff(d):
                pe.wait_ge(diff_normed, 2 * d + 2)
                if d >= 1:
                    pe.wait_ge(diff_split, d)
                for e in range(2):
                    for tt in range(TT):
                        last = nc.tensor.transpose(ps[:, 6, e * SEQ + tt * P:e * SEQ + (tt + 1) * P],
                                                   diff_out[:, d % 2, tt, e * P:(e + 1) * P], ident[:, :])
                last.then_inc(diff_turned, 1)

            pe.wait_ge(qk_copied, QK_TURNS.after("q_pe", MLA_HEADS // 2))
            pe.wait_ge(rows0_copied, TOKEN_MAJOR.after("v", 2))
            pe.wait_ge(rows1_copied, TOKEN_MAJOR.after("v", 2))
            for t in range(MAPS + 3):
                if t < MAPS:
                    scores(t)
                if unit_of(t - 2) is not None:
                    turn_probs(unit_of(t - 2))
                if unit_of(t - 3) is not None:
                    values(unit_of(t - 3))
                u = unit_of(t - 5)
                if u is not None and u < DIFF_HEADS:
                    turn_diff(u)

            pe.wait_ge(mla_split, MLA_HEADS)
            pe.wait_ge(diff_split, DIFF_HEADS)
            column_blocks("out", mixed, KT, lambda q: None)
            up_stage(2, "ffn2_pre")
            column_blocks("down2", hidden, FT, hidden_ready(2))


_OUT = ((1, SEQ, D_MODEL), "float32")


def _rope_table():
    cols = []
    for d in (DIFF_D, ROPE):
        inv_freq = np.float32(10000.0) ** (-np.arange(0, d, 2, dtype=np.float32) / np.float32(d))
        angle = np.arange(SEQ, dtype=np.float32)[:, None] * inv_freq[None, :].astype(np.float32)
        cols += [np.cos(angle), np.sin(angle)]
    return np.ascontiguousarray(np.concatenate(cols, axis=1).astype(np.float32))


def kernel(**inputs):
    import concourse.bacc as _bacc
    from concourse.bass_utils import run_bass_kernel_spmd as _run

    nc = _bacc.Bacc("TRN2", target_bir_lowering=False, num_devices=1)
    arrays, io = {}, {}
    for name, a in [*inputs.items(), ("rope_table", _rope_table())]:
        a = np.ascontiguousarray(a)
        arrays[f"in_{name}"] = a
        io[name] = nc.dram_tensor(f"in_{name}", a.shape, mybir.dt.from_np(a.dtype), kind="ExternalInput").ap()
    out = nc.dram_tensor("out", _OUT[0], mybir.dt.from_np(np.dtype(_OUT[1])), kind="ExternalOutput").ap()
    encoder_block(nc, io, out)
    return _run(nc, [arrays], core_ids=[0]).results[0]["out"]
```

```python
from contextlib import ExitStack

import numpy as np

import concourse.bass as bass
from concourse import mybir

F32 = mybir.dt.float32
F32R = mybir.dt.float32r
ALU = mybir.AluOpType
ACT = mybir.ActivationFunctionType
AX_X = mybir.AxisListType.X

P = 128
SEQ, D_MODEL, D_FF = 256, 2048, 5632
TT = SEQ // P
KT = D_MODEL // P
FT = D_FF // P
RANK = 512
RT = RANK // P
MLA_HEADS, NOPE, ROPE, MLA_V = 8, 128, 64, 128
QK_DIM = NOPE + ROPE
DIFF_HEADS, DIFF_D = 4, 128
DIFF_V = 2 * DIFF_D
DIFF_W = DIFF_HEADS * 2 * DIFF_D
LATENT_W = 2 * RANK + ROPE
EPS = 1e-6
LAMBDA_INIT = 0.2
CHUNK_FRAMES = 64
MASKED = -1.0e30

RAW = 4
SPLIT = 4
LEAD = 3
CHUNK = 2048
PIECE = CHUNK // 2
NB = 512
BANKS = 8
MAPS = 2 * DIFF_HEADS + MLA_HEADS
UNITS = DIFF_HEADS + MLA_HEADS
MAP_W = P + 2 * P
OUT_PIECE_STEPS = (MAPS - 2, MAPS - 1, MAPS, MAPS + 1)
Q_COLS = [(0, P), (P, MAP_W)]


class Stage:

    def __init__(self, name, iters, chunks, pieces_per_chunk=2, dmas=1):
        self.name, self.iters, self.chunks, self.ppc, self.dmas = name, iters, chunks, pieces_per_chunk, dmas
        self.pieces = chunks * pieces_per_chunk


def stage_list():
    return [
        Stage("up1", FT // 2, 4), Stage("down1", 4, FT // 4),
        Stage("diff_in", 3, 8), Stage("rope_in", 1, 1, 1), Stage("latent_in", 1, 8),
        Stage("expand", 1, 7, dmas=RT), Stage("out", 4, 4),
        Stage("up2", FT // 2, 4), Stage("down2", 4, FT // 4),
    ]


class Stream:

    def __init__(self):
        self.stages = {s.name: s for s in stage_list()}
        self.piece0, self.fill0, self.raw_owner, self.split_owner = {}, {}, {}, {}
        self.first_raw, self.first_split, raw_at, split_at = {}, {}, 0, 0
        piece, fills, raw_last, split_last = 0, [0] * RAW, {}, {}
        for s in self.stages.values():
            self.piece0[s.name] = piece
            self.fill0[s.name] = list(fills)
            self.first_raw[s.name], self.first_split[s.name] = raw_at, split_at
            for i in range(s.iters):
                for j in range(s.chunks):
                    r = self.raw_slot(s.name, j)
                    self.raw_owner[s.name, i, j] = raw_last.get(r)
                    raw_last[r] = piece + (j + 1) * s.ppc
                    fills[r] += s.dmas
                for q in range(s.pieces):
                    r = self.split_slot(s.name, q)
                    self.split_owner[s.name, i, q] = split_last.get(r)
                    split_last[r] = piece + q + 1
                piece += s.pieces
            raw_at, split_at = (raw_at + s.chunks) % RAW, (split_at + s.pieces) % SPLIT

    def raw_slot(self, name, j):
        return (self.first_raw[name] + j) % RAW

    def split_slot(self, name, q):
        return (self.first_split[name] + q) % SPLIT

    def pieces(self, name, i, q):
        return self.piece0[name] + i * self.stages[name].pieces + q + 1

    def filled(self, name, i, j):
        s = self.stages[name]
        per = len(range(j % RAW, s.chunks, RAW))
        return 16 * (self.fill0[name][self.raw_slot(name, j)] + s.dmas * (j // RAW + 1)) + i * (16 * s.dmas * per)

    def owner(self, table, name, i, q):
        if isinstance(i, int):
            return table[name, i, q]
        s = self.stages[name]
        return table[name, 1, q] + (i - 1) * s.pieces


class Order:

    def __init__(self, *events):
        self.at, n = {}, 0
        for name, count in events:
            self.at[name] = n
            n += count

    def after(self, name, n=1):
        return self.at[name] + n


RSQRT = Order(("ffn1_pre", 1), ("ffn1_post", 1), ("mix_pre", 1), ("cq", 1), ("ckv", 1),
              ("diff", DIFF_HEADS), ("mix_post", 1), ("ffn2_pre", 1), ("ffn2_post", 1))
N_RSQRT = RSQRT.after("ffn2_post")
SQUARES = Order(("ffn1_pre", TT), ("ffn1_post", 4 * TT), ("mix_pre", TT), ("cq", TT), ("ckv", TT),
                ("diff", DIFF_HEADS * TT), ("mix_post", 4 * TT), ("ffn2_pre", TT), ("ffn2_post", 4 * TT))
SCALED = Order(("cq", TT), ("ckv", TT))
NORM_GROUPS = Order(("ffn1_pre", KT // 2), ("mix_pre", KT // 2), ("cq", RT // 2), ("ckv", RT // 2),
                    ("ffn2_pre", KT // 2))
NORM_TILES = Order(("ffn1_pre", KT), ("mix_pre", KT), ("cq", RT), ("ckv", RT), ("ffn2_pre", KT))
TOKEN_MAJOR = Order(("diff_in", 6), ("cq", 1), ("ckv", 1), ("q_pe", 1), ("v", 2))
QK_TURNS = Order(("dqk", 8), ("k_pe", 1), ("q_pe", MLA_HEADS // 2))
RESIDUAL = Order(("ffn1_post", 4 * TT), ("mix_post", 4 * TT), ("ffn2_post", 4 * TT))
BRANCH = Order(("ffn1_post", 4 * TT), ("mix_post", 4 * TT), ("ffn2_post", 4 * TT))
GAIN_COLS = {"ffn1_pre": 0, "mix_pre": KT, "ffn2_pre": 2 * KT, "cq": 3 * KT, "ckv": 3 * KT + RT}
GAIN_ROWS = 3 * KT + 2 * RT
LATER_GAINS = ("mix_pre_g", "ffn2_pre_g", "mla_q_norm_g", "mla_kv_norm_g")

COLUMN_BLOCKS = D_MODEL // NB
TILES = KT // COLUMN_BLOCKS
PIECES_WITH_TILES = {"up1": ((), (0, 1, 2), (3,), (4,)), "diff_in": ((3,), (4,), (5,), (6,)), "up2": ((3,), (4,), (5,), (6,))}
PRE_NORM = {"up1": "ffn1_pre", "diff_in": "mix_pre", "up2": "ffn2_pre"}
X_FROM = {"ffn1_pre": None, "mix_pre": "ffn1_post", "ffn2_pre": "mix_post"}


def encoder_block(nc, io, out):
    stream = Stream()

    with ExitStack() as ctx:
        def sb(name, shape, dt=F32):
            return ctx.enter_context(nc.sbuf_tensor(name, shape, dt))

        def sem(name):
            return ctx.enter_context(nc.semaphore(name))

        x = sb("x", [P, TT, D_MODEL])
        w_raw = sb("w_raw", [P, RAW, CHUNK])
        w_hi = sb("w_hi", [P, SPLIT, PIECE], F32R)
        w_lo = sb("w_lo", [P, SPLIT, PIECE], F32R)
        post_gain = sb("post_gain", [P, D_MODEL])
        rms_row = post_gain[:, 0:SEQ]
        rms_diag = post_gain[:, SEQ:2 * SEQ]
        ones = post_gain[:, 2 * SEQ:2 * SEQ + P]
        part = sb("part", [P, 2, SEQ])
        gate = sb("gate", [P, 2, SEQ])
        up = sb("up", [P, 2, SEQ])
        ident = sb("ident", [P, P])
        gains = sb("gains", [P, GAIN_ROWS])
        square_sum = sb("square_sum", [P, N_RSQRT, TT])
        block_squares = sb("block_squares", [P, TT, 4])
        mean_square = sb("mean_square", [P, N_RSQRT, TT])
        inv_rms = sb("inv_rms", [P, N_RSQRT, TT])
        minus_half = sb("minus_half", [P, TT])

        def region(name, size):
            sb(name, [P, size // 4])
            start, end = nc.sbuf_base - size, [0]

            def place(name, shape, dt=F32, at=None):
                at = end[0] if at is None else at
                end[0] = at + 4 * int(np.prod(shape[1:]))
                assert end[0] <= size, (name, end[0], size)
                return nc.alloc_sbuf_tensor_at(name, shape, dt, offset=start + at)

            return place

        in_b = region("region_b", KT * 2 * SEQ * 4)
        in_a = region("region_a", FT * 2 * SEQ * 4)

        xn = in_b("xn", [P, KT, 2, SEQ], F32R)
        branch_b = in_b("branch_b", [P, COLUMN_BLOCKS, TT, NB], at=KT * SEQ * 4)
        cn = in_b("cn", [P, 2, RT, 2, SEQ], F32R, at=0)
        mixed = in_b("mixed", [P, KT, 2, SEQ], F32R, at=0)

        hidden = in_a("hidden", [P, FT, 2, SEQ], F32R)
        proj = in_a("proj", [P, 3, TT, DIFF_W], at=0)
        dqk_t = in_a("dqk_t", [P, 2, 2 * DIFF_HEADS, SEQ])
        latent_at = 4 * (3 * TT * DIFF_W + 4 * DIFF_HEADS * SEQ)
        latent = in_a("latent", [P, TT, LATENT_W])
        v_tok = in_a("v_tok", [P, TT, MLA_HEADS * MLA_V])
        q_pe_t = in_a("q_pe_t", [ROPE, MLA_HEADS, SEQ])
        k_pe_t = in_a("k_pe_t", [ROPE, SEQ])
        q_pe = in_a("q_pe", [P, TT, MLA_HEADS * ROPE])
        turn_a = in_a("turn_a", [P, 512])
        turn_b = in_a("turn_b", [P, 512])
        rope = in_a("rope", [P, TT, 2 * (64 + 32)])
        mask = in_a("mask", [P, MAP_W])
        sub_gain = in_a("sub_gain", [P, DIFF_V])
        probs_t = in_a("probs_t", [P, 2, MAP_W])
        small = in_a("small", [P, 8 + 3 * TT * MAPS])
        probs = in_a("probs", [P, 4, MAP_W])
        lam_vec = in_a("lam_vec", [P, 4, DIFF_D], at=probs.manual_sbuf_range[0] - proj.manual_sbuf_range[0])
        nope_t = in_a("nope_t", [P, 2, MLA_HEADS, SEQ], at=0)
        diff_out = in_a("diff_out", [P, 2, TT, DIFF_V], at=latent_at)
        x_squares = in_a("x_squares", [P, TT, D_MODEL], at=0)
        branch_a = in_a("branch_a", [P, COLUMN_BLOCKS, TT, NB], at=4 * TT * D_MODEL)

        lam = small[:, 0:8]
        row_min, row_sum, row_inv = (
            small[:, 8 + n * TT * MAPS:8 + (n + 1) * TT * MAPS].rearrange("p (m t) -> p m t", t=TT)
            for n in range(3))

        ps = ctx.enter_context(nc.psum_tensor("ps", [P, BANKS, NB], F32))

        raw_filled = [sem(f"raw_filled{r}") for r in range(RAW)]
        pieces_rounded = sem("pieces_rounded")
        pieces_split = sem("pieces_split")
        pieces_multiplied = sem("pieces_multiplied")
        x_loaded = [sem(f"x_loaded{c}") for c in range(COLUMN_BLOCKS)]
        gain_loaded = sem("gain_loaded")
        gains_loaded = sem("gains_loaded")
        tables_loaded = sem("tables_loaded")
        post_gain_loaded = sem("post_gain_loaded")
        ident_ready = sem("ident_ready")
        consts_ready = sem("consts_ready")
        mask_ready = sem("mask_ready")
        gains_turned = sem("gains_turned")
        gains_ready = sem("gains_ready")
        squares_summed = sem("squares_summed")
        mean_squares = sem("mean_squares")
        rms_inverted = sem("rms_inverted")
        vector_step = sem("vector_step")
        scaled = sem("scaled")
        diag_ready = sem("diag_ready")
        row_summed = sem("row_summed")
        row_copied = sem("row_copied")
        norm_turned = sem("norm_turned")
        norm_rounded = sem("norm_rounded")
        norm_split = sem("norm_split")
        part_copied = sem("part_copied")
        gate_banks_free = sem("gate_banks_free")
        up_banks_free = sem("up_banks_free")
        gate_scaled = sem("gate_scaled")
        up_scaled = sem("up_scaled")
        silu_done = sem("silu_done")
        hidden_full = sem("hidden_full")
        hidden_rounded = sem("hidden_rounded")
        hidden_split = sem("hidden_split")
        branch_done = sem("branch_done")
        x_updated = sem("x_updated")
        rows0_copied = sem("rows0_copied")
        rows1_copied = sem("rows1_copied")
        nope_part = sem("nope_part")
        nope_done = sem("nope_done")
        k_rope_copied = sem("k_rope_copied")
        roped_k_pe = sem("roped_k_pe")
        roped_q_pe = sem("roped_q_pe")
        roped_dqk = sem("roped_dqk")
        qk_turned = sem("qk_turned")
        qk_copied = sem("qk_copied")
        lam_dots = sem("lam_dots")
        lam_exps = sem("lam_exps")
        scores_ready = sem("scores_ready")
        scores_masked = sem("scores_masked")
        exps_done = sem("exps_done")
        probs_ready = sem("probs_ready")
        probs_turned = sem("probs_turned")
        probs_copied = sem("probs_copied")
        values_summed = sem("values_summed")
        mla_rounded = sem("mla_rounded")
        mla_split = sem("mla_split")
        diff_normed = sem("diff_normed")
        diff_turned = sem("diff_turned")
        diff_rounded = sem("diff_rounded")
        diff_split = sem("diff_split")
        stored = sem("stored")

        block = ctx.enter_context(nc.Block())

        def rows_by_tile(w):
            return w[0].rearrange("(k p) n -> p k n", p=P)

        def columns(w, k0, nk, start, n):
            return rows_by_tile(w)[:, k0:k0 + nk, bass.ds(start, n)]

        ukv = io["mla_w_ukv"][0].rearrange("(k p) (h c) -> p k h c", p=P, c=NOPE + MLA_V)
        uq = io["mla_w_uq"][0].rearrange("(k p) (h c) -> p k h c", p=P, c=QK_DIM)

        def expand_chunk(j):
            if j == 0:
                return [(uq[:, k, :, NOPE:QK_DIM], k) for k in range(RT)]
            w, c0 = [(uq, 0), (ukv, 0), (ukv, NOPE)][(j - 1) // 2]
            h0 = 4 * ((j - 1) % 2)
            return [(w[:, k, h0:h0 + 4, c0:c0 + P], k) for k in range(RT)]

        def load(sp, name, i, j):
            free = stream.owner(stream.raw_owner, name, i, j)
            if free is not None:
                sp.wait_ge(pieces_split, free)
            slot, full = w_raw[:, stream.raw_slot(name, j), :], raw_filled[stream.raw_slot(name, j)]
            if name in ("up1", "up2"):
                w = io[f"ffn{name[2]}_w_{('gate', 'up')[j // 2]}"]
                src = columns(w, 8 * (j % 2), 8, i * 256, 256)
                sp.dma_start(slot.rearrange("p (k n) -> p k n", k=8), src).then_inc(full, 16)
            elif name in ("down1", "down2"):
                src = columns(io[f"ffn{name[4]}_w_down"], 4 * j, 4, i * NB, NB)
                sp.dma_start(slot.rearrange("p (k n) -> p k n", k=4), src).then_inc(full, 16)
            elif name == "diff_in":
                src = columns(io["w_in"], 4 * (j % 4), 4, i * 2 * NB + (LATENT_W + NB * (j // 4)), NB)
                sp.dma_start(slot.rearrange("p (k n) -> p k n", k=4), src).then_inc(full, 16)
            elif name == "latent_in":
                src = columns(io["w_in"], 4 * (j % 4), 4, NB * (j // 4), NB)
                sp.dma_start(slot.rearrange("p (k n) -> p k n", k=4), src).then_inc(full, 16)
            elif name == "rope_in":
                src = columns(io["w_in"], 0, KT, 2 * RANK, ROPE)
                sp.dma_start(slot[:, 0:PIECE].rearrange("p (k n) -> p k n", k=KT), src).then_inc(full, 16)
            elif name == "expand":
                for src, k in expand_chunk(j):
                    dst = slot[:, k * NB:(k + 1) * NB].rearrange("p (h c) -> p h c", h=src.shape[1])
                    sp.dma_start(dst, src).then_inc(full, 16)
            else:
                src = columns(io["w_out"], 4 * j, 4, i * NB, NB)
                sp.dma_start(slot.rearrange("p (k n) -> p k n", k=4), src).then_inc(full, 16)

        def round_piece(act, name, i, q):
            s = stream.stages[name]
            j, half = q // s.ppc, q % s.ppc
            slot = stream.raw_slot(name, j)
            act.wait_ge(raw_filled[slot], stream.filled(name, i, j))
            free = stream.owner(stream.split_owner, name, i, q)
            if free is not None:
                act.wait_ge(pieces_multiplied, free)
            nc.scalar.activation(w_hi[:, stream.split_slot(name, q), :],
                                 w_raw[:, slot, half * PIECE:(half + 1) * PIECE], ACT.Copy).then_inc(pieces_rounded, 1)

        def split_piece(dve, name, i, q):
            s = stream.stages[name]
            j, half = q // s.ppc, q % s.ppc
            dve.wait_ge(pieces_rounded, stream.pieces(name, i, q))
            slot = stream.split_slot(name, q)
            nc.vector.tensor_tensor(w_lo[:, slot, :],
                                    w_raw[:, stream.raw_slot(name, j), half * PIECE:(half + 1) * PIECE],
                                    w_hi[:, slot, :].bitcast(F32), ALU.subtract)\
                .then_inc(pieces_split, 1)

        def norm_bank(name, k):
            first, ring = {"cq": (4, 2), "ckv": (4, 2), "mix_pre": (2, 4)}.get(name, (0, 4))
            return ps[:, first + (k // 2) % ring, (k % 2) * SEQ:(k % 2 + 1) * SEQ]

        def turn_bank(name, g):
            return 6 + g % 2 if name == "dqk" else 4 if name == "k_pe" else 4 + (g + 1) % 4

        def nope_bank(n):
            return (2, 0, 4, 6)[n % 4]

        K_ROPE_BANK = 6
        V_BANK = (2, 0)

        nope_part_buf = (part[:, :, :], up[:, :, :])

        def bank(b):
            return ps[:, bass.ds(b, 1), :].rearrange("p a n -> p (a n)")

        def proj_rows(i, blk, tt):
            return proj[:, bass.ds(i, 1), tt, blk * NB:(blk + 1) * NB].rearrange("p a n -> p (a n)")

        def heads_of(name, g):
            for tt in range(TT):
                if name == "k_pe":
                    yield 0, tt, latent[:, tt, 2 * RANK:LATENT_W]
                for h in range(2):
                    if name == "dqk":
                        yield h, tt, proj[:, g // 4, tt, (2 * (g % 4) + h) * P:(2 * (g % 4) + h + 1) * P]
                    if name == "q_pe":
                        yield h, tt, q_pe[:, tt, (2 * g + h) * ROPE:(2 * g + h + 1) * ROPE]

        def turned(name, g):
            if name == "k_pe":
                return k_pe_t[:, :].rearrange("p (h s) -> p h s", h=1), ROPE
            if name == "q_pe":
                return q_pe_t[:, 2 * g:2 * g + 2, :], ROPE
            return dqk_t[:, g // 4, 2 * (g % 4):2 * (g % 4) + 2, :], P

        def unit_of(s):
            if s < 0 or s >= MAPS:
                return None
            if s < 2 * DIFF_HEADS:
                return s // 2 if s % 2 else None
            return s - DIFF_HEADS

        def first_map(u):
            return 2 * u if u < DIFF_HEADS else u + DIFF_HEADS

        @block.sync
        def _(sp):
            x_in = io["x"][0].rearrange("(t p) n -> p t n", p=P)
            for name, s in stream.stages.items():
                for j in range(s.chunks):
                    if name == "up1" and j < 2:
                        for c in (2 * j, 2 * j + 1):
                            cols = slice(c * NB, (c + 1) * NB)
                            sp.dma_start(x[:, :, cols], x_in[:, :, cols]).then_inc(x_loaded[c], 16)
                    load(sp, name, 0, j)
                if s.iters > 1:
                    with sp.Fori(1, s.iters) as i:
                        for j in range(s.chunks):
                            load(sp, name, i, j)
            x_out = out[0].rearrange("(t p) n -> p t n", p=P)
            for c in range(COLUMN_BLOCKS):
                sp.wait_ge(x_updated, RESIDUAL.after("ffn2_post", TT * (c + 1)))
                cols = slice(c * NB, (c + 1) * NB)
                sp.dma_start(x_out[:, :, cols], x[:, :, cols]).then_inc(stored, 16)
            sp.wait_ge(stored, 16 * COLUMN_BLOCKS)

        @block.gpsimd
        def _(pool):
            nc.gpsimd.memset(ident[:, :], 0.0).then_inc(ident_ready, 1)
            nc.gpsimd.memset(minus_half[:, :], -0.5).then_inc(consts_ready, 1)
            pool.wait_ge(ident_ready, 1)
            nc.gpsimd.affine_select(out=ident[:, :], in_=ident[:, :], compare_op=ALU.not_equal, fill=1.0,
                                    base=0, pattern=[[-1, P]], channel_multiplier=1).then_inc(ident_ready, 1)
            pool.wait_ge(consts_ready, 1)
            for n in range(N_RSQRT):
                if n == RSQRT.after("mix_pre"):
                    pool.wait_ge(x_updated, RESIDUAL.after("ffn1_post", 4 * TT))
                    nc.gpsimd.memset(mask[:, :], 0.0).then_inc(mask_ready, 1)
                    pool.wait_ge(mask_ready, 1)
                    for _, end in Q_COLS:
                        nc.gpsimd.memset(mask[0:CHUNK_FRAMES, end - CHUNK_FRAMES:end], MASKED)\
                            .then_inc(mask_ready, 1)
                pool.wait_ge(mean_squares, n + 1)
                nc.gpsimd.tensor_tensor(inv_rms[:, n, :], mean_square[:, n, :], minus_half[:, :], ALU.pow)\
                    .then_inc(rms_inverted, 1)

        @block.scalar
        def _(act):
            act.dma_start(up[0:KT, 0, 0:P], io["ffn1_pre_g"][0].rearrange("(k p) -> k p", p=P)).then_inc(gain_loaded, 16)
            row = 0
            for name in LATER_GAINS:
                g = io[name][0].rearrange("(k p) -> k p", p=P)
                act.dma_start(up[row:row + g.shape[0], 1, 0:P], g).then_inc(gains_loaded, 16)
                row += g.shape[0]

            def load_post_gain(name):
                act.dma_start(post_gain[:, :], io[name][0].partition_broadcast(P)).then_inc(post_gain_loaded, 16)

            dump = [t[:, :, :].rearrange("p a b -> p (a b)") for t in (gate, up)]

            def dump_free(name, n):
                act.wait_ge(squares_summed, SQUARES.at[name] - 1 + n)

            def square_rows(name, rows):
                for tt in range(TT):
                    dump_free(name, tt)
                    nc.scalar.activation(dump[tt], rows[tt], ACT.Square,
                                         accum_out=square_sum[:, RSQRT.at[name], tt:tt + 1])\
                        .then_inc(squares_summed, 1)

            def square_x(name):
                for c in range(COLUMN_BLOCKS):
                    if X_FROM[name] is None:
                        act.wait_ge(x_loaded[c], 16)
                if X_FROM[name] is not None:
                    act.wait_ge(x_updated, RESIDUAL.after(X_FROM[name], 4 * TT))
                for tt in range(TT):
                    nc.scalar.activation(x_squares[:, tt, :], x[:, tt, :], ACT.Square,
                                         accum_out=square_sum[:, RSQRT.at[name], tt:tt + 1])\
                        .then_inc(squares_summed, 1)

            def round_norm(name, dst, tiles):
                for k in tiles:
                    act.wait_ge(norm_turned, NORM_GROUPS.after(name, k // 2 + 1))
                    g = GAIN_COLS[name] + k
                    nc.scalar.activation(dst[:, k, 0, :], norm_bank(name, k), ACT.Copy, scale=gains[:, g:g + 1])\
                        .then_inc(norm_rounded, 1)

            def start_stage(stage):
                name = PRE_NORM[stage]
                for c, pieces in enumerate(PIECES_WITH_TILES[stage]):
                    if X_FROM[name] is not None and c == COLUMN_BLOCKS // 2:
                        act.wait_ge(x_updated, RESIDUAL.after(X_FROM[name], 4 * TT))
                    round_norm(name, xn, range(c * TILES, (c + 1) * TILES))
                    for q in pieces:
                        round_piece(act, stage, 0, q)
                for q in range(pieces[-1] + 1, LEAD + COLUMN_BLOCKS):
                    round_piece(act, stage, 0, q)
                square_x(name)

            def gate_part(L, i):
                act.wait_ge(pieces_multiplied, stream.pieces(f"up{L}", i, 3))
                nc.scalar.activation(part[:, :, :], ps[:, 4:6, SEQ:2 * SEQ], ACT.Copy).then_inc(part_copied, 1)

            def gate_silu(L, i):
                act.wait_ge(gate_scaled, (L - 1) * (FT // 2) + i + 1)
                nc.scalar.activation(gate[:, :, :], gate[:, :, :], ACT.Silu).then_inc(silu_done, 1)

            def up_part(L, i):
                act.wait_ge(pieces_multiplied, stream.pieces(f"up{L}", i, 7))
                nc.scalar.activation(part[:, :, :], ps[:, 6:8, SEQ:2 * SEQ], ACT.Copy).then_inc(part_copied, 1)

            def round_hidden(L, i):
                act.wait_ge(hidden_full, (L - 1) * (FT // 2) + i + 1)
                nc.scalar.activation(hidden[:, bass.ds(2 * i, 2), 0, :], up[:, :, :], ACT.Copy)\
                    .then_inc(hidden_rounded, 1)

            def square_block(name, stage, b):
                act.wait_ge(pieces_multiplied, stream.pieces(stage, b, stream.stages[stage].pieces - 1))
                for tt in range(TT):
                    dump_free(name, b * TT + tt)
                    if tt == 1:
                        act.wait_ge(branch_done, b * TT + BRANCH.after(name))
                    nc.scalar.activation(dump[tt], bank(2 * b + tt), ACT.Square,
                                         accum_out=block_squares[:, tt, bass.ds(b, 1)]).then_inc(squares_summed, 1)

            def up_stage(L):
                start_stage(f"up{L}")
                gate_part(L, 0)
                round_piece(act, f"up{L}", 0, 7)
                act.wait_ge(row_summed, L)
                nc.scalar.activation(rms_row, ps[:, 0, 0:SEQ], ACT.Copy).then_inc(row_copied, 1)
                if L == 1:
                    act.wait_ge(gains_turned, 2)
                    nc.scalar.activation(gains[:, KT:], ps[:, 1, 0:GAIN_ROWS - KT], ACT.Copy)\
                        .then_inc(gains_ready, 1)
                gate_silu(L, 0)
                with act.Fori(1, FT // 2) as i:
                    for q in range(8):
                        round_piece(act, f"up{L}", i, q)
                        if q == 2:
                            up_part(L, i - 1)
                        if q == 3:
                            round_hidden(L, i - 1)
                        if q == 6:
                            gate_part(L, i)
                        if q == 7:
                            gate_silu(L, i)

            def down_stage(L):
                stage = f"down{L}"

                def body(b, lead):
                    for q in range(stream.stages[stage].pieces):
                        round_piece(act, stage, b, q)
                        if not lead and q == 2:
                            up_part(L, FT // 2 - 1)
                        if not lead and q == 3:
                            round_hidden(L, FT // 2 - 1)
                            load_post_gain(f"ffn{L}_post_g")
                        if lead and q == 3:
                            square_block(f"ffn{L}_post", stage, b - 1)
                body(0, False)
                with act.Fori(1, 4) as b:
                    body(b, True)
                if L == 1:
                    for q in range(LEAD):
                        round_piece(act, "diff_in", 0, q)
                square_block(f"ffn{L}_post", stage, 3)

            act.wait_ge(gains_turned, 1)
            nc.scalar.activation(gains[:, 0:KT], ps[:, 4, 0:KT], ACT.Copy).then_inc(gains_ready, 1)
            act.wait_ge(gains_ready, 1)
            up_stage(1)
            down_stage(1)
            act.wait_ge(gains_ready, 2)
            start_stage("diff_in")
            load_post_gain("mix_post_g")
            act.dma_start(rope[:, :, :], io["rope_table"].rearrange("(t p) c -> p t c", p=P)).then_inc(tables_loaded, 16)
            act.dma_start(sub_gain[:, :], io["diff_subln_g"][0].partition_broadcast(P)).then_inc(tables_loaded, 16)
            for n, name in enumerate(("diff_lambda_q1", "diff_lambda_k1", "diff_lambda_q2", "diff_lambda_k2")):
                act.dma_start(lam_vec[:, n, :], io[name][0].partition_broadcast(P)).then_inc(tables_loaded, 16)
            mix_rms = inv_rms[:, RSQRT.at["mix_pre"], :]

            def copy_rows0(stage, i, q, b, dst, scale=1.0):
                act.wait_ge(pieces_multiplied, stream.pieces(stage, i, q))
                nc.scalar.activation(dst, ps[:, b, :], ACT.Copy, scale=scale).then_inc(rows0_copied, 1)

            def copy_turned(name, g):
                act.wait_ge(qk_turned, QK_TURNS.after(name, g + 1))
                dst, rows = turned(name, g)
                nc.scalar.activation(dst, ps[0:rows, turn_bank(name, g), 0:dst.shape[1] * SEQ]
                                     .rearrange("p (h s) -> p h s", s=SEQ), ACT.Copy).then_inc(qk_copied, 1)

            def diff_in(i, lead):
                for q in range(0 if lead else LEAD + COLUMN_BLOCKS, 16):
                    round_piece(act, "diff_in", i, q)
                    if lead and q == 2:
                        copy_rows0("diff_in", i - 1, 15, 2, proj_rows(i - 1, 1, 0), mix_rms[:, 0:1])
                    if q == 10:
                        if not lead:
                            act.wait_ge(rms_inverted, RSQRT.after("mix_pre"))
                        copy_rows0("diff_in", i, 7, 0, proj_rows(i, 0, 0), mix_rms[:, 0:1])
            diff_in(0, False)
            with act.Fori(1, 3) as i:
                diff_in(i, True)
            round_piece(act, "rope_in", 0, 0)
            for q in range(16):
                round_piece(act, "latent_in", 0, q)
                if q == 2:
                    copy_rows0("diff_in", 2, 15, 2, proj_rows(2, 1, 0), mix_rms[:, 0:1])
                    act.wait_ge(pieces_multiplied, stream.pieces("rope_in", 0, 0))
                    for tt in range(TT):
                        nc.scalar.activation(latent[:, tt, 2 * RANK:LATENT_W],
                                             ps[:, K_ROPE_BANK, tt * ROPE:(tt + 1) * ROPE],
                                             ACT.Copy, scale=mix_rms[:, tt:tt + 1]).then_inc(k_rope_copied, 1)
                if q == 10:
                    copy_rows0("latent_in", 0, 7, 0, latent[:, 0, 0:RANK], mix_rms[:, 0:1])
                    act.wait_ge(rows1_copied, TOKEN_MAJOR.after("cq"))
                    act.wait_ge(rows0_copied, TOKEN_MAJOR.after("cq"))
                    square_rows("cq", [latent[:, tt, 0:RANK] for tt in range(TT)])
                if q in (13, 14):
                    for g in (2 * (q - 13), 2 * (q - 13) + 1):
                        copy_turned("dqk", g)
            round_norm("cq", cn[:, 0], range(RT))
            copy_rows0("latent_in", 0, 15, 2, latent[:, 0, RANK:2 * RANK], mix_rms[:, 0:1])
            act.wait_ge(rows1_copied, TOKEN_MAJOR.after("ckv"))
            act.wait_ge(rows0_copied, TOKEN_MAJOR.after("ckv"))
            square_rows("ckv", [latent[:, tt, RANK:2 * RANK] for tt in range(TT)])
            for q in range(4):
                round_piece(act, "expand", 0, q)
            copy_rows0("expand", 0, 1, 0, q_pe[:, 0, :])
            for g in range(4, 8):
                copy_turned("dqk", g)
            round_norm("ckv", cn[:, 1], range(RT))
            act.wait_ge(lam_dots, 2)
            nc.scalar.activation(lam[:, 2:4], lam[:, 0:2], ACT.Exp).then_inc(lam_exps, 1)
            for j in range(1, 7):
                for q in (2 * j + 2, 2 * j + 3):
                    if q < 14:
                        round_piece(act, "expand", 0, q)
                if j <= 4:
                    for n in (2 * j - 2, 2 * j - 1):
                        act.wait_ge(pieces_multiplied, stream.pieces("expand", 0, 2 * j + 1))
                        if n >= 2:
                            act.wait_ge(nope_done, n - 1)
                        nc.scalar.activation(nope_part_buf[n % 2], ps[:, nope_bank(n):nope_bank(n) + 2, SEQ:2 * SEQ],
                                             ACT.Copy).then_inc(nope_part, 1)
                else:
                    copy_rows0("expand", 0, 2 * j + 1, V_BANK[j - 5], v_tok[:, 0, (j - 5) * NB:(j - 4) * NB])
            copy_turned("k_pe", 0)
            for g in range(MLA_HEADS // 2):
                copy_turned("q_pe", g)

            def exps(s):
                for tt, (a, b) in enumerate(Q_COLS):
                    act.wait_ge(scores_masked, 2 * s + tt + 1)
                    nc.scalar.activation(probs[:, s % 4, a:b], probs[:, s % 4, a:b], ACT.Exp, scale=-1.0,
                                         bias=row_min[:, s, tt:tt + 1], accum_out=row_sum[:, s, tt:tt + 1])\
                        .then_inc(exps_done, 1)

            def copy_probs(u):
                act.wait_ge(probs_turned, u + 1)
                if u >= 2:
                    act.wait_ge(values_summed, u - 1)
                nc.scalar.activation(probs_t[:, u % 2, :], ps[:, 2 + u % 2, 0:MAP_W], ACT.Copy).then_inc(probs_copied, 1)

            def round_mla(u):
                act.wait_ge(values_summed, u + 1)
                nc.scalar.activation(mixed[:, u - DIFF_HEADS, 0, :], ps[:, 4 + u % 2, 0:SEQ], ACT.Copy)\
                    .then_inc(mla_rounded, 1)

            def square_diff(d):
                act.wait_ge(values_summed, d + 1)
                for tt in range(TT):
                    dump_free("diff", TT * d + tt)
                    nc.scalar.activation(dump[tt][:, 0:DIFF_V], ps[:, 4 + d % 2, tt * DIFF_V:(tt + 1) * DIFF_V],
                                         ACT.Square, accum_out=square_sum[:, RSQRT.at["diff"] + d, tt:tt + 1])\
                        .then_inc(squares_summed, 1)

            def round_diff(d):
                act.wait_ge(diff_turned, d + 1)
                k = MLA_HEADS + 2 * d
                nc.scalar.activation(mixed[:, k:k + 2, 0, :], ps[:, 6, :].rearrange("p (k s) -> p k s", k=2), ACT.Copy)\
                    .then_inc(diff_rounded, 1)

            for t in range(MAPS + 3):
                if t in OUT_PIECE_STEPS:
                    round_piece(act, "out", 0, OUT_PIECE_STEPS.index(t))
                if t < MAPS:
                    exps(t)
                if unit_of(t - 2) is not None:
                    copy_probs(unit_of(t - 2))
                u = unit_of(t - 3)
                if u is not None:
                    if u < DIFF_HEADS:
                        square_diff(u)
                    else:
                        round_mla(u)
                u = unit_of(t - 5)
                if u is not None and u < DIFF_HEADS:
                    round_diff(u)

            def out_body(b, lead):
                for q in range(0 if lead else SPLIT, 8):
                    round_piece(act, "out", b, q)
                    if lead and q == 3:
                        square_block("mix_post", "out", b - 1)
            out_body(0, False)
            with act.Fori(1, 4) as b:
                out_body(b, True)
            for q in range(LEAD):
                round_piece(act, "up2", 0, q)
            square_block("mix_post", "out", 3)
            up_stage(2)
            down_stage(2)

        @block.vector
        def _(dve):
            steps = [0]

            def then(instruction):
                steps[0] += 1
                instruction.then_inc(vector_step, 1)
                dve.wait_ge(vector_step, steps[0])

            nc.vector.memset(mean_square[:, :, 0:1], 1.0).then_inc(gate_banks_free, 1)
            nc.vector.memset(mean_square[:, :, 1:2], 1.0).then_inc(up_banks_free, 1)
            dve.wait_ge(gate_banks_free, 1)
            dve.wait_ge(up_banks_free, 1)

            def mean_square_of(name, n, width, factor=1.0):
                dve.wait_ge(squares_summed, n)
                k = RSQRT.at[name.split(":")[0]] + (int(name.split(":")[1]) if ":" in name else 0)
                nc.vector.tensor_scalar(mean_square[:, k, :], square_sum[:, k, :], factor / width, factor * EPS,
                                        ALU.mult, ALU.add).then_inc(mean_squares, 1)
                return k

            def scale_rows(name, dst, src):
                k = RSQRT.at[name]
                dve.wait_ge(rms_inverted, k + 1)
                for tt in range(TT):
                    nc.vector.tensor_scalar(dst[tt], src[tt], inv_rms[:, k, tt:tt + 1], None, ALU.mult)\
                        .then_inc(scaled, 1)

            def split_norm(name, dst, tiles):
                for k in tiles:
                    if k % 2 == 0:
                        dve.wait_ge(norm_rounded, NORM_TILES.after(name, k + 2))
                    g = GAIN_COLS[name] + k
                    nc.vector.scalar_tensor_tensor(out=dst[:, k, 1, :], in0=norm_bank(name, k), scalar=gains[:, g:g + 1],
                                                   in1=dst[:, k, 0, :].bitcast(F32), op0=ALU.mult, op1=ALU.subtract)\
                        .then_inc(norm_split, 1)

            rms_of_token = rms_row.unsqueeze(1).broadcast_to([P, 2, SEQ])

            def gate_sum(L, i):
                dve.wait_ge(part_copied, (L - 1) * FT + 2 * i + 1)
                nc.vector.tensor_tensor(gate[:, :, :], ps[:, 4:6, 0:SEQ], part[:, :, :], ALU.add)\
                    .then_inc(gate_banks_free, 1)
                if isinstance(i, int):
                    dve.wait_ge(row_copied, L)
                dve.wait_ge(gate_banks_free, (L - 1) * (FT // 2) + i + 2)
                nc.vector.tensor_tensor(gate[:, :, :], gate[:, :, :], rms_of_token, ALU.mult).then_inc(gate_scaled, 1)

            def up_sum(L, i):
                dve.wait_ge(part_copied, (L - 1) * FT + 2 * i + 2)
                nc.vector.tensor_tensor(up[:, :, :], ps[:, 6:8, 0:SEQ], part[:, :, :], ALU.add)\
                    .then_inc(up_banks_free, 1)
                dve.wait_ge(up_banks_free, (L - 1) * (FT // 2) + i + 2)
                nc.vector.tensor_tensor(up[:, :, :], up[:, :, :], rms_of_token, ALU.mult).then_inc(up_scaled, 1)
                dve.wait_ge(up_scaled, (L - 1) * (FT // 2) + i + 1)
                dve.wait_ge(silu_done, (L - 1) * (FT // 2) + i + 1)
                nc.vector.tensor_tensor(up[:, :, :], up[:, :, :], gate[:, :, :], ALU.mult).then_inc(hidden_full, 1)

            def split_hidden(L, i):
                dve.wait_ge(hidden_rounded, (L - 1) * (FT // 2) + i + 1)
                nc.vector.tensor_tensor(hidden[:, bass.ds(2 * i, 2), 1, :], up[:, :, :],
                                        hidden[:, bass.ds(2 * i, 2), 0, :].bitcast(F32), ALU.subtract)\
                    .then_inc(hidden_split, 1)

            def up_stage(L, branch=None):
                start_stage(f"up{L}", branch)
                k = RSQRT.at[f"ffn{L}_pre"]
                nc.vector.memset(ones, 1.0).then_inc(diag_ready, 1)
                dve.wait_ge(rms_inverted, k + 1)
                for tt in range(TT):
                    nc.vector.tensor_scalar(rms_diag[:, tt * P:(tt + 1) * P], ident[:, :], inv_rms[:, k, tt:tt + 1],
                                            None, ALU.mult).then_inc(diag_ready, 1)
                split_piece(dve, f"up{L}", 0, 7)
                gate_sum(L, 0)
                with dve.Fori(1, FT // 2) as i:
                    for q in range(8):
                        split_piece(dve, f"up{L}", i, q)
                        if q == 2:
                            up_sum(L, i - 1)
                        if q == 3:
                            split_hidden(L, i - 1)
                        if q == 6:
                            gate_sum(L, i)

            def branch_block(name, stage, branch, b):
                dve.wait_ge(pieces_multiplied, stream.pieces(stage, b, stream.stages[stage].pieces - 1))
                for tt in reversed(range(TT)):
                    if tt == 0:
                        dve.wait_ge(squares_summed, b * TT + SQUARES.after(name))
                    nc.vector.tensor_tensor(branch[:, bass.ds(b, 1), tt, :].rearrange("p a n -> p (a n)"), bank(2 * b + tt),
                                            post_gain[:, bass.ds(b * NB, NB)], ALU.mult).then_inc(branch_done, 1)

            def down_stage(L, branch):
                stage, name = f"down{L}", f"ffn{L}_post"

                def body(b, lead):
                    for q in range(stream.stages[stage].pieces):
                        split_piece(dve, stage, b, q)
                        if not lead and q == 2:
                            up_sum(L, FT // 2 - 1)
                        if not lead and q == 3:
                            split_hidden(L, FT // 2 - 1)
                        if lead and q == 3:
                            branch_block(name, stage, branch, b - 1)
                body(0, False)
                dve.wait_ge(post_gain_loaded, 16 * (2 * L - 1))
                with dve.Fori(1, 4) as b:
                    body(b, True)
                if L == 1:
                    for q in range(LEAD):
                        split_piece(dve, "diff_in", 0, q)
                branch_block(name, stage, branch, 3)

            def invert_branch_rms(name, factor):
                k = RSQRT.at[name]
                dve.wait_ge(squares_summed, SQUARES.after(name, 4 * TT))
                then(nc.vector.tensor_reduce(square_sum[:, k, :], block_squares[:, :, :], AX_X, ALU.add))
                mean_square_of(name, SQUARES.after(name, 4 * TT), D_MODEL, factor)
                dve.wait_ge(branch_done, BRANCH.after(name, 4 * TT))
                dve.wait_ge(rms_inverted, k + 1)

            def update_x(name, branch, c):
                cols = slice(c * NB, (c + 1) * NB)
                for tt in range(TT):
                    nc.vector.scalar_tensor_tensor(out=x[:, tt, cols], in0=branch[:, c, tt, :],
                                                   scalar=inv_rms[:, RSQRT.at[name], tt:tt + 1],
                                                   in1=x[:, tt, cols], op0=ALU.mult, op1=ALU.add).then_inc(x_updated, 1)

            def start_stage(stage, branch=None):
                name = PRE_NORM[stage]
                if branch is not None:
                    for c in (0, 1):
                        update_x(X_FROM[name], branch, c)
                for c, pieces in enumerate(PIECES_WITH_TILES[stage]):
                    split_norm(name, xn, range(c * TILES, (c + 1) * TILES))
                    if branch is not None and c < 2:
                        update_x(X_FROM[name], branch, c + 2)
                    for q in pieces:
                        split_piece(dve, stage, 0, q)
                for q in range(pieces[-1] + 1, LEAD + COLUMN_BLOCKS):
                    split_piece(dve, stage, 0, q)
                mean_square_of(name, SQUARES.after(name, TT), D_MODEL)

            up_stage(1)
            down_stage(1, branch_b)
            invert_branch_rms("ffn1_post", 4.0)
            start_stage("diff_in", branch_b)
            mix_rms = inv_rms[:, RSQRT.at["mix_pre"], :]

            def copy_rows1(stage, i, q, b, dst, scale=None):
                dve.wait_ge(pieces_multiplied, stream.pieces(stage, i, q))
                if scale is None:
                    nc.vector.tensor_copy(dst, ps[:, b, :]).then_inc(rows1_copied, 1)
                else:
                    nc.vector.tensor_scalar(dst, ps[:, b, :], scale, None, ALU.mult).then_inc(rows1_copied, 1)

            def rotary_step(n, x_pairs, cos, sin, t1, t2, done):
                x1, x2 = x_pairs
                if n == 0:
                    then(nc.vector.tensor_tensor(t1, x2, sin, ALU.mult))
                elif n == 1:
                    then(nc.vector.tensor_tensor(t2, x1, sin, ALU.mult))
                elif n == 2:
                    then(nc.vector.tensor_tensor(x1, x1, cos, ALU.mult))
                elif n == 3:
                    nc.vector.tensor_tensor(x1, x1, t1, ALU.subtract).then_inc(done, 1)
                elif n == 4:
                    then(nc.vector.tensor_tensor(x2, x2, cos, ALU.mult))
                else:
                    nc.vector.tensor_tensor(x2, x2, t2, ALU.add).then_inc(done, 1)

            def rotate_dqk(step):
                n, tt = step // 12, step // 6 % 2
                h = proj[:, n, tt, :].rearrange("p (h two d) -> p h two d", two=2, d=64)
                wide = [P, 2 * DIFF_HEADS, 64]
                rotary_step(step % 6, (h[:, :, 0, :], h[:, :, 1, :]),
                            rope[:, tt, 0:64].unsqueeze(1).broadcast_to(wide),
                            rope[:, tt, 64:128].unsqueeze(1).broadcast_to(wide),
                            turn_a[:, :].rearrange("p (h d) -> p h d", d=64),
                            turn_b[:, :].rearrange("p (h d) -> p h d", d=64), roped_dqk)

            def rotate_pe(step):
                if step < 6:
                    kr = latent[:, :, 2 * RANK:LATENT_W].rearrange("p t (two d) -> p t two d", two=2)
                    rotary_step(step, (kr[:, :, 0, :], kr[:, :, 1, :]), rope[:, :, 128:160], rope[:, :, 160:192],
                                turn_a[:, 0:64].rearrange("p (t d) -> p t d", t=TT),
                                turn_b[:, 0:64].rearrange("p (t d) -> p t d", t=TT), roped_k_pe)
                else:
                    tt = step // 6 - 1
                    qh = q_pe[:, tt, :].rearrange("p (h two d) -> p h two d", two=2, d=32)
                    wide = [P, MLA_HEADS, 32]
                    rotary_step(step % 6, (qh[:, :, 0, :], qh[:, :, 1, :]),
                                rope[:, tt, 128:160].unsqueeze(1).broadcast_to(wide),
                                rope[:, tt, 160:192].unsqueeze(1).broadcast_to(wide),
                                turn_a[:, 0:256].rearrange("p (h d) -> p h d", d=32),
                                turn_b[:, 0:256].rearrange("p (h d) -> p h d", d=32), roped_q_pe)

            def diff_in(i, lead):
                for q in range(0 if lead else LEAD + COLUMN_BLOCKS, 16):
                    split_piece(dve, "diff_in", i, q)
                    if lead and q == 2:
                        copy_rows1("diff_in", i - 1, 15, 3, proj_rows(i - 1, 1, 1), mix_rms[:, 1:2])
                    if q == 10:
                        if not lead:
                            dve.wait_ge(rms_inverted, RSQRT.after("mix_pre"))
                        copy_rows1("diff_in", i, 7, 1, proj_rows(i, 0, 1), mix_rms[:, 1:2])
            diff_in(0, False)
            with dve.Fori(1, 3) as i:
                diff_in(i, True)

            dve.wait_ge(tables_loaded, 16 * 6)
            split_piece(dve, "rope_in", 0, 0)
            for q in range(16):
                split_piece(dve, "latent_in", 0, q)
                if q == 2:
                    copy_rows1("diff_in", 2, 15, 3, proj_rows(2, 1, 1), mix_rms[:, 1:2])
                    dve.wait_ge(rows0_copied, TOKEN_MAJOR.after("diff_in", 4))
                    dve.wait_ge(rows1_copied, TOKEN_MAJOR.after("diff_in", 4))
                if 3 <= q < 15:
                    for step in (2 * (q - 3), 2 * (q - 3) + 1):
                        rotate_dqk(step)
                if q == 10:
                    copy_rows1("latent_in", 0, 7, 1, latent[:, 1, 0:RANK], mix_rms[:, 1:2])
                    mean_square_of("cq", SQUARES.after("cq", TT), RANK)
                if q == 11:
                    rows = [latent[:, tt, 0:RANK] for tt in range(TT)]
                    dve.wait_ge(rows1_copied, TOKEN_MAJOR.after("cq"))
                    scale_rows("cq", rows, rows)
            split_norm("cq", cn[:, 0], range(RT))
            copy_rows1("latent_in", 0, 15, 3, latent[:, 1, RANK:2 * RANK], mix_rms[:, 1:2])
            mean_square_of("ckv", SQUARES.after("ckv", TT), RANK)
            split_piece(dve, "expand", 0, 0)
            rows = [latent[:, tt, RANK:2 * RANK] for tt in range(TT)]
            dve.wait_ge(rows1_copied, TOKEN_MAJOR.after("ckv"))
            scale_rows("ckv", rows, rows)
            for q in (1, 2, 3):
                split_piece(dve, "expand", 0, q)
            copy_rows1("expand", 0, 1, 1, q_pe[:, 1, :])
            dve.wait_ge(roped_dqk, 8)
            for n in range(2):
                nc.vector.tensor_tensor_reduce(turn_a[:, n * DIFF_D:(n + 1) * DIFF_D], lam_vec[:, 2 * n, :], lam_vec[:, 2 * n + 1, :],
                                               1.0, 0.0, ALU.mult, ALU.add, lam[:, n:n + 1]).then_inc(lam_dots, 1)
            split_norm("ckv", cn[:, 1], range(RT))
            dve.wait_ge(lam_exps, 1)
            then(nc.vector.tensor_tensor(lam[:, 4:5], lam[:, 3:4], lam[:, 2:3], ALU.subtract))
            then(nc.vector.tensor_scalar(lam[:, 4:5], lam[:, 4:5], -LAMBDA_INIT, None, ALU.add))
            then(nc.vector.tensor_scalar(sub_gain[:, :], sub_gain[:, :], 1.0 - LAMBDA_INIT, None, ALU.mult))

            for j in range(1, 7):
                for q in (2 * j + 2, 2 * j + 3):
                    if q < 14:
                        split_piece(dve, "expand", 0, q)
                if j <= 4:
                    for n in (2 * j - 2, 2 * j - 1):
                        dve.wait_ge(nope_part, n + 1)
                        nc.vector.tensor_tensor(nope_t[:, n // 4, 2 * (n % 4):2 * (n % 4) + 2, :],
                                                ps[:, nope_bank(n):nope_bank(n) + 2, 0:SEQ], nope_part_buf[n % 2],
                                                ALU.add).then_inc(nope_done, 1)
                else:
                    copy_rows1("expand", 0, 2 * j + 1, V_BANK[j - 5] + 1, v_tok[:, 1, (j - 5) * NB:(j - 4) * NB])
                if j == 1:
                    dve.wait_ge(k_rope_copied, TT)
                    dve.wait_ge(rows0_copied, TOKEN_MAJOR.after("q_pe"))
                    dve.wait_ge(rows1_copied, TOKEN_MAJOR.after("q_pe"))
                for step in range(3 * j - 3, 3 * j):
                    rotate_pe(step)

            dve.wait_ge(mask_ready, 3)
            dve.wait_ge(rows0_copied, TOKEN_MAJOR.after("v", 2))

            def mask_scores(s):
                if s >= 4:
                    dve.wait_ge(probs_turned, ((s - 4) // 2 if s - 4 < 2 * DIFF_HEADS else s - 4 - DIFF_HEADS) + 1)
                dve.wait_ge(scores_ready, s + 1)
                scale = DIFF_D ** -0.5 if s < 2 * DIFF_HEADS else QK_DIM ** -0.5
                for tt, (a, b) in enumerate(Q_COLS):
                    nc.vector.tensor_tensor_reduce(probs[:, s % 4, a:b], ps[:, s % 2, a:b], mask[:, a:b], -scale, 3.0e38,
                                                   ALU.add, ALU.min, row_min[:, s, tt:tt + 1])\
                        .then_inc(scores_masked, 1)

            def normalise(s):
                dve.wait_ge(exps_done, 2 * s + 2)
                then(nc.vector.reciprocal(row_inv[:, s, :], row_sum[:, s, :]))
                second = s < 2 * DIFF_HEADS and s % 2
                if second:
                    then(nc.vector.tensor_scalar(row_inv[:, s, :], row_inv[:, s, :], lam[:, 4:5], None, ALU.mult))
                for tt, (a, b) in enumerate(Q_COLS):
                    inv = row_inv[:, s, tt:tt + 1]
                    if second:
                        nc.vector.scalar_tensor_tensor(out=probs[:, (s - 1) % 4, a:b], in0=probs[:, s % 4, a:b], scalar=inv,
                                                       in1=probs[:, (s - 1) % 4, a:b], op0=ALU.mult, op1=ALU.add)\
                            .then_inc(probs_ready, 1)
                    elif s < 2 * DIFF_HEADS:
                        then(nc.vector.tensor_scalar(probs[:, s % 4, a:b], probs[:, s % 4, a:b], inv, None, ALU.mult))
                    else:
                        nc.vector.tensor_scalar(probs[:, s % 4, a:b], probs[:, s % 4, a:b], inv, None, ALU.mult)\
                            .then_inc(probs_ready, 1)

            def split_mla(u):
                m = u - DIFF_HEADS
                dve.wait_ge(mla_rounded, m + 1)
                nc.vector.tensor_tensor(mixed[:, m, 1, :], ps[:, 4 + u % 2, 0:SEQ], mixed[:, m, 0, :].bitcast(F32),
                                        ALU.subtract).then_inc(mla_split, 1)

            def norm_diff(d):
                k = RSQRT.at["diff"] + d
                dve.wait_ge(rms_inverted, k + 1)
                if d >= 2:
                    dve.wait_ge(diff_turned, d - 1)
                for tt in range(TT):
                    nc.vector.scalar_tensor_tensor(out=diff_out[:, d % 2, tt, :],
                                                   in0=ps[:, 4 + d % 2, tt * DIFF_V:(tt + 1) * DIFF_V],
                                                   scalar=inv_rms[:, k, tt:tt + 1], in1=sub_gain[:, :],
                                                   op0=ALU.mult, op1=ALU.mult).then_inc(diff_normed, 1)

            def split_diff(d):
                k = MLA_HEADS + 2 * d
                dve.wait_ge(diff_rounded, d + 1)
                nc.vector.tensor_tensor(mixed[:, k:k + 2, 1, :], ps[:, 6, :].rearrange("p (k s) -> p k s", k=2),
                                        mixed[:, k:k + 2, 0, :].bitcast(F32), ALU.subtract).then_inc(diff_split, 1)

            for t in range(MAPS + 3):
                if t in OUT_PIECE_STEPS:
                    split_piece(dve, "out", 0, OUT_PIECE_STEPS.index(t))
                if t < MAPS:
                    mask_scores(t)
                if 1 <= t <= MAPS:
                    normalise(t - 1)
                u = unit_of(t - 3)
                if u is not None:
                    if u < DIFF_HEADS:
                        mean_square_of(f"diff:{u}", SQUARES.after("diff", TT * (u + 1)), DIFF_V)
                    else:
                        split_mla(u)
                u = unit_of(t - 4)
                if u is not None and u < DIFF_HEADS:
                    norm_diff(u)
                u = unit_of(t - 5)
                if u is not None and u < DIFF_HEADS:
                    split_diff(u)

            dve.wait_ge(post_gain_loaded, 32)

            def out_body(b, lead):
                for q in range(0 if lead else SPLIT, 8):
                    split_piece(dve, "out", b, q)
                    if lead and q == 3:
                        branch_block("mix_post", "out", branch_a, b - 1)
            out_body(0, False)
            with dve.Fori(1, 4) as b:
                out_body(b, True)
            for q in range(LEAD):
                split_piece(dve, "up2", 0, q)
            branch_block("mix_post", "out", branch_a, 3)
            invert_branch_rms("mix_post", 1.0)
            up_stage(2, branch_a)
            down_stage(2, branch_b)
            invert_branch_rms("ffn2_post", 4.0)
            for c in range(COLUMN_BLOCKS):
                update_x("ffn2_post", branch_b, c)

        @block.tensor
        def _(pe):
            mm = nc.tensor.matmul

            def ready(name, i, q):
                pe.wait_ge(pieces_split, stream.pieces(name, i, q))

            def feature_major(b, slot, col, right, start, stop):
                mm(ps[:, b, :], w_hi[:, slot, col:col + P], right.rearrange("p a s -> p (a s)"), start=start, stop=False)
                return mm(ps[:, b, 0:SEQ], w_lo[:, slot, col:col + P], right[:, 0, :], start=False, stop=stop)

            def token_major(dst, left, slot, cols, start, stop):
                mm(dst, left[:, 0, :], w_hi[:, slot, cols], start=start, stop=False)
                mm(dst, left[:, 0, :], w_lo[:, slot, cols], start=False, stop=False)
                return mm(dst, left[:, 1, :], w_hi[:, slot, cols], start=False, stop=stop)

            def turn_norm(name, src, g):
                if name in ("cq", "ckv"):
                    pe.wait_ge(scaled, SCALED.after(name, TT))
                elif X_FROM[name] is None:
                    pe.wait_ge(x_loaded[2 * g // TILES], 16)
                else:
                    pe.wait_ge(x_updated, RESIDUAL.after(X_FROM[name], TT * (2 * g // TILES + 1)))
                ring = 2 if name in ("cq", "ckv") else 4
                if name == "ckv":
                    pe.wait_ge(norm_split, NORM_TILES.after("cq", 2 * g + 2))
                elif g >= ring:
                    pe.wait_ge(norm_split, NORM_TILES.after(name, 2 * (g - ring) + 2))
                for k in (2 * g, 2 * g + 1):
                    for tt in range(TT):
                        last = nc.tensor.transpose(norm_bank(name, k)[:, tt * P:(tt + 1) * P],
                                                   src[tt][:, k * P:(k + 1) * P], ident[:, :])
                last.then_inc(norm_turned, 1)

            def turn_heads(name, g):
                b = turn_bank(name, g)
                for h, tt, src in heads_of(name, g):
                    rows = src.shape[1]
                    last = nc.tensor.transpose(ps[0:rows, b, h * SEQ + tt * P:h * SEQ + (tt + 1) * P], src, ident[:, :])
                last.then_inc(qk_turned, 1)

            x_rows = [x[:, tt, :] for tt in range(TT)]

            def turn_block(name, c):
                for g in range(c * TILES // 2, (c + 1) * TILES // 2):
                    turn_norm(name, x_rows, g)

            def up_stage(L, norm):
                def body(i, first):
                    for q in range(8):
                        side, k0 = q // 4, 4 * (q % 4)
                        if q % 4 == 0:
                            pe.wait_ge((gate_banks_free, up_banks_free)[side], (L - 1) * (FT // 2) + i + 1)
                        if first and side == 0:
                            pe.wait_ge(norm_split, NORM_TILES.after(norm, k0 + 4))
                        ready(f"up{L}", i, q)
                        for f in range(2):
                            for k in range(4):
                                last = feature_major(4 + 2 * side + f, stream.split_slot(f"up{L}", q), k * 256 + f * P,
                                                     xn[:, k0 + k, :, :], start=k0 + k == 0, stop=k0 + k == KT - 1)
                        last.then_inc(pieces_multiplied, 1)
                        if first and q < 2:
                            turn_block(norm, q + 2)
                        if first and q == 5:
                            pe.wait_ge(diag_ready, L * (1 + TT))
                            mm(ps[:, 0, 0:SEQ], ones, rms_diag, start=True, stop=True).then_inc(row_summed, 1)
                            if L == 1:
                                pe.wait_ge(gains_loaded, 16 * len(LATER_GAINS))
                                n = GAIN_ROWS - KT
                                nc.tensor.transpose(ps[:, 1, 0:n], up[0:n, 1, 0:P], ident[0:n, 0:n])\
                                    .then_inc(gains_turned, 1)

                for c in (0, 1):
                    turn_block(norm, c)
                body(0, True)
                with pe.Fori(1, FT // 2) as i:
                    body(i, False)

            def column_blocks(stage, left, tiles, operands_ready):
                with pe.Fori(0, 4) as b:
                    for q in range(tiles // 2):
                        operands_ready(q)
                        ready(stage, b, q)
                        for k in (2 * q, 2 * q + 1):
                            for tt in range(TT):
                                last = token_major(bank(2 * b + tt), left[:, k, :, tt * P:(tt + 1) * P],
                                                   stream.split_slot(stage, q), slice((k % 2) * NB, (k % 2 + 1) * NB), start=k == 0, stop=k == tiles - 1)
                        last.then_inc(pieces_multiplied, 1)

            def hidden_ready(L):
                return lambda q: pe.wait_ge(hidden_split, (L - 1) * (FT // 2) + q + 1)

            pe.wait_ge(ident_ready, 2)
            pe.wait_ge(gain_loaded, 16)
            nc.tensor.transpose(ps[:, 4, 0:KT], up[0:KT, 0, 0:P], ident[0:KT, 0:KT]).then_inc(gains_turned, 1)
            up_stage(1, "ffn1_pre")
            column_blocks("down1", hidden, FT, hidden_ready(1))

            for c in (0, 1):
                turn_block("mix_pre", c)

            def in_block(stage, i, blk, q):
                ready(stage, i, 8 * blk + q)
                for k in (2 * q, 2 * q + 1):
                    for tt in range(TT):
                        last = token_major(ps[:, 2 * blk + tt, :], xn[:, k, :, tt * P:(tt + 1) * P],
                                           stream.split_slot(stage, 8 * blk + q), slice((k % 2) * NB, (k % 2 + 1) * NB), start=k == 0, stop=k == KT - 1)
                last.then_inc(pieces_multiplied, 1)

            def diff_in(i, lead):
                for blk in range(2):
                    for q in range(8):
                        if q == 0 and lead:
                            pe.wait_ge(rows0_copied, 2 * i + (blk - 1))
                            pe.wait_ge(rows1_copied, 2 * i + (blk - 1))
                        if not lead and blk == 0:
                            pe.wait_ge(norm_split, NORM_TILES.after("mix_pre", 2 * q + 2))
                        in_block("diff_in", i, blk, q)
                        if not lead and blk == 0 and q < 2:
                            turn_block("mix_pre", q + 2)
            diff_in(0, False)
            with pe.Fori(1, 3) as i:
                diff_in(i, True)

            ready("rope_in", 0, 0)
            for tt in range(TT):
                for k in range(KT):
                    last = token_major(ps[:, K_ROPE_BANK, tt * ROPE:(tt + 1) * ROPE], xn[:, k, :, tt * P:(tt + 1) * P],
                                       stream.split_slot("rope_in", 0), slice(k * ROPE, (k + 1) * ROPE), start=k == 0, stop=k == KT - 1)
            last.then_inc(pieces_multiplied, 1)

            for blk in range(2):
                for q in range(8):
                    if q == 0:
                        pe.wait_ge(rows0_copied, TOKEN_MAJOR.after("diff_in", 5 + blk))
                        pe.wait_ge(rows1_copied, TOKEN_MAJOR.after("diff_in", 5 + blk))
                    in_block("latent_in", 0, blk, q)
                    if blk == 1 and q in (2, 3):
                        for g in (2 * (q - 2), 2 * (q - 2) + 1):
                            pe.wait_ge(roped_dqk, 4)
                            pe.wait_ge(k_rope_copied, TT)
                            if g >= 2:
                                pe.wait_ge(qk_copied, QK_TURNS.after("dqk", g - 1))
                            turn_heads("dqk", g)
                    if blk == 1 and q == 5:
                        for g in range(RT // 2):
                            turn_norm("cq", [latent[:, tt, 0:RANK] for tt in range(TT)], g)
            def expand_rows(j, b0, c):
                for q in (2 * j, 2 * j + 1):
                    ready("expand", 0, q)
                    for k in (2 * (q % 2), 2 * (q % 2) + 1):
                        for tt in range(TT):
                            last = token_major(ps[:, b0 + tt, :], cn[:, c, k, :, tt * P:(tt + 1) * P],
                                               stream.split_slot("expand", q), slice((k % 2) * NB, (k % 2 + 1) * NB), start=k == 0, stop=k == RT - 1)
                    last.then_inc(pieces_multiplied, 1)

            pe.wait_ge(norm_split, NORM_TILES.after("cq", RT))
            pe.wait_ge(rows0_copied, TOKEN_MAJOR.after("cq"))
            pe.wait_ge(rows1_copied, TOKEN_MAJOR.after("cq"))
            expand_rows(0, 0, 0)
            for g in range(RT // 2):
                turn_norm("ckv", [latent[:, tt, RANK:2 * RANK] for tt in range(TT)], g)
            pe.wait_ge(roped_dqk, 8)
            for g in range(4, 8):
                pe.wait_ge(qk_copied, QK_TURNS.after("dqk", g - 1))
                turn_heads("dqk", g)
            for j in range(1, 5):
                for q in (2 * j, 2 * j + 1):
                    ready("expand", 0, q)
                    for n in (2 * j - 2, 2 * j - 1):
                        if q % 2 == 0:
                            if n == 0:
                                pe.wait_ge(rows0_copied, TOKEN_MAJOR.after("ckv"))
                                pe.wait_ge(rows1_copied, TOKEN_MAJOR.after("ckv"))
                            elif n == 1:
                                pe.wait_ge(rows0_copied, TOKEN_MAJOR.after("q_pe"))
                                pe.wait_ge(rows1_copied, TOKEN_MAJOR.after("q_pe"))
                            elif n == 2:
                                pe.wait_ge(norm_split, NORM_TILES.after("ckv", RT))
                            elif n == 3:
                                pe.wait_ge(qk_copied, QK_TURNS.after("dqk", 8))
                            else:
                                pe.wait_ge(nope_done, n - 3)
                        for h in range(2):
                            for k in (2 * (q % 2), 2 * (q % 2) + 1):
                                last = feature_major(nope_bank(n) + h, stream.split_slot("expand", q), (k % 2) * NB + (2 * (n % 2) + h) * P,
                                                     cn[:, n // 4, k, :, :], start=k == 0, stop=k == RT - 1)
                    last.then_inc(pieces_multiplied, 1)
            for j in (5, 6):
                pe.wait_ge(nope_done, j)
                expand_rows(j, V_BANK[j - 5], 1)
            pe.wait_ge(nope_done, 8)
            pe.wait_ge(roped_k_pe, 2)
            turn_heads("k_pe", 0)
            pe.wait_ge(roped_q_pe, 4)
            for g in range(MLA_HEADS // 2):
                if g == 3:
                    pe.wait_ge(qk_copied, QK_TURNS.after("k_pe"))
                turn_heads("q_pe", g)

            def scores(s):
                b = s % 2
                if s >= 2:
                    pe.wait_ge(scores_masked, 2 * (s - 2) + 2)
                for tt, (a, e) in enumerate(Q_COLS):
                    q_cols, n = slice(tt * P, (tt + 1) * P), e - a
                    if s < 2 * DIFF_HEADS:
                        last = mm(ps[:, b, a:e], dqk_t[:, 0, s, q_cols], dqk_t[:, 1, s, 0:n], start=True, stop=True)
                    else:
                        m = s - 2 * DIFF_HEADS
                        mm(ps[:, b, a:e], nope_t[:, 0, m, q_cols], nope_t[:, 1, m, 0:n], start=True, stop=False)
                        last = mm(ps[:, b, a:e], q_pe_t[:, m, q_cols], k_pe_t[:, 0:n], start=False, stop=True)
                last.then_inc(scores_ready, 1)

            def turn_probs(u):
                pe.wait_ge(probs_ready, 2 * u + 2)
                if u >= 2:
                    pe.wait_ge(probs_copied, u - 1)
                for n in range(3):
                    last = nc.tensor.transpose(ps[:, 2 + u % 2, n * P:(n + 1) * P],
                                               probs[:, first_map(u) % 4, n * P:(n + 1) * P], ident[:, :])
                last.then_inc(probs_turned, 1)

            def values(u):
                b = 4 + u % 2
                pe.wait_ge(probs_copied, u + 1)
                if 2 <= u < 2 + DIFF_HEADS:
                    pe.wait_ge(diff_normed, 2 * (u - 2) + 2)
                elif u >= 2 + DIFF_HEADS:
                    pe.wait_ge(mla_split, u - 2 - DIFF_HEADS + 1)
                for tt in range(TT):
                    for kb in range(tt + 1):
                        block_t = probs_t[:, u % 2, (tt + kb) * P:(tt + kb + 1) * P]
                        if u < DIFF_HEADS:
                            last = mm(ps[:, b, tt * DIFF_V:(tt + 1) * DIFF_V], block_t,
                                      proj[:, 2, kb, u * DIFF_V:(u + 1) * DIFF_V], start=kb == 0, stop=kb == tt)
                        else:
                            m = u - DIFF_HEADS
                            last = mm(ps[:, b, tt * P:(tt + 1) * P], v_tok[:, kb, m * P:(m + 1) * P], block_t,
                                      start=kb == 0, stop=kb == tt)
                last.then_inc(values_summed, 1)

            def turn_diff(d):
                pe.wait_ge(diff_normed, 2 * d + 2)
                if d >= 1:
                    pe.wait_ge(diff_split, d)
                for e in range(2):
                    for tt in range(TT):
                        last = nc.tensor.transpose(ps[:, 6, e * SEQ + tt * P:e * SEQ + (tt + 1) * P],
                                                   diff_out[:, d % 2, tt, e * P:(e + 1) * P], ident[:, :])
                last.then_inc(diff_turned, 1)

            pe.wait_ge(qk_copied, QK_TURNS.after("q_pe", MLA_HEADS // 2))
            pe.wait_ge(rows0_copied, TOKEN_MAJOR.after("v", 2))
            pe.wait_ge(rows1_copied, TOKEN_MAJOR.after("v", 2))
            for t in range(MAPS + 3):
                if t < MAPS:
                    scores(t)
                if unit_of(t - 2) is not None:
                    turn_probs(unit_of(t - 2))
                if unit_of(t - 3) is not None:
                    values(unit_of(t - 3))
                u = unit_of(t - 5)
                if u is not None and u < DIFF_HEADS:
                    turn_diff(u)

            pe.wait_ge(mla_split, MLA_HEADS)
            pe.wait_ge(diff_split, DIFF_HEADS)
            column_blocks("out", mixed, KT, lambda q: None)
            up_stage(2, "ffn2_pre")
            column_blocks("down2", hidden, FT, hidden_ready(2))


_OUT = ((1, SEQ, D_MODEL), "float32")


def _rope_table():
    cols = []
    for d in (DIFF_D, ROPE):
        inv_freq = np.float32(10000.0) ** (-np.arange(0, d, 2, dtype=np.float32) / np.float32(d))
        angle = np.arange(SEQ, dtype=np.float32)[:, None] * inv_freq[None, :].astype(np.float32)
        cols += [np.cos(angle), np.sin(angle)]
    return np.ascontiguousarray(np.concatenate(cols, axis=1).astype(np.float32))


def kernel(**inputs):
    import concourse.bacc as _bacc
    from concourse.bass_utils import run_bass_kernel_spmd as _run

    nc = _bacc.Bacc("TRN2", target_bir_lowering=False, num_devices=1, dynamic_dma_scratch_size=1024)
    arrays, io = {}, {}
    for name, a in [*inputs.items(), ("rope_table", _rope_table())]:
        a = np.ascontiguousarray(a)
        arrays[f"in_{name}"] = a
        io[name] = nc.dram_tensor(f"in_{name}", a.shape, mybir.dt.from_np(a.dtype), kind="ExternalInput").ap()
    out = nc.dram_tensor("out", _OUT[0], mybir.dt.from_np(np.dtype(_OUT[1])), kind="ExternalOutput").ap()
    encoder_block(nc, io, out)
    return _run(nc, [arrays], core_ids=[0]).results[0]["out"]
```

```python
from contextlib import ExitStack

import numpy as np

import concourse.bass as bass
from concourse import mybir

F32 = mybir.dt.float32
F32R = mybir.dt.float32r
ALU = mybir.AluOpType
ACT = mybir.ActivationFunctionType
AX_X = mybir.AxisListType.X

P = 128
SEQ, D_MODEL, D_FF = 256, 2048, 5632
TT = SEQ // P
KT = D_MODEL // P
FT = D_FF // P
RANK = 512
RT = RANK // P
MLA_HEADS, NOPE, ROPE, MLA_V = 8, 128, 64, 128
QK_DIM = NOPE + ROPE
DIFF_HEADS, DIFF_D = 4, 128
DIFF_V = 2 * DIFF_D
DIFF_W = DIFF_HEADS * 2 * DIFF_D
LATENT_W = 2 * RANK + ROPE
LATENT_BLOCKS = ((0, 384), (384, 384), (768, 320))
EPS = 1e-6
LAMBDA_INIT = 0.2
CHUNK_FRAMES = 64
MASKED = -1.0e30

RAW = 4
SPLIT = 4
LEAD = 3
CHUNK = 2048
PIECE = CHUNK // 2
NB = 512
BANKS = 8
MAPS = 2 * DIFF_HEADS + MLA_HEADS
MAP_W = P + 2 * P

DQK_TURN_PIECES = (12, 13, 19, 20)
V_PIECES = {0: 12, 1: 13}
V_STEPS = {1: (0, 0), 2: (0, 1), 3: (1, 0), 4: (1, 1)}
PE_TURN_STEPS = {5: ("k_pe", 0), 6: ("q_pe", 0), 7: ("q_pe", 1), 8: ("q_pe", 2), 9: ("q_pe", 3)}
OUT_SPLIT_STEPS = {10: 0, 12: 1, 13: 2, 14: 3, 15: 4, 16: 5, 17: 6, 18: 7}
OUT_STEPS = {13: 0, 14: 1, 15: 2, 16: 3, 17: 4, 18: 5}
Q_COLS = [(0, P), (P, MAP_W)]


class Stage:

    def __init__(self, name, iters, chunks, pieces_per_chunk=2, dmas=1):
        self.name, self.iters, self.chunks, self.ppc, self.dmas = name, iters, chunks, pieces_per_chunk, dmas
        self.pieces = chunks * pieces_per_chunk


def stage_list():
    return [
        Stage("up1", FT // 2, 4), Stage("down1", 4, FT // 4),
        Stage("diff_in", 3, 8), Stage("latent_in", 1, 12),
        Stage("expand", 1, 7, dmas=RT), Stage("out", 4, 4),
        Stage("up2", FT // 2, 4), Stage("down2", 4, FT // 4),
    ]


class Stream:

    def __init__(self):
        self.stages = {s.name: s for s in stage_list()}
        self.piece0, self.fill0, self.raw_owner, self.split_owner = {}, {}, {}, {}
        self.first_raw, self.first_split, raw_at, split_at = {}, {}, 0, 0
        piece, fills, raw_last, split_last = 0, [0] * RAW, {}, {}
        for s in self.stages.values():
            self.piece0[s.name] = piece
            self.fill0[s.name] = list(fills)
            self.first_raw[s.name], self.first_split[s.name] = raw_at, split_at
            for i in range(s.iters):
                for j in range(s.chunks):
                    r = self.raw_slot(s.name, j)
                    self.raw_owner[s.name, i, j] = raw_last.get(r)
                    raw_last[r] = piece + (j + 1) * s.ppc
                    fills[r] += s.dmas
                for q in range(s.pieces):
                    r = self.split_slot(s.name, q)
                    self.split_owner[s.name, i, q] = split_last.get(r)
                    split_last[r] = piece + q + 1
                piece += s.pieces
            raw_at, split_at = (raw_at + s.chunks) % RAW, (split_at + s.pieces) % SPLIT

    def raw_slot(self, name, j):
        return (self.first_raw[name] + j) % RAW

    def split_slot(self, name, q):
        return (self.first_split[name] + q) % SPLIT

    @staticmethod
    def columns(name, q):
        return LATENT_BLOCKS[q // 8][1] if name == "latent_in" else NB

    def pieces(self, name, i, q):
        return self.piece0[name] + i * self.stages[name].pieces + q + 1

    def filled(self, name, i, j):
        s = self.stages[name]
        per = len(range(j % RAW, s.chunks, RAW))
        return 16 * (self.fill0[name][self.raw_slot(name, j)] + s.dmas * (j // RAW + 1)) + i * (16 * s.dmas * per)

    def owner(self, table, name, i, q):
        if isinstance(i, int):
            return table[name, i, q]
        s = self.stages[name]
        return table[name, 1, q] + (i - 1) * s.pieces


class Order:

    def __init__(self, *events):
        self.at, n = {}, 0
        for name, count in events:
            self.at[name] = n
            n += count

    def after(self, name, n=1):
        return self.at[name] + n


RSQRT = Order(("ffn1_pre", 1), ("ffn1_post", 1), ("mix_pre", 1), ("cq", 1), ("ckv", 1),
              ("diff", DIFF_HEADS), ("mix_post", 1), ("ffn2_pre", 1), ("ffn2_post", 1))
N_RSQRT = RSQRT.after("ffn2_post")
SQUARES = Order(("ffn1_pre", TT), ("ffn1_post", 4 * TT), ("mix_pre", TT), ("cq", TT), ("ckv", TT),
                ("diff", DIFF_HEADS * TT), ("mix_post", 4 * TT), ("ffn2_pre", TT), ("ffn2_post", 4 * TT))
SCALED = Order(("cq", TT), ("ckv", TT))
NORM_GROUPS = Order(("ffn1_pre", KT // 2), ("mix_pre", KT // 2), ("cq", RT // 2), ("ckv", RT // 2),
                    ("ffn2_pre", KT // 2))
NORM_TILES = Order(("ffn1_pre", KT), ("mix_pre", KT), ("cq", RT), ("ckv", RT), ("ffn2_pre", KT))
TOKEN_MAJOR = Order(("diff_in", 6), ("latent", len(LATENT_BLOCKS)), ("q_pe", 1), ("v", 2))
LATENT_FULL = {"cq": TOKEN_MAJOR.after("latent", 2), "ckv": TOKEN_MAJOR.after("latent", 3)}
QK_TURNS = Order(("dqk", 8), ("k_pe", 1), ("q_pe", MLA_HEADS // 2))
RESIDUAL = Order(("ffn1_post", 4 * TT), ("mix_post", 4 * TT), ("ffn2_post", 4 * TT))
BRANCH = Order(("ffn1_post", 4 * TT), ("mix_post", 4 * TT), ("ffn2_post", 4 * TT))
GAIN_COLS = {"ffn1_pre": 0, "mix_pre": KT, "ffn2_pre": 2 * KT, "cq": 3 * KT, "ckv": 3 * KT + RT}
GAIN_ROWS = 3 * KT + 2 * RT
LATER_GAINS = ("mix_pre_g", "ffn2_pre_g", "mla_q_norm_g", "mla_kv_norm_g")

COLUMN_BLOCKS = D_MODEL // NB
TILES = KT // COLUMN_BLOCKS
PIECES_WITH_TILES = {"up1": ((0,), (1,), (2, 3), (4,)), "diff_in": ((3,), (4,), (5,), (6,)),
                     "up2": ((3,), (4,), (5,), (6,))}
PRE_NORM = {"up1": "ffn1_pre", "diff_in": "mix_pre", "up2": "ffn2_pre"}
X_FROM = {"ffn1_pre": None, "mix_pre": "ffn1_post", "ffn2_pre": "mix_post"}


def encoder_block(nc, io, out):
    stream = Stream()

    with ExitStack() as ctx:
        def sb(name, shape, dt=F32):
            return ctx.enter_context(nc.sbuf_tensor(name, shape, dt))

        def sem(name):
            return ctx.enter_context(nc.semaphore(name))

        x = sb("x", [P, TT, D_MODEL])
        w_raw = sb("w_raw", [P, RAW, CHUNK])
        w_hi = sb("w_hi", [P, SPLIT, PIECE], F32R)
        w_lo = sb("w_lo", [P, SPLIT, PIECE], F32R)
        post_gain = sb("post_gain", [P, D_MODEL])
        rms_row = post_gain[:, 0:SEQ]
        rms_diag = post_gain[:, SEQ:2 * SEQ]
        ones = post_gain[:, 2 * SEQ:2 * SEQ + P]
        part = sb("part", [P, 2, SEQ])
        gate = sb("gate", [P, 2, SEQ])
        up = sb("up", [P, 2, SEQ])
        ident = sb("ident", [P, P])
        gains = sb("gains", [P, GAIN_ROWS])
        square_sum = sb("square_sum", [P, N_RSQRT, TT])
        block_squares = sb("block_squares", [P, TT, 4])
        mean_square = sb("mean_square", [P, N_RSQRT, TT])
        inv_rms = sb("inv_rms", [P, N_RSQRT, TT])
        minus_half = sb("minus_half", [P, TT])

        def region(name, size):
            sb(name, [P, size // 4])
            start, end = nc.sbuf_base - size, [0]

            def place(name, shape, dt=F32, at=None):
                at = end[0] if at is None else at
                end[0] = at + 4 * int(np.prod(shape[1:]))
                assert end[0] <= size, (name, end[0], size)
                return nc.alloc_sbuf_tensor_at(name, shape, dt, offset=start + at)

            return place

        in_b = region("region_b", KT * 2 * SEQ * 4)
        in_a = region("region_a", FT * 2 * SEQ * 4)

        xn = in_b("xn", [P, KT, 2, SEQ], F32R)
        branch_b = in_b("branch_b", [P, COLUMN_BLOCKS, TT, NB], at=KT * SEQ * 4)
        cn = in_b("cn", [P, 2, RT, 2, SEQ], F32R, at=0)
        mixed = in_b("mixed", [P, KT, 2, SEQ], F32R, at=0)

        hidden = in_a("hidden", [P, FT, 2, SEQ], F32R)
        proj = in_a("proj", [P, 3, TT, DIFF_W], at=0)
        dqk_t = in_a("dqk_t", [P, 2, 2 * DIFF_HEADS, SEQ])
        latent_at = 4 * (3 * TT * DIFF_W + 4 * DIFF_HEADS * SEQ)
        latent = in_a("latent", [P, TT, LATENT_W])
        v_tok = in_a("v_tok", [P, TT, MLA_HEADS * MLA_V])
        q_pe_t = in_a("q_pe_t", [ROPE, MLA_HEADS, SEQ])
        k_pe_t = in_a("k_pe_t", [ROPE, SEQ])
        q_pe = in_a("q_pe", [P, TT, MLA_HEADS * ROPE])
        turn_a = in_a("turn_a", [P, 512])
        turn_b = in_a("turn_b", [P, 512])
        rope = in_a("rope", [P, TT, 2 * (64 + 32)])
        mask = in_a("mask", [P, MAP_W])
        sub_gain = in_a("sub_gain", [P, DIFF_V])
        probs_t = in_a("probs_t", [P, 2, MAP_W])
        small = in_a("small", [P, 8 + 3 * TT * MAPS])
        probs = in_a("probs", [P, 4, MAP_W])
        lam_vec = in_a("lam_vec", [P, 4, DIFF_D], at=probs.manual_sbuf_range[0] - proj.manual_sbuf_range[0])
        nope_t = in_a("nope_t", [P, 2, MLA_HEADS, SEQ], at=0)
        diff_out = in_a("diff_out", [P, 2, TT, DIFF_V], at=latent_at)
        x_squares = in_a("x_squares", [P, TT, D_MODEL], at=0)
        branch_a = in_a("branch_a", [P, COLUMN_BLOCKS, TT, NB], at=4 * TT * D_MODEL)

        lam = small[:, 0:8]
        row_min, row_sum, row_inv = (
            small[:, 8 + n * TT * MAPS:8 + (n + 1) * TT * MAPS].rearrange("p (m t) -> p m t", t=TT)
            for n in range(3))

        ps = ctx.enter_context(nc.psum_tensor("ps", [P, BANKS, NB], F32))

        raw_filled = [sem(f"raw_filled{r}") for r in range(RAW)]
        pieces_rounded = sem("pieces_rounded")
        pieces_split = sem("pieces_split")
        pieces_multiplied = sem("pieces_multiplied")
        x_loaded = [sem(f"x_loaded{c}") for c in range(COLUMN_BLOCKS)]
        gain_loaded = sem("gain_loaded")
        gains_loaded = sem("gains_loaded")
        tables_loaded = sem("tables_loaded")
        post_gain_loaded = sem("post_gain_loaded")
        ident_ready = sem("ident_ready")
        consts_ready = sem("consts_ready")
        mask_ready = sem("mask_ready")
        gains_turned = sem("gains_turned")
        gains_ready = sem("gains_ready")
        squares_summed = sem("squares_summed")
        mean_squares = sem("mean_squares")
        rms_inverted = sem("rms_inverted")
        vector_step = sem("vector_step")
        scaled = sem("scaled")
        diag_ready = sem("diag_ready")
        row_summed = sem("row_summed")
        row_copied = sem("row_copied")
        norm_turned = sem("norm_turned")
        norm_rounded = sem("norm_rounded")
        norm_split = sem("norm_split")
        part_copied = sem("part_copied")
        gate_banks_free = sem("gate_banks_free")
        up_banks_free = sem("up_banks_free")
        gate_scaled = sem("gate_scaled")
        up_scaled = sem("up_scaled")
        silu_done = sem("silu_done")
        hidden_full = sem("hidden_full")
        hidden_rounded = sem("hidden_rounded")
        hidden_split = sem("hidden_split")
        branch_done = sem("branch_done")
        x_updated = sem("x_updated")
        rows0_copied = sem("rows0_copied")
        rows1_copied = sem("rows1_copied")
        nope_part = sem("nope_part")
        nope_done = sem("nope_done")
        roped_k_pe = sem("roped_k_pe")
        roped_q_pe = sem("roped_q_pe")
        roped_dqk = sem("roped_dqk")
        qk_turned = sem("qk_turned")
        qk_copied = sem("qk_copied")
        lam_dots = sem("lam_dots")
        lam_exps = sem("lam_exps")
        scores_ready = sem("scores_ready")
        scores_masked = sem("scores_masked")
        exps_done = sem("exps_done")
        probs_ready = sem("probs_ready")
        probs_turned = sem("probs_turned")
        probs_copied = sem("probs_copied")
        values_summed = sem("values_summed")
        v_summed = sem("v_summed")
        mla_rounded = sem("mla_rounded")
        mla_split = sem("mla_split")
        diff_normed = sem("diff_normed")
        diff_turned = sem("diff_turned")
        diff_rounded = sem("diff_rounded")
        diff_split = sem("diff_split")
        stored = sem("stored")

        block = ctx.enter_context(nc.Block())

        def rows_by_tile(w):
            return w[0].rearrange("(k p) n -> p k n", p=P)

        def columns(w, k0, nk, start, n):
            return rows_by_tile(w)[:, k0:k0 + nk, bass.ds(start, n)]

        def contraction_tile(stage, b, n):
            first = stage == "out" and isinstance(b, int) and b == 0
            return (n + MLA_HEADS) % KT if first else n

        ukv = io["mla_w_ukv"][0].rearrange("(k p) (h c) -> p k h c", p=P, c=NOPE + MLA_V)
        uq = io["mla_w_uq"][0].rearrange("(k p) (h c) -> p k h c", p=P, c=QK_DIM)

        def expand_chunk(j):
            if j == 0:
                return [(uq[:, k, :, NOPE:QK_DIM], k) for k in range(RT)]
            w, c0 = [(uq, 0), (ukv, 0), (ukv, NOPE)][(j - 1) // 2]
            h0 = 4 * ((j - 1) % 2)
            return [(w[:, k, h0:h0 + 4, c0:c0 + P], k) for k in range(RT)]

        def load(sp, name, i, j):
            free = stream.owner(stream.raw_owner, name, i, j)
            if free is not None:
                sp.wait_ge(pieces_split, free)
            slot, full = w_raw[:, stream.raw_slot(name, j), :], raw_filled[stream.raw_slot(name, j)]
            if name in ("up1", "up2"):
                w = io[f"ffn{name[2]}_w_{('gate', 'up')[j // 2]}"]
                src = columns(w, 8 * (j % 2), 8, i * 256, 256)
                sp.dma_start(slot.rearrange("p (k n) -> p k n", k=8), src).then_inc(full, 16)
            elif name in ("down1", "down2"):
                src = columns(io[f"ffn{name[4]}_w_down"], 4 * j, 4, i * NB, NB)
                sp.dma_start(slot.rearrange("p (k n) -> p k n", k=4), src).then_inc(full, 16)
            elif name == "diff_in":
                src = columns(io["w_in"], 4 * (j % 4), 4, i * 2 * NB + (LATENT_W + NB * (j // 4)), NB)
                sp.dma_start(slot.rearrange("p (k n) -> p k n", k=4), src).then_inc(full, 16)
            elif name == "latent_in":
                start, n = LATENT_BLOCKS[j // 4]
                src = columns(io["w_in"], 4 * (j % 4), 4, start, n)
                sp.dma_start(slot[:, 0:4 * n].rearrange("p (k n) -> p k n", k=4), src).then_inc(full, 16)
            elif name == "expand":
                for src, k in expand_chunk(j):
                    dst = slot[:, k * NB:(k + 1) * NB].rearrange("p (h c) -> p h c", h=src.shape[1])
                    sp.dma_start(dst, src).then_inc(full, 16)
            else:
                src = columns(io["w_out"], contraction_tile(name, i, 4 * j), 4, i * NB, NB)
                sp.dma_start(slot.rearrange("p (k n) -> p k n", k=4), src).then_inc(full, 16)

        def load_x(sp, c):
            cols = slice(c * NB, (c + 1) * NB)
            sp.dma_start(x[:, :, cols], io["x"][0].rearrange("(t p) n -> p t n", p=P)[:, :, cols])\
                .then_inc(x_loaded[c], 16)

        def round_piece(act, name, i, q):
            s = stream.stages[name]
            j, half = q // s.ppc, q % s.ppc
            slot = stream.raw_slot(name, j)
            act.wait_ge(raw_filled[slot], stream.filled(name, i, j))
            free = stream.owner(stream.split_owner, name, i, q)
            if free is not None:
                act.wait_ge(pieces_multiplied, free)
            n = 2 * stream.columns(name, q)
            nc.scalar.activation(w_hi[:, stream.split_slot(name, q), 0:n],
                                 w_raw[:, slot, half * n:(half + 1) * n], ACT.Copy).then_inc(pieces_rounded, 1)

        def split_piece(dve, name, i, q):
            s = stream.stages[name]
            j, half = q // s.ppc, q % s.ppc
            dve.wait_ge(pieces_rounded, stream.pieces(name, i, q))
            slot = stream.split_slot(name, q)
            n = 2 * stream.columns(name, q)
            nc.vector.tensor_tensor(w_lo[:, slot, 0:n],
                                    w_raw[:, stream.raw_slot(name, j), half * n:(half + 1) * n],
                                    w_hi[:, slot, 0:n].bitcast(F32), ALU.subtract)\
                .then_inc(pieces_split, 1)

        def norm_bank(name, k):
            first, ring = {"cq": (4, 2), "ckv": (4, 2), "mix_pre": (2, 4)}.get(name, (0, 4))
            return ps[:, first + (k // 2) % ring, (k % 2) * SEQ:(k % 2 + 1) * SEQ]

        def turn_bank(name, g):
            return 6 + g % 2 if name == "dqk" else 7

        def nope_bank(n):
            return (0, 2, 6, 4)[n % 4]

        LATENT_BANK = (0, 2, 0)
        Q_PE_BANK = 2
        V_BANK = (7, 6)

        def block_bank(stage, b):
            if stage == "out":
                return 6 if isinstance(b, int) and b == 0 else 2 * b - 2
            return 2 * b

        nope_part_buf = (part[:, :, :], up[:, :, :])

        def bank(b):
            return ps[:, bass.ds(b, 1), :].rearrange("p a n -> p (a n)")

        def proj_rows(i, blk, tt):
            return proj[:, bass.ds(i, 1), tt, blk * NB:(blk + 1) * NB].rearrange("p a n -> p (a n)")

        def heads_of(name, g):
            for tt in range(TT):
                if name == "k_pe":
                    yield 0, tt, latent[:, tt, 2 * RANK:LATENT_W]
                for h in range(2):
                    if name == "dqk":
                        yield h, tt, proj[:, g // 4, tt, (2 * (g % 4) + h) * P:(2 * (g % 4) + h + 1) * P]
                    if name == "q_pe":
                        yield h, tt, q_pe[:, tt, (2 * g + h) * ROPE:(2 * g + h + 1) * ROPE]

        def turned(name, g):
            if name == "k_pe":
                return k_pe_t[:, :].rearrange("p (h s) -> p h s", h=1), ROPE
            if name == "q_pe":
                return q_pe_t[:, 2 * g:2 * g + 2, :], ROPE
            return dqk_t[:, g // 4, 2 * (g % 4):2 * (g % 4) + 2, :], P

        def unit_of(s):
            if s < 0 or s >= MAPS:
                return None
            if s < 2 * DIFF_HEADS:
                return s // 2 if s % 2 else None
            return s - DIFF_HEADS

        def first_map(u):
            return 2 * u if u < DIFF_HEADS else u + DIFF_HEADS

        @block.sync
        def _(sp):
            for name, s in stream.stages.items():
                for j in range(s.chunks):
                    if name == "up1" and j < 2:
                        load_x(sp, 2 * j)
                    load(sp, name, 0, j)
                    if name == "up1" and j < 2:
                        load_x(sp, 2 * j + 1)
                if name == "up1":
                    row = 0
                    for norm in LATER_GAINS:
                        g = io[norm][0].rearrange("(k p) -> k p", p=P)
                        sp.dma_start(up[row:row + g.shape[0], 1, 0:P], g).then_inc(gains_loaded, 16)
                        row += g.shape[0]
                if s.iters > 1:
                    with sp.Fori(1, s.iters) as i:
                        for j in range(s.chunks):
                            load(sp, name, i, j)
            x_out = out[0].rearrange("(t p) n -> p t n", p=P)
            for c in range(COLUMN_BLOCKS):
                sp.wait_ge(x_updated, RESIDUAL.after("ffn2_post", TT * (c + 1)))
                cols = slice(c * NB, (c + 1) * NB)
                sp.dma_start(x_out[:, :, cols], x[:, :, cols]).then_inc(stored, 16)
            sp.wait_ge(stored, 16 * COLUMN_BLOCKS)

        @block.gpsimd
        def _(pool):
            nc.gpsimd.memset(ident[:, :], 0.0).then_inc(ident_ready, 1)
            nc.gpsimd.memset(minus_half[:, :], -0.5).then_inc(consts_ready, 1)
            pool.wait_ge(ident_ready, 1)
            nc.gpsimd.affine_select(out=ident[:, :], in_=ident[:, :], compare_op=ALU.not_equal, fill=1.0,
                                    base=0, pattern=[[-1, P]], channel_multiplier=1).then_inc(ident_ready, 1)
            pool.wait_ge(consts_ready, 1)
            for n in range(N_RSQRT):
                if n == RSQRT.after("mix_pre"):
                    pool.wait_ge(x_updated, RESIDUAL.after("ffn1_post", 4 * TT))
                    nc.gpsimd.memset(mask[:, :], 0.0).then_inc(mask_ready, 1)
                    pool.wait_ge(mask_ready, 1)
                    for _, end in Q_COLS:
                        nc.gpsimd.memset(mask[0:CHUNK_FRAMES, end - CHUNK_FRAMES:end], MASKED)\
                            .then_inc(mask_ready, 1)
                pool.wait_ge(mean_squares, n + 1)
                nc.gpsimd.tensor_tensor(inv_rms[:, n, :], mean_square[:, n, :], minus_half[:, :], ALU.pow)\
                    .then_inc(rms_inverted, 1)

        @block.scalar
        def _(act):
            act.dma_start(up[0:KT, 0, 0:P], io["ffn1_pre_g"][0].rearrange("(k p) -> k p", p=P))\
                .then_inc(gain_loaded, 16)
            def load_post_gain(name):
                act.dma_start(post_gain[:, :], io[name][0].partition_broadcast(P)).then_inc(post_gain_loaded, 16)

            dump = [t[:, :, :].rearrange("p a b -> p (a b)") for t in (gate, up)]

            def dump_free(name, n):
                act.wait_ge(squares_summed, SQUARES.at[name] - 1 + n)

            def square_rows(name, rows):
                for tt in range(TT):
                    dump_free(name, tt)
                    nc.scalar.activation(dump[tt], rows[tt], ACT.Square,
                                         accum_out=square_sum[:, RSQRT.at[name], tt:tt + 1])\
                        .then_inc(squares_summed, 1)

            def square_x(name):
                for c in range(COLUMN_BLOCKS):
                    if X_FROM[name] is None:
                        act.wait_ge(x_loaded[c], 16)
                if X_FROM[name] is not None:
                    act.wait_ge(x_updated, RESIDUAL.after(X_FROM[name], 4 * TT))
                for tt in range(TT):
                    nc.scalar.activation(x_squares[:, tt, :], x[:, tt, :], ACT.Square,
                                         accum_out=square_sum[:, RSQRT.at[name], tt:tt + 1])\
                        .then_inc(squares_summed, 1)

            def round_norm(name, dst, tiles):
                for k in tiles:
                    act.wait_ge(norm_turned, NORM_GROUPS.after(name, k // 2 + 1))
                    g = GAIN_COLS[name] + k
                    nc.scalar.activation(dst[:, k, 0, :], norm_bank(name, k), ACT.Copy, scale=gains[:, g:g + 1])\
                        .then_inc(norm_rounded, 1)

            def start_stage(stage):
                name = PRE_NORM[stage]
                for c, pieces in enumerate(PIECES_WITH_TILES[stage]):
                    if X_FROM[name] is not None and c == COLUMN_BLOCKS // 2:
                        act.wait_ge(x_updated, RESIDUAL.after(X_FROM[name], 4 * TT))
                    round_norm(name, xn, range(c * TILES, (c + 1) * TILES))
                    for q in pieces:
                        round_piece(act, stage, 0, q)
                for q in range(pieces[-1] + 1, LEAD + COLUMN_BLOCKS):
                    round_piece(act, stage, 0, q)
                square_x(name)

            def gate_part(L, i):
                act.wait_ge(pieces_multiplied, stream.pieces(f"up{L}", i, 3))
                nc.scalar.activation(part[:, :, :], ps[:, 4:6, SEQ:2 * SEQ], ACT.Copy).then_inc(part_copied, 1)

            def gate_silu(L, i):
                act.wait_ge(gate_scaled, (L - 1) * (FT // 2) + i + 1)
                nc.scalar.activation(gate[:, :, :], gate[:, :, :], ACT.Silu).then_inc(silu_done, 1)

            def up_part(L, i):
                act.wait_ge(pieces_multiplied, stream.pieces(f"up{L}", i, 7))
                nc.scalar.activation(part[:, :, :], ps[:, 6:8, SEQ:2 * SEQ], ACT.Copy).then_inc(part_copied, 1)

            def round_hidden(L, i):
                act.wait_ge(hidden_full, (L - 1) * (FT // 2) + i + 1)
                nc.scalar.activation(hidden[:, bass.ds(2 * i, 2), 0, :], up[:, :, :], ACT.Copy)\
                    .then_inc(hidden_rounded, 1)

            def square_block(name, stage, b):
                act.wait_ge(pieces_multiplied, stream.pieces(stage, b, stream.stages[stage].pieces - 1))
                for tt in range(TT):
                    dump_free(name, b * TT + tt)
                    if tt == 1 and not (isinstance(b, int) and b == 3):
                        act.wait_ge(branch_done, b * TT + BRANCH.after(name))
                    nc.scalar.activation(dump[tt], bank(block_bank(stage, b) + tt), ACT.Square,
                                         accum_out=block_squares[:, tt, bass.ds(b, 1)]).then_inc(squares_summed, 1)

            def up_stage(L):
                start_stage(f"up{L}")
                gate_part(L, 0)
                round_piece(act, f"up{L}", 0, 7)
                act.wait_ge(row_summed, L)
                nc.scalar.activation(rms_row, ps[:, 0, 0:SEQ], ACT.Copy).then_inc(row_copied, 1)
                if L == 1:
                    act.wait_ge(gains_turned, 2)
                    nc.scalar.activation(gains[:, KT:], ps[:, 1, 0:GAIN_ROWS - KT], ACT.Copy)\
                        .then_inc(gains_ready, 1)
                gate_silu(L, 0)
                with act.Fori(1, FT // 2) as i:
                    for q in range(8):
                        round_piece(act, f"up{L}", i, q)
                        if q == 2:
                            up_part(L, i - 1)
                        if q == 3:
                            round_hidden(L, i - 1)
                        if q == 6:
                            gate_part(L, i)
                        if q == 7:
                            gate_silu(L, i)

            def down_stage(L):
                stage = f"down{L}"

                def body(b, lead):
                    for q in range(stream.stages[stage].pieces):
                        round_piece(act, stage, b, q)
                        if not lead and q == 2:
                            up_part(L, FT // 2 - 1)
                        if not lead and q == 3:
                            round_hidden(L, FT // 2 - 1)
                            load_post_gain(f"ffn{L}_post_g")
                        if lead and q == 3:
                            square_block(f"ffn{L}_post", stage, b - 1)
                body(0, False)
                with act.Fori(1, 4) as b:
                    body(b, True)
                if L == 1:
                    for q in range(LEAD):
                        round_piece(act, "diff_in", 0, q)
                square_block(f"ffn{L}_post", stage, 3)

            act.wait_ge(gains_turned, 1)
            nc.scalar.activation(gains[:, 0:KT], ps[:, 4, 0:KT], ACT.Copy).then_inc(gains_ready, 1)
            act.wait_ge(gains_ready, 1)
            up_stage(1)
            down_stage(1)
            act.wait_ge(gains_ready, 2)
            start_stage("diff_in")
            load_post_gain("mix_post_g")
            act.dma_start(rope[:, :, :], io["rope_table"].rearrange("(t p) c -> p t c", p=P))\
                .then_inc(tables_loaded, 16)
            act.dma_start(sub_gain[:, :], io["diff_subln_g"][0].partition_broadcast(P)).then_inc(tables_loaded, 16)
            for n, name in enumerate(("diff_lambda_q1", "diff_lambda_k1", "diff_lambda_q2", "diff_lambda_k2")):
                act.dma_start(lam_vec[:, n, :], io[name][0].partition_broadcast(P)).then_inc(tables_loaded, 16)
            mix_rms = inv_rms[:, RSQRT.at["mix_pre"], :]

            def copy_rows0(stage, i, q, b, dst, scale=1.0):
                act.wait_ge(pieces_multiplied, stream.pieces(stage, i, q))
                nc.scalar.activation(dst, ps[:, b, 0:stream.columns(stage, q)], ACT.Copy, scale=scale)\
                    .then_inc(rows0_copied, 1)

            def copy_turned(name, g):
                act.wait_ge(qk_turned, QK_TURNS.after(name, g + 1))
                dst, rows = turned(name, g)
                nc.scalar.activation(dst, ps[0:rows, turn_bank(name, g), 0:dst.shape[1] * SEQ]
                                     .rearrange("p (h s) -> p h s", s=SEQ), ACT.Copy).then_inc(qk_copied, 1)

            def diff_in(i, lead):
                for q in range(0 if lead else LEAD + COLUMN_BLOCKS, 16):
                    round_piece(act, "diff_in", i, q)
                    if lead and q == 2:
                        copy_rows0("diff_in", i - 1, 15, 2, proj_rows(i - 1, 1, 0), mix_rms[:, 0:1])
                    if q == 10:
                        if not lead:
                            act.wait_ge(rms_inverted, RSQRT.after("mix_pre"))
                        copy_rows0("diff_in", i, 7, 0, proj_rows(i, 0, 0), mix_rms[:, 0:1])
            diff_in(0, False)
            with act.Fori(1, 3) as i:
                diff_in(i, True)
            def copy_latent0(blk):
                start, n = LATENT_BLOCKS[blk]
                copy_rows0("latent_in", 0, 8 * blk + 7, LATENT_BANK[blk], latent[:, 0, start:start + n],
                           mix_rms[:, 0:1])

            for q in range(24):
                round_piece(act, "latent_in", 0, q)
                if q == 2:
                    copy_rows0("diff_in", 2, 15, 2, proj_rows(2, 1, 0), mix_rms[:, 0:1])
                if q in (10, 18):
                    copy_latent0(q // 8 - 1)
                if q == 18:
                    act.wait_ge(rows1_copied, LATENT_FULL["cq"])
                    act.wait_ge(rows0_copied, LATENT_FULL["cq"])
                    square_rows("cq", [latent[:, tt, 0:RANK] for tt in range(TT)])
                if q - 3 in DQK_TURN_PIECES:
                    g = 2 * DQK_TURN_PIECES.index(q - 3)
                    for g in (g, g + 1):
                        copy_turned("dqk", g)
            round_norm("cq", cn[:, 0], range(RT))
            for q in range(LEAD):
                round_piece(act, "expand", 0, q)
            copy_latent0(2)
            act.wait_ge(rows1_copied, LATENT_FULL["ckv"])
            act.wait_ge(rows0_copied, LATENT_FULL["ckv"])
            square_rows("ckv", [latent[:, tt, RANK:2 * RANK] for tt in range(TT)])
            round_piece(act, "expand", 0, LEAD)
            copy_rows0("expand", 0, 1, Q_PE_BANK, q_pe[:, 0, :])
            round_norm("ckv", cn[:, 1], range(RT))
            act.wait_ge(lam_dots, 2)
            nc.scalar.activation(lam[:, 2:4], lam[:, 0:2], ACT.Exp).then_inc(lam_exps, 1)
            for j in range(1, 5):
                for q in (2 * j + 2, 2 * j + 3):
                    round_piece(act, "expand", 0, q)
                for n in (2 * j - 2, 2 * j - 1):
                    act.wait_ge(pieces_multiplied, stream.pieces("expand", 0, 2 * j + 1))
                    if n >= 2:
                        act.wait_ge(nope_done, n - 1)
                    nc.scalar.activation(nope_part_buf[n % 2], ps[:, nope_bank(n):nope_bank(n) + 2, SEQ:2 * SEQ],
                                         ACT.Copy).then_inc(nope_part, 1)

            def copy_v0(blk):
                act.wait_ge(v_summed, blk + 1)
                nc.scalar.activation(v_tok[:, 0, blk * NB:(blk + 1) * NB], ps[:, V_BANK[0], :], ACT.Copy)\
                    .then_inc(rows0_copied, 1)

            def exps(s):
                for tt, (a, b) in enumerate(Q_COLS):
                    act.wait_ge(scores_masked, 2 * s + tt + 1)
                    nc.scalar.activation(probs[:, s % 4, a:b], probs[:, s % 4, a:b], ACT.Exp, scale=-1.0,
                                         bias=row_min[:, s, tt:tt + 1], accum_out=row_sum[:, s, tt:tt + 1])\
                        .then_inc(exps_done, 1)

            def copy_probs(u):
                act.wait_ge(probs_turned, u + 1)
                if u >= 2:
                    act.wait_ge(values_summed, u - 1)
                nc.scalar.activation(probs_t[:, u % 2, :], ps[:, 2 + u % 2, 0:MAP_W], ACT.Copy)\
                    .then_inc(probs_copied, 1)

            def round_mla(u):
                act.wait_ge(values_summed, u + 1)
                nc.scalar.activation(mixed[:, u - DIFF_HEADS, 0, :], ps[:, 4 + u % 2, 0:SEQ], ACT.Copy)\
                    .then_inc(mla_rounded, 1)

            def square_diff(d):
                act.wait_ge(values_summed, d + 1)
                for tt in range(TT):
                    dump_free("diff", TT * d + tt)
                    nc.scalar.activation(dump[tt][:, 0:DIFF_V], ps[:, 4 + d % 2, tt * DIFF_V:(tt + 1) * DIFF_V],
                                         ACT.Square, accum_out=square_sum[:, RSQRT.at["diff"] + d, tt:tt + 1])\
                        .then_inc(squares_summed, 1)

            def round_diff(d):
                act.wait_ge(diff_turned, d + 1)
                k = MLA_HEADS + 2 * d
                nc.scalar.activation(mixed[:, k:k + 2, 0, :], ps[:, 6, :].rearrange("p (k s) -> p k s", k=2), ACT.Copy)\
                    .then_inc(diff_rounded, 1)

            for t in range(MAPS + 3):
                blk, tt = V_STEPS.get(t - 1, (0, 1))
                if tt == 0:
                    copy_v0(blk)
                if t - 1 in PE_TURN_STEPS:
                    copy_turned(*PE_TURN_STEPS[t - 1])
                if t < MAPS:
                    exps(t)
                if unit_of(t - 2) is not None:
                    copy_probs(unit_of(t - 2))
                u = unit_of(t - 3)
                if u is not None:
                    if u < DIFF_HEADS:
                        square_diff(u)
                    else:
                        round_mla(u)
                u = unit_of(t - 5)
                if u is not None and u < DIFF_HEADS:
                    round_diff(u)
                if t in V_PIECES:
                    round_piece(act, "expand", 0, V_PIECES[t])
                if t in OUT_SPLIT_STEPS:
                    round_piece(act, "out", 0, OUT_SPLIT_STEPS[t])

            def out_body(b):
                for q in range(8):
                    round_piece(act, "out", b, q)
                    if q == 3:
                        square_block("mix_post", "out", b - 1)
            out_body(1)
            with act.Fori(2, 4) as b:
                out_body(b)
            for q in range(LEAD):
                round_piece(act, "up2", 0, q)
            square_block("mix_post", "out", 3)
            up_stage(2)
            down_stage(2)

        @block.vector
        def _(dve):
            steps = [0]

            def then(instruction):
                steps[0] += 1
                instruction.then_inc(vector_step, 1)
                dve.wait_ge(vector_step, steps[0])

            nc.vector.memset(mean_square[:, :, 0:1], 1.0).then_inc(gate_banks_free, 1)
            nc.vector.memset(mean_square[:, :, 1:2], 1.0).then_inc(up_banks_free, 1)
            dve.wait_ge(gate_banks_free, 1)
            dve.wait_ge(up_banks_free, 1)

            def mean_square_of(name, n, width, factor=1.0, head=0):
                dve.wait_ge(squares_summed, n)
                k = RSQRT.at[name] + head
                nc.vector.tensor_scalar(mean_square[:, k, :], square_sum[:, k, :], factor / width, factor * EPS,
                                        ALU.mult, ALU.add).then_inc(mean_squares, 1)

            def scale_rows(name, dst, src):
                k = RSQRT.at[name]
                dve.wait_ge(rms_inverted, k + 1)
                for tt in range(TT):
                    nc.vector.tensor_scalar(dst[tt], src[tt], inv_rms[:, k, tt:tt + 1], None, ALU.mult)\
                        .then_inc(scaled, 1)

            def split_norm(name, dst, tiles):
                for k in tiles:
                    if k % 2 == 0:
                        dve.wait_ge(norm_rounded, NORM_TILES.after(name, k + 2))
                    g = GAIN_COLS[name] + k
                    nc.vector.scalar_tensor_tensor(out=dst[:, k, 1, :], in0=norm_bank(name, k), scalar=gains[:, g:g + 1],
                                                   in1=dst[:, k, 0, :].bitcast(F32), op0=ALU.mult, op1=ALU.subtract)\
                        .then_inc(norm_split, 1)

            rms_of_token = rms_row.unsqueeze(1).broadcast_to([P, 2, SEQ])

            def gate_sum(L, i):
                dve.wait_ge(part_copied, (L - 1) * FT + 2 * i + 1)
                nc.vector.tensor_tensor(gate[:, :, :], ps[:, 4:6, 0:SEQ], part[:, :, :], ALU.add)\
                    .then_inc(gate_banks_free, 1)
                if isinstance(i, int):
                    dve.wait_ge(row_copied, L)
                dve.wait_ge(gate_banks_free, (L - 1) * (FT // 2) + i + 2)
                nc.vector.tensor_tensor(gate[:, :, :], gate[:, :, :], rms_of_token, ALU.mult).then_inc(gate_scaled, 1)

            def up_sum(L, i):
                dve.wait_ge(part_copied, (L - 1) * FT + 2 * i + 2)
                nc.vector.tensor_tensor(up[:, :, :], ps[:, 6:8, 0:SEQ], part[:, :, :], ALU.add)\
                    .then_inc(up_banks_free, 1)
                dve.wait_ge(up_banks_free, (L - 1) * (FT // 2) + i + 2)
                nc.vector.tensor_tensor(up[:, :, :], up[:, :, :], rms_of_token, ALU.mult).then_inc(up_scaled, 1)
                dve.wait_ge(up_scaled, (L - 1) * (FT // 2) + i + 1)
                dve.wait_ge(silu_done, (L - 1) * (FT // 2) + i + 1)
                nc.vector.tensor_tensor(up[:, :, :], up[:, :, :], gate[:, :, :], ALU.mult).then_inc(hidden_full, 1)

            def split_hidden(L, i):
                dve.wait_ge(hidden_rounded, (L - 1) * (FT // 2) + i + 1)
                nc.vector.tensor_tensor(hidden[:, bass.ds(2 * i, 2), 1, :], up[:, :, :],
                                        hidden[:, bass.ds(2 * i, 2), 0, :].bitcast(F32), ALU.subtract)\
                    .then_inc(hidden_split, 1)

            def up_stage(L, branch=None):
                start_stage(f"up{L}", branch)
                k = RSQRT.at[f"ffn{L}_pre"]
                nc.vector.memset(ones, 1.0).then_inc(diag_ready, 1)
                dve.wait_ge(rms_inverted, k + 1)
                for tt in range(TT):
                    nc.vector.tensor_scalar(rms_diag[:, tt * P:(tt + 1) * P], ident[:, :], inv_rms[:, k, tt:tt + 1],
                                            None, ALU.mult).then_inc(diag_ready, 1)
                split_piece(dve, f"up{L}", 0, 7)
                gate_sum(L, 0)
                with dve.Fori(1, FT // 2) as i:
                    for q in range(8):
                        split_piece(dve, f"up{L}", i, q)
                        if q == 2:
                            up_sum(L, i - 1)
                        if q == 3:
                            split_hidden(L, i - 1)
                        if q == 6:
                            gate_sum(L, i)

            def times_gain(branch, stage, b, tt):
                nc.vector.tensor_tensor(branch[:, bass.ds(b, 1), tt, :].rearrange("p a n -> p (a n)"),
                                        bank(block_bank(stage, b) + tt), post_gain[:, bass.ds(b * NB, NB)], ALU.mult)\
                    .then_inc(branch_done, 1)

            def branch_block(name, stage, branch, b):
                dve.wait_ge(pieces_multiplied, stream.pieces(stage, b, stream.stages[stage].pieces - 1))
                times_gain(branch, stage, b, 1)
                dve.wait_ge(squares_summed, b * TT + SQUARES.after(name))
                times_gain(branch, stage, b, 0)

            def last_branch_block(name, stage, branch):
                k = RSQRT.at[name]
                dve.wait_ge(squares_summed, SQUARES.after(name, 4 * TT - 1))
                times_gain(branch, stage, 3, 0)
                dve.wait_ge(squares_summed, SQUARES.after(name, 4 * TT))
                then(nc.vector.tensor_reduce(square_sum[:, k, :], block_squares[:, :, :], AX_X, ALU.add))
                mean_square_of(name, SQUARES.after(name, 4 * TT), D_MODEL, 1.0 if name == "mix_post" else 4.0)
                times_gain(branch, stage, 3, 1)
                dve.wait_ge(branch_done, BRANCH.after(name, 4 * TT))
                dve.wait_ge(rms_inverted, k + 1)

            def down_stage(L, branch):
                stage, name = f"down{L}", f"ffn{L}_post"

                def body(b, lead):
                    for q in range(stream.stages[stage].pieces):
                        split_piece(dve, stage, b, q)
                        if not lead and q == 2:
                            up_sum(L, FT // 2 - 1)
                        if not lead and q == 3:
                            split_hidden(L, FT // 2 - 1)
                        if lead and q == 3:
                            branch_block(name, stage, branch, b - 1)
                body(0, False)
                dve.wait_ge(post_gain_loaded, 16 * (2 * L - 1))
                with dve.Fori(1, 4) as b:
                    body(b, True)
                if L == 1:
                    for q in range(LEAD):
                        split_piece(dve, "diff_in", 0, q)
                last_branch_block(name, stage, branch)

            def update_x(name, branch, c):
                cols = slice(c * NB, (c + 1) * NB)
                for tt in range(TT):
                    nc.vector.scalar_tensor_tensor(out=x[:, tt, cols], in0=branch[:, c, tt, :],
                                                   scalar=inv_rms[:, RSQRT.at[name], tt:tt + 1],
                                                   in1=x[:, tt, cols], op0=ALU.mult, op1=ALU.add).then_inc(x_updated, 1)

            def start_stage(stage, branch=None):
                name = PRE_NORM[stage]
                if branch is not None:
                    for c in (0, 1):
                        update_x(X_FROM[name], branch, c)
                for c, pieces in enumerate(PIECES_WITH_TILES[stage]):
                    split_norm(name, xn, range(c * TILES, (c + 1) * TILES))
                    if branch is not None and c < 2:
                        update_x(X_FROM[name], branch, c + 2)
                    for q in pieces:
                        split_piece(dve, stage, 0, q)
                for q in range(pieces[-1] + 1, LEAD + COLUMN_BLOCKS):
                    split_piece(dve, stage, 0, q)
                mean_square_of(name, SQUARES.after(name, TT), D_MODEL)

            up_stage(1)
            down_stage(1, branch_b)
            start_stage("diff_in", branch_b)
            mix_rms = inv_rms[:, RSQRT.at["mix_pre"], :]

            def copy_rows1(stage, i, q, b, dst, scale=None):
                dve.wait_ge(pieces_multiplied, stream.pieces(stage, i, q))
                if scale is None:
                    nc.vector.tensor_copy(dst, ps[:, b, :]).then_inc(rows1_copied, 1)
                else:
                    nc.vector.tensor_scalar(dst, ps[:, b, 0:stream.columns(stage, q)], scale, None, ALU.mult)\
                        .then_inc(rows1_copied, 1)

            def rotary_step(n, x_pairs, cos, sin, t1, t2, done):
                x1, x2 = x_pairs
                if n == 0:
                    then(nc.vector.tensor_tensor(t1, x2, sin, ALU.mult))
                elif n == 1:
                    then(nc.vector.tensor_tensor(t2, x1, sin, ALU.mult))
                elif n == 2:
                    then(nc.vector.tensor_tensor(x1, x1, cos, ALU.mult))
                elif n == 3:
                    nc.vector.tensor_tensor(x1, x1, t1, ALU.subtract).then_inc(done, 1)
                elif n == 4:
                    then(nc.vector.tensor_tensor(x2, x2, cos, ALU.mult))
                else:
                    nc.vector.tensor_tensor(x2, x2, t2, ALU.add).then_inc(done, 1)

            def rotate_dqk(step):
                n, tt = step // 12, step // 6 % 2
                h = proj[:, n, tt, :].rearrange("p (h two d) -> p h two d", two=2, d=64)
                wide = [P, 2 * DIFF_HEADS, 64]
                rotary_step(step % 6, (h[:, :, 0, :], h[:, :, 1, :]),
                            rope[:, tt, 0:64].unsqueeze(1).broadcast_to(wide),
                            rope[:, tt, 64:128].unsqueeze(1).broadcast_to(wide),
                            turn_a[:, :].rearrange("p (h d) -> p h d", d=64),
                            turn_b[:, :].rearrange("p (h d) -> p h d", d=64), roped_dqk)

            def rotate_pe(step):
                if step < 6:
                    kr = latent[:, :, 2 * RANK:LATENT_W].rearrange("p t (two d) -> p t two d", two=2)
                    rotary_step(step, (kr[:, :, 0, :], kr[:, :, 1, :]), rope[:, :, 128:160], rope[:, :, 160:192],
                                turn_a[:, 0:64].rearrange("p (t d) -> p t d", t=TT),
                                turn_b[:, 0:64].rearrange("p (t d) -> p t d", t=TT), roped_k_pe)
                else:
                    tt = step // 6 - 1
                    qh = q_pe[:, tt, :].rearrange("p (h two d) -> p h two d", two=2, d=32)
                    wide = [P, MLA_HEADS, 32]
                    rotary_step(step % 6, (qh[:, :, 0, :], qh[:, :, 1, :]),
                                rope[:, tt, 128:160].unsqueeze(1).broadcast_to(wide),
                                rope[:, tt, 160:192].unsqueeze(1).broadcast_to(wide),
                                turn_a[:, 0:256].rearrange("p (h d) -> p h d", d=32),
                                turn_b[:, 0:256].rearrange("p (h d) -> p h d", d=32), roped_q_pe)

            def diff_in(i, lead):
                for q in range(0 if lead else LEAD + COLUMN_BLOCKS, 16):
                    split_piece(dve, "diff_in", i, q)
                    if lead and q == 2:
                        copy_rows1("diff_in", i - 1, 15, 3, proj_rows(i - 1, 1, 1), mix_rms[:, 1:2])
                    if q == 10:
                        if not lead:
                            dve.wait_ge(rms_inverted, RSQRT.after("mix_pre"))
                        copy_rows1("diff_in", i, 7, 1, proj_rows(i, 0, 1), mix_rms[:, 1:2])
            diff_in(0, False)
            with dve.Fori(1, 3) as i:
                diff_in(i, True)

            dve.wait_ge(tables_loaded, 16 * 6)

            def copy_latent1(blk):
                start, n = LATENT_BLOCKS[blk]
                copy_rows1("latent_in", 0, 8 * blk + 7, LATENT_BANK[blk] + 1, latent[:, 1, start:start + n],
                           mix_rms[:, 1:2])

            for q in range(24):
                split_piece(dve, "latent_in", 0, q)
                if q == 2:
                    copy_rows1("diff_in", 2, 15, 3, proj_rows(2, 1, 1), mix_rms[:, 1:2])
                    dve.wait_ge(rows0_copied, TOKEN_MAJOR.after("diff_in", 4))
                    dve.wait_ge(rows1_copied, TOKEN_MAJOR.after("diff_in", 4))
                if q in (10, 18):
                    copy_latent1(q // 8 - 1)
                if q == 18:
                    mean_square_of("cq", SQUARES.after("cq", TT), RANK)
                if q == 19:
                    rows = [latent[:, tt, 0:RANK] for tt in range(TT)]
                    dve.wait_ge(rows1_copied, LATENT_FULL["cq"])
                    scale_rows("cq", rows, rows)
                if 3 <= q < 19:
                    for step in range(3 * (q - 3) // 2, 3 * (q - 2) // 2):
                        rotate_dqk(step)
            split_norm("cq", cn[:, 0], range(RT))
            for q in range(LEAD):
                split_piece(dve, "expand", 0, q)
            copy_latent1(2)
            mean_square_of("ckv", SQUARES.after("ckv", TT), RANK)
            rows = [latent[:, tt, RANK:2 * RANK] for tt in range(TT)]
            dve.wait_ge(rows1_copied, LATENT_FULL["ckv"])
            scale_rows("ckv", rows, rows)
            split_piece(dve, "expand", 0, LEAD)
            copy_rows1("expand", 0, 1, Q_PE_BANK + 1, q_pe[:, 1, :])
            dve.wait_ge(roped_dqk, 8)
            for n in range(2):
                nc.vector.tensor_tensor_reduce(turn_a[:, n * DIFF_D:(n + 1) * DIFF_D], lam_vec[:, 2 * n, :],
                                               lam_vec[:, 2 * n + 1, :],
                                               1.0, 0.0, ALU.mult, ALU.add, lam[:, n:n + 1]).then_inc(lam_dots, 1)
            split_norm("ckv", cn[:, 1], range(RT))
            dve.wait_ge(lam_exps, 1)
            then(nc.vector.tensor_tensor(lam[:, 4:5], lam[:, 3:4], lam[:, 2:3], ALU.subtract))
            then(nc.vector.tensor_scalar(lam[:, 4:5], lam[:, 4:5], -LAMBDA_INIT, None, ALU.add))
            then(nc.vector.tensor_scalar(sub_gain[:, :], sub_gain[:, :], 1.0 - LAMBDA_INIT, None, ALU.mult))

            for j in range(1, 5):
                for q in (2 * j + 2, 2 * j + 3):
                    split_piece(dve, "expand", 0, q)
                for n in (2 * j - 2, 2 * j - 1):
                    dve.wait_ge(nope_part, n + 1)
                    nc.vector.tensor_tensor(nope_t[:, n // 4, 2 * (n % 4):2 * (n % 4) + 2, :],
                                            ps[:, nope_bank(n):nope_bank(n) + 2, 0:SEQ], nope_part_buf[n % 2],
                                            ALU.add).then_inc(nope_done, 1)
                if j == 1:
                    dve.wait_ge(rows0_copied, TOKEN_MAJOR.after("q_pe"))
                    dve.wait_ge(rows1_copied, TOKEN_MAJOR.after("q_pe"))
                for step in range(5 * (j - 1), min(5 * j, 18)):
                    rotate_pe(step)

            dve.wait_ge(mask_ready, 3)

            def copy_v1(blk):
                dve.wait_ge(pieces_multiplied, stream.pieces("expand", 0, 11 + 2 * blk))
                nc.vector.tensor_copy(v_tok[:, 1, blk * NB:(blk + 1) * NB], ps[:, V_BANK[1], :])\
                    .then_inc(rows1_copied, 1)

            def mask_scores(s):
                if s >= 4:
                    dve.wait_ge(probs_turned, ((s - 4) // 2 if s - 4 < 2 * DIFF_HEADS else s - 4 - DIFF_HEADS) + 1)
                dve.wait_ge(scores_ready, s + 1)
                scale = DIFF_D ** -0.5 if s < 2 * DIFF_HEADS else QK_DIM ** -0.5
                for tt, (a, b) in enumerate(Q_COLS):
                    nc.vector.tensor_tensor_reduce(probs[:, s % 4, a:b], ps[:, s % 2, a:b], mask[:, a:b], -scale, 3.0e38,
                                                   ALU.add, ALU.min, row_min[:, s, tt:tt + 1])\
                        .then_inc(scores_masked, 1)

            def normalise(s):
                dve.wait_ge(exps_done, 2 * s + 2)
                then(nc.vector.reciprocal(row_inv[:, s, :], row_sum[:, s, :]))
                second = s < 2 * DIFF_HEADS and s % 2
                if second:
                    then(nc.vector.tensor_scalar(row_inv[:, s, :], row_inv[:, s, :], lam[:, 4:5], None, ALU.mult))
                for tt, (a, b) in enumerate(Q_COLS):
                    inv = row_inv[:, s, tt:tt + 1]
                    if second:
                        nc.vector.scalar_tensor_tensor(out=probs[:, (s - 1) % 4, a:b], in0=probs[:, s % 4, a:b], scalar=inv,
                                                       in1=probs[:, (s - 1) % 4, a:b], op0=ALU.mult, op1=ALU.add)\
                            .then_inc(probs_ready, 1)
                    elif s < 2 * DIFF_HEADS:
                        then(nc.vector.tensor_scalar(probs[:, s % 4, a:b], probs[:, s % 4, a:b], inv, None, ALU.mult))
                    else:
                        nc.vector.tensor_scalar(probs[:, s % 4, a:b], probs[:, s % 4, a:b], inv, None, ALU.mult)\
                            .then_inc(probs_ready, 1)

            def split_mla(u):
                m = u - DIFF_HEADS
                dve.wait_ge(mla_rounded, m + 1)
                nc.vector.tensor_tensor(mixed[:, m, 1, :], ps[:, 4 + u % 2, 0:SEQ], mixed[:, m, 0, :].bitcast(F32),
                                        ALU.subtract).then_inc(mla_split, 1)

            def norm_diff(d):
                k = RSQRT.at["diff"] + d
                dve.wait_ge(rms_inverted, k + 1)
                if d >= 2:
                    dve.wait_ge(diff_turned, d - 1)
                for tt in range(TT):
                    nc.vector.scalar_tensor_tensor(out=diff_out[:, d % 2, tt, :],
                                                   in0=ps[:, 4 + d % 2, tt * DIFF_V:(tt + 1) * DIFF_V],
                                                   scalar=inv_rms[:, k, tt:tt + 1], in1=sub_gain[:, :],
                                                   op0=ALU.mult, op1=ALU.mult).then_inc(diff_normed, 1)

            def split_diff(d):
                k = MLA_HEADS + 2 * d
                dve.wait_ge(diff_rounded, d + 1)
                nc.vector.tensor_tensor(mixed[:, k:k + 2, 1, :], ps[:, 6, :].rearrange("p (k s) -> p k s", k=2),
                                        mixed[:, k:k + 2, 0, :].bitcast(F32), ALU.subtract).then_inc(diff_split, 1)

            for t in range(MAPS + 3):
                blk, tt = V_STEPS.get(t - 1, (0, 0))
                if tt == 1:
                    copy_v1(blk)
                if t < MAPS:
                    mask_scores(t)
                if 1 <= t <= MAPS:
                    normalise(t - 1)
                u = unit_of(t - 3)
                if u is not None:
                    if u < DIFF_HEADS:
                        mean_square_of("diff", SQUARES.after("diff", TT * (u + 1)), DIFF_V, head=u)
                    else:
                        split_mla(u)
                u = unit_of(t - 4)
                if u is not None and u < DIFF_HEADS:
                    norm_diff(u)
                u = unit_of(t - 5)
                if u is not None and u < DIFF_HEADS:
                    split_diff(u)
                if t in V_PIECES:
                    split_piece(dve, "expand", 0, V_PIECES[t])
                if t in OUT_SPLIT_STEPS:
                    split_piece(dve, "out", 0, OUT_SPLIT_STEPS[t])

            dve.wait_ge(post_gain_loaded, 32)

            def out_body(b):
                for q in range(8):
                    split_piece(dve, "out", b, q)
                    if q == 3:
                        branch_block("mix_post", "out", branch_a, b - 1)
            out_body(1)
            with dve.Fori(2, 4) as b:
                out_body(b)
            for q in range(LEAD):
                split_piece(dve, "up2", 0, q)
            last_branch_block("mix_post", "out", branch_a)
            up_stage(2, branch_a)
            down_stage(2, branch_b)
            for c in range(COLUMN_BLOCKS):
                update_x("ffn2_post", branch_b, c)

        @block.tensor
        def _(pe):
            mm = nc.tensor.matmul

            def ready(name, i, q):
                pe.wait_ge(pieces_split, stream.pieces(name, i, q))

            def feature_major(b, slot, col, right, start, stop):
                mm(ps[:, b, :], w_hi[:, slot, col:col + P], right.rearrange("p a s -> p (a s)"), start=start, stop=False)
                return mm(ps[:, b, 0:SEQ], w_lo[:, slot, col:col + P], right[:, 0, :], start=False, stop=stop)

            def token_major(dst, left, slot, cols, start, stop):
                mm(dst, left[:, 0, :], w_hi[:, slot, cols], start=start, stop=False)
                mm(dst, left[:, 0, :], w_lo[:, slot, cols], start=False, stop=False)
                return mm(dst, left[:, 1, :], w_hi[:, slot, cols], start=False, stop=stop)

            def turn_norm(name, src, g):
                if name in ("cq", "ckv"):
                    pe.wait_ge(scaled, SCALED.after(name, TT))
                elif X_FROM[name] is None:
                    pe.wait_ge(x_loaded[2 * g // TILES], 16)
                else:
                    pe.wait_ge(x_updated, RESIDUAL.after(X_FROM[name], TT * (2 * g // TILES + 1)))
                ring = 2 if name in ("cq", "ckv") else 4
                if name == "ckv":
                    pe.wait_ge(norm_split, NORM_TILES.after("cq", 2 * g + 2))
                elif g >= ring:
                    pe.wait_ge(norm_split, NORM_TILES.after(name, 2 * (g - ring) + 2))
                for k in (2 * g, 2 * g + 1):
                    for tt in range(TT):
                        last = nc.tensor.transpose(norm_bank(name, k)[:, tt * P:(tt + 1) * P],
                                                   src[tt][:, k * P:(k + 1) * P], ident[:, :])
                last.then_inc(norm_turned, 1)

            def turn_heads(name, g):
                b = turn_bank(name, g)
                for h, tt, src in heads_of(name, g):
                    rows = src.shape[1]
                    last = nc.tensor.transpose(ps[0:rows, b, h * SEQ + tt * P:h * SEQ + (tt + 1) * P], src, ident[:, :])
                last.then_inc(qk_turned, 1)

            def turn_block(name, c):
                for g in range(c * TILES // 2, (c + 1) * TILES // 2):
                    turn_norm(name, [x[:, tt, :] for tt in range(TT)], g)

            def up_stage(L, norm):
                def body(i, first):
                    for q in range(8):
                        side, k0 = q // 4, 4 * (q % 4)
                        if q % 4 == 0:
                            pe.wait_ge((gate_banks_free, up_banks_free)[side], (L - 1) * (FT // 2) + i + 1)
                        if first and side == 0:
                            pe.wait_ge(norm_split, NORM_TILES.after(norm, k0 + 4))
                        ready(f"up{L}", i, q)
                        for f in range(2):
                            for k in range(4):
                                last = feature_major(4 + 2 * side + f, stream.split_slot(f"up{L}", q), k * 256 + f * P,
                                                     xn[:, k0 + k, :, :], start=k0 + k == 0, stop=k0 + k == KT - 1)
                        last.then_inc(pieces_multiplied, 1)
                        if first and q < 2:
                            turn_block(norm, q + 2)
                        if first and q == 5:
                            pe.wait_ge(diag_ready, L * (1 + TT))
                            mm(ps[:, 0, 0:SEQ], ones, rms_diag, start=True, stop=True).then_inc(row_summed, 1)
                            if L == 1:
                                pe.wait_ge(gains_loaded, 16 * len(LATER_GAINS))
                                n = GAIN_ROWS - KT
                                nc.tensor.transpose(ps[:, 1, 0:n], up[0:n, 1, 0:P], ident[0:n, 0:n])\
                                    .then_inc(gains_turned, 1)

                for c in (0, 1):
                    turn_block(norm, c)
                body(0, True)
                with pe.Fori(1, FT // 2) as i:
                    body(i, False)

            def block_piece(stage, b, q, left):
                ready(stage, b, q)
                for n in (2 * q, 2 * q + 1):
                    k = contraction_tile(stage, b, n)
                    for tt in range(TT):
                        last = token_major(bank(block_bank(stage, b) + tt), left[:, k, :, tt * P:(tt + 1) * P],
                                           stream.split_slot(stage, q), slice((n % 2) * NB, (n % 2 + 1) * NB),
                                           start=n == 0, stop=q == stream.stages[stage].pieces - 1 and n % 2 == 1)
                last.then_inc(pieces_multiplied, 1)

            def down_stage(L):
                with pe.Fori(0, 4) as b:
                    for q in range(FT // 2):
                        pe.wait_ge(hidden_split, (L - 1) * (FT // 2) + q + 1)
                        block_piece(f"down{L}", b, q, hidden)

            pe.wait_ge(ident_ready, 2)
            pe.wait_ge(gain_loaded, 16)
            nc.tensor.transpose(ps[:, 4, 0:KT], up[0:KT, 0, 0:P], ident[0:KT, 0:KT]).then_inc(gains_turned, 1)
            up_stage(1, "ffn1_pre")
            down_stage(1)

            for c in (0, 1):
                turn_block("mix_pre", c)

            def in_block(stage, i, blk, q):
                ready(stage, i, 8 * blk + q)
                for k in (2 * q, 2 * q + 1):
                    for tt in range(TT):
                        last = token_major(ps[:, 2 * blk + tt, :], xn[:, k, :, tt * P:(tt + 1) * P],
                                           stream.split_slot(stage, 8 * blk + q), slice((k % 2) * NB, (k % 2 + 1) * NB),
                                           start=k == 0, stop=k == KT - 1)
                last.then_inc(pieces_multiplied, 1)

            def diff_in(i, lead):
                for blk in range(2):
                    for q in range(8):
                        if q == 0 and lead:
                            pe.wait_ge(rows0_copied, 2 * i + (blk - 1))
                            pe.wait_ge(rows1_copied, 2 * i + (blk - 1))
                        if not lead and blk == 0:
                            pe.wait_ge(norm_split, NORM_TILES.after("mix_pre", 2 * q + 2))
                        in_block("diff_in", i, blk, q)
                        if not lead and blk == 0 and q < 2:
                            turn_block("mix_pre", q + 2)
            diff_in(0, False)
            with pe.Fori(1, 3) as i:
                diff_in(i, True)

            for q in range(24):
                blk, (_, n) = q // 8, LATENT_BLOCKS[q // 8]
                if q % 8 == 0:
                    before = TOKEN_MAJOR.after("diff_in", 5 + blk) if blk < 2 else TOKEN_MAJOR.after("latent")
                    pe.wait_ge(rows0_copied, before)
                    pe.wait_ge(rows1_copied, before)
                ready("latent_in", 0, q)
                for k in (2 * (q % 8), 2 * (q % 8) + 1):
                    for tt in range(TT):
                        last = token_major(ps[:, LATENT_BANK[blk] + tt, 0:n], xn[:, k, :, tt * P:(tt + 1) * P],
                                           stream.split_slot("latent_in", q), slice((k % 2) * n, (k % 2 + 1) * n),
                                           start=k == 0, stop=k == KT - 1)
                last.then_inc(pieces_multiplied, 1)
                if q in DQK_TURN_PIECES:
                    first = 2 * DQK_TURN_PIECES.index(q)
                    for g in (first, first + 1):
                        pe.wait_ge(roped_dqk, 4 if g < 4 else 8)
                        if g >= 2:
                            pe.wait_ge(qk_copied, QK_TURNS.after("dqk", g - 1))
                        turn_heads("dqk", g)
                if q == 21:
                    for g in range(RT // 2):
                        turn_norm("cq", [latent[:, tt, 0:RANK] for tt in range(TT)], g)

            def expand_q_pe():
                for q in range(2):
                    ready("expand", 0, q)
                    for k in (2 * q, 2 * q + 1):
                        for tt in range(TT):
                            last = token_major(ps[:, Q_PE_BANK + tt, :], cn[:, 0, k, :, tt * P:(tt + 1) * P],
                                               stream.split_slot("expand", q), slice((k % 2) * NB, (k % 2 + 1) * NB),
                                               start=k == 0, stop=k == RT - 1)
                    last.then_inc(pieces_multiplied, 1)

            pe.wait_ge(norm_split, NORM_TILES.after("cq", RT))
            expand_q_pe()
            for g in range(RT // 2):
                turn_norm("ckv", [latent[:, tt, RANK:2 * RANK] for tt in range(TT)], g)
            for j in range(1, 5):
                for q in (2 * j, 2 * j + 1):
                    ready("expand", 0, q)
                    for n in (2 * j - 2, 2 * j - 1):
                        if q % 2 == 0:
                            if n == 0:
                                pe.wait_ge(rows0_copied, LATENT_FULL["ckv"])
                                pe.wait_ge(rows1_copied, LATENT_FULL["ckv"])
                            elif n == 1:
                                pe.wait_ge(rows0_copied, TOKEN_MAJOR.after("q_pe"))
                                pe.wait_ge(rows1_copied, TOKEN_MAJOR.after("q_pe"))
                            elif n == 2:
                                pe.wait_ge(qk_copied, QK_TURNS.after("dqk", 8))
                            elif n == 3:
                                pe.wait_ge(norm_split, NORM_TILES.after("ckv", RT))
                            else:
                                pe.wait_ge(nope_done, n - 3)
                        for h in range(2):
                            for k in (2 * (q % 2), 2 * (q % 2) + 1):
                                last = feature_major(nope_bank(n) + h, stream.split_slot("expand", q),
                                                     (k % 2) * NB + (2 * (n % 2) + h) * P,
                                                     cn[:, n // 4, k, :, :], start=k == 0, stop=k == RT - 1)
                    last.then_inc(pieces_multiplied, 1)
            def scores(s):
                b = s % 2
                if s >= 2 * DIFF_HEADS:
                    pe.wait_ge(qk_copied, QK_TURNS.after("q_pe", (s - 2 * DIFF_HEADS) // 2 + 1))
                if s >= 2:
                    pe.wait_ge(scores_masked, 2 * (s - 2) + 2)
                for tt, (a, e) in enumerate(Q_COLS):
                    q_cols, n = slice(tt * P, (tt + 1) * P), e - a
                    if s < 2 * DIFF_HEADS:
                        last = mm(ps[:, b, a:e], dqk_t[:, 0, s, q_cols], dqk_t[:, 1, s, 0:n], start=True, stop=True)
                    else:
                        m = s - 2 * DIFF_HEADS
                        mm(ps[:, b, a:e], nope_t[:, 0, m, q_cols], nope_t[:, 1, m, 0:n], start=True, stop=False)
                        last = mm(ps[:, b, a:e], q_pe_t[:, m, q_cols], k_pe_t[:, 0:n], start=False, stop=True)
                last.then_inc(scores_ready, 1)

            def turn_probs(u):
                pe.wait_ge(probs_ready, 2 * u + 2)
                if u >= 2:
                    pe.wait_ge(probs_copied, u - 1)
                for n in range(3):
                    last = nc.tensor.transpose(ps[:, 2 + u % 2, n * P:(n + 1) * P],
                                               probs[:, first_map(u) % 4, n * P:(n + 1) * P], ident[:, :])
                last.then_inc(probs_turned, 1)

            def values(u):
                b = 4 + u % 2
                pe.wait_ge(probs_copied, u + 1)
                if u == 0:
                    pe.wait_ge(nope_done, 8)
                elif 2 <= u < 2 + DIFF_HEADS:
                    pe.wait_ge(diff_normed, 2 * (u - 2) + 2)
                elif u >= 2 + DIFF_HEADS:
                    pe.wait_ge(mla_split, u - 2 - DIFF_HEADS + 1)
                for tt in range(TT):
                    for kb in range(tt + 1):
                        block_t = probs_t[:, u % 2, (tt + kb) * P:(tt + kb + 1) * P]
                        if u < DIFF_HEADS:
                            last = mm(ps[:, b, tt * DIFF_V:(tt + 1) * DIFF_V], block_t,
                                      proj[:, 2, kb, u * DIFF_V:(u + 1) * DIFF_V], start=kb == 0, stop=kb == tt)
                        else:
                            m = u - DIFF_HEADS
                            last = mm(ps[:, b, tt * P:(tt + 1) * P], v_tok[:, kb, m * P:(m + 1) * P], block_t,
                                      start=kb == 0, stop=kb == tt)
                last.then_inc(values_summed, 1)

            def turn_diff(d):
                pe.wait_ge(diff_normed, 2 * d + 2)
                if d >= 1:
                    pe.wait_ge(diff_split, d)
                else:
                    pe.wait_ge(rows1_copied, TOKEN_MAJOR.after("v", 2))
                for e in range(2):
                    for tt in range(TT):
                        last = nc.tensor.transpose(ps[:, 6, e * SEQ + tt * P:e * SEQ + (tt + 1) * P],
                                                   diff_out[:, d % 2, tt, e * P:(e + 1) * P], ident[:, :])
                last.then_inc(diff_turned, 1)

            def expand_v(blk, tt):
                if blk == 0:
                    pe.wait_ge(nope_done, 7)
                else:
                    pe.wait_ge((rows0_copied, rows1_copied)[tt], TOKEN_MAJOR.after("v", blk))
                for q in (10 + 2 * blk, 11 + 2 * blk):
                    ready("expand", 0, q)
                    for k in (2 * (q % 2), 2 * (q % 2) + 1):
                        last = token_major(ps[:, V_BANK[tt], :], cn[:, 1, k, :, tt * P:(tt + 1) * P],
                                           stream.split_slot("expand", q), slice((k % 2) * NB, (k % 2 + 1) * NB),
                                           start=k == 0, stop=k == RT - 1)
                if tt == 0:
                    last.then_inc(v_summed, 1)
                else:
                    last.then_inc(pieces_multiplied, 2)

            def turn_pe(name, g):
                if name == "k_pe":
                    pe.wait_ge(rows0_copied, TOKEN_MAJOR.after("v", 2))
                    pe.wait_ge(roped_k_pe, 2)
                else:
                    pe.wait_ge(qk_copied, QK_TURNS.after("k_pe", g + 1))
                    pe.wait_ge(roped_q_pe, 4)
                turn_heads(name, g)

            def out_piece(q):
                if q < DIFF_HEADS:
                    pe.wait_ge(diff_split, DIFF_HEADS)
                    pe.wait_ge(qk_copied, QK_TURNS.after("q_pe", MLA_HEADS // 2))
                else:
                    pe.wait_ge(mla_split, 2 * (q - DIFF_HEADS) + 2)
                block_piece("out", 0, q, mixed)

            pe.wait_ge(qk_copied, QK_TURNS.after("dqk", 8))
            pe.wait_ge(nope_done, 6)
            for t in range(MAPS + 3):
                if t < MAPS:
                    scores(t)
                if t in V_STEPS:
                    expand_v(*V_STEPS[t])
                if t in PE_TURN_STEPS:
                    turn_pe(*PE_TURN_STEPS[t])
                if unit_of(t - 2) is not None:
                    turn_probs(unit_of(t - 2))
                if unit_of(t - 3) is not None:
                    values(unit_of(t - 3))
                u = unit_of(t - 5)
                if u is not None and u < DIFF_HEADS:
                    turn_diff(u)
                if t in OUT_STEPS:
                    out_piece(OUT_STEPS[t])

            for q in range(len(OUT_STEPS), 8):
                out_piece(q)
            with pe.Fori(1, 4) as b:
                for q in range(8):
                    block_piece("out", b, q, mixed)
            up_stage(2, "ffn2_pre")
            down_stage(2)


_OUT = ((1, SEQ, D_MODEL), "float32")


def _rope_table():
    cols = []
    for d in (DIFF_D, ROPE):
        inv_freq = np.float32(10000.0) ** (-np.arange(0, d, 2, dtype=np.float32) / np.float32(d))
        angle = np.arange(SEQ, dtype=np.float32)[:, None] * inv_freq[None, :].astype(np.float32)
        cols += [np.cos(angle), np.sin(angle)]
    return np.ascontiguousarray(np.concatenate(cols, axis=1).astype(np.float32))


def kernel(**inputs):
    import concourse.bacc as _bacc
    from concourse.bass_utils import run_bass_kernel_spmd as _run

    nc = _bacc.Bacc("TRN2", target_bir_lowering=False, num_devices=1, dynamic_dma_scratch_size=1024)
    arrays, io = {}, {}
    for name, a in [*inputs.items(), ("rope_table", _rope_table())]:
        a = np.ascontiguousarray(a)
        arrays[f"in_{name}"] = a
        io[name] = nc.dram_tensor(f"in_{name}", a.shape, mybir.dt.from_np(a.dtype), kind="ExternalInput").ap()
    out = nc.dram_tensor("out", _OUT[0], mybir.dt.from_np(np.dtype(_OUT[1])), kind="ExternalOutput").ap()
    encoder_block(nc, io, out)
    return _run(nc, [arrays], core_ids=[0]).results[0]["out"]
```
